# Optimizing a Trainium2 kernel written in Bass

```python
import jax
import jax.numpy as jnp
from jax import lax
import numpy as np
import jax, jax.numpy as jnp

D_MODEL = 1024
BATCH = 1
SEQ = 512
DEPTH = 2

GRID_W = 64
CTX_LEN = 256
HEAD_DIM = 64
GLA_HEADS = 4
NA_HEADS = 6
SWA_HEADS = 6
SWA_KV_HEADS = 2
GLA_W = GLA_HEADS * HEAD_DIM
NA_W = NA_HEADS * HEAD_DIM
SWA_W = SWA_HEADS * HEAD_DIM
SWA_KV_W = SWA_KV_HEADS * HEAD_DIM
MIX_WIDTH = GLA_W + NA_W + SWA_W
GLA_RANK = 16
GLA_TAU = 16.0
GLA_CHUNK = 64
NA_KH = 8
NA_KW = 16
NA_QW = 16
NA_CB = NA_KW + NA_QW
SWA_WINDOW = 128
SWA_BLOCK = 128
ROPE_THETA = 10000.0
NORM_EPS = 1e-6
D_FF = -(-8 * D_MODEL // (3 * 256)) * 256
IN_SPLITS = (GLA_W, GLA_W, GLA_W, GLA_W, GLA_RANK, GLA_RANK, NA_W, NA_W, NA_W, SWA_W, SWA_KV_W, SWA_KV_W)
IN_WIDTH = sum(IN_SPLITS)


def rms_norm(x, g):
    xf = x.astype(jnp.float32)
    y = xf * lax.rsqrt(jnp.mean(xf * xf, axis=-1, keepdims=True) + NORM_EPS)
    return (y * g.astype(jnp.float32)).astype(x.dtype)

def split_cols(p):
    bounds = [int(b) for b in np.cumsum(IN_SPLITS)[:-1]]
    return jnp.split(p, bounds, axis=-1)

def split_heads(a, n_heads):
    return a.reshape(a.shape[:-1] + (n_heads, HEAD_DIM))

def axial_rope(n_tokens):
    t = jnp.arange(n_tokens, dtype=jnp.int32)
    row = (t // GRID_W).astype(jnp.float32)
    col = (t % GRID_W).astype(jnp.float32)
    n_freq = HEAD_DIM // 4
    inv_freq = ROPE_THETA ** (-jnp.arange(n_freq, dtype=jnp.float32) / n_freq)
    ang = jnp.concatenate([row[:, None] * inv_freq, col[:, None] * inv_freq], axis=-1)
    return jnp.cos(ang), jnp.sin(ang)

def apply_rope(a, cos, sin):
    half = HEAD_DIM // 2
    af = a.astype(jnp.float32)
    a1, a2 = af[..., :half], af[..., half:]
    cs = cos[None, :, None, :]
    sn = sin[None, :, None, :]
    return jnp.concatenate([a1 * cs - a2 * sn, a1 * sn + a2 * cs], axis=-1).astype(a.dtype)

def gla_heads(a):
    B, T, _ = a.shape
    return a.reshape(B, T, GLA_HEADS, HEAD_DIM).transpose(0, 2, 1, 3)

def gla_log_decay(z_low, w2, b2):
    z = (z_low @ w2 + b2).astype(jnp.float32)
    return gla_heads(jax.nn.log_sigmoid(z) / GLA_TAU)

def gla_chunked(q, k, v, log_a, s0):
    B, H, T, dk = q.shape
    dv = v.shape[-1]
    n = T // GLA_CHUNK

    def chunks(a):
        return a.astype(jnp.float32).reshape(B, H, n, GLA_CHUNK, a.shape[-1])

    qc, kc, vc, la = chunks(q), chunks(k), chunks(v), chunks(log_a)
    b = jnp.cumsum(la, axis=3)
    b_last = b[:, :, :, -1:, :]
    q_in = qc * jnp.exp(b)
    k_in = kc * jnp.exp(-b)
    k_end = kc * jnp.exp(b_last - b)
    lower = jnp.tril(jnp.ones((GLA_CHUNK, GLA_CHUNK), dtype=bool))
    a_intra = jnp.where(lower, jnp.einsum('bhncd,bhnsd->bhncs', q_in, k_in), 0.0)
    o_intra = jnp.einsum('bhncs,bhnse->bhnce', a_intra, vc)
    chunk_state = jnp.einsum('bhnsd,bhnse->bhnde', k_end, vc)
    chunk_decay = jnp.exp(b_last[:, :, :, 0, :])

    def step(state, inp):
        dec, cs = inp
        return dec[..., None] * state + cs, state

    s_final, s_enter = lax.scan(step, s0, (jnp.moveaxis(chunk_decay, 2, 0), jnp.moveaxis(chunk_state, 2, 0)))
    o_inter = jnp.einsum('bhncd,nbhde->bhnce', q_in, s_enter)
    o = (o_intra + o_inter).reshape(B, H, T, dv).astype(v.dtype)
    return o, s_final

def gla_final_state(k, v, log_a):
    A = jnp.cumsum(log_a.astype(jnp.float32), axis=2)
    w = jnp.exp(A[:, :, -1:, :] - A)
    return jnp.einsum('bhtd,bhte->bhde', k.astype(jnp.float32) * w, v.astype(jnp.float32))

def gla_output(o, g, norm_g):
    B, H, T, dv = o.shape
    o = rms_norm(o.transpose(0, 2, 1, 3), norm_g.reshape(H, dv))
    return o.reshape(B, T, H * dv) * jax.nn.silu(g)

def gla_mixer(parts, parts_c, wa2_f, ba_f, wa2_b, ba_b, norm_g, need_ctx_out):
    q, k, v, g, za_f, za_b = parts
    qc, kc, vc, gc, zac_f, zac_b = parts_c
    scale = HEAD_DIM ** -0.5

    def flip(a):
        return jnp.flip(a, axis=2)

    K_c, V_c = gla_heads(kc), gla_heads(vc)
    la_cf = gla_log_decay(zac_f, wa2_f, ba_f)
    la_cb = gla_log_decay(zac_b, wa2_b, ba_b)
    if need_ctx_out:
        Q_c = gla_heads(qc) * scale
        zeros = jnp.zeros(K_c.shape[:2] + (HEAD_DIM, HEAD_DIM), jnp.float32)
        oc_f, s_f = gla_chunked(Q_c, K_c, V_c, la_cf, zeros)
        oc_b, s_b = gla_chunked(flip(Q_c), flip(K_c), flip(V_c), flip(la_cb), zeros)
        yc = gla_output(oc_f + flip(oc_b), gc, norm_g)
    else:
        s_f = gla_final_state(K_c, V_c, la_cf)
        s_b = gla_final_state(flip(K_c), flip(V_c), flip(la_cb))
        yc = None
    Q, K, V = gla_heads(q) * scale, gla_heads(k), gla_heads(v)
    o_f, _ = gla_chunked(Q, K, V, gla_log_decay(za_f, wa2_f, ba_f), s_f)
    o_b, _ = gla_chunked(flip(Q), flip(K), flip(V), flip(gla_log_decay(za_b, wa2_b, ba_b)), s_b)
    y = gla_output(o_f + flip(o_b), g, norm_g)
    return y, yc

def context_attention(qc, kc, vc, sink):
    B, L, Hq, dh = qc.shape
    Hkv = kc.shape[2]
    G = Hq // Hkv
    s = jnp.einsum('bqhgd,bkhd->bhgqk', qc.reshape(B, L, Hkv, G, dh), kc).astype(jnp.float32) * dh ** -0.5
    if sink is None:
        p = jax.nn.softmax(s, axis=-1)
    else:
        s_sink = jnp.broadcast_to(sink.astype(jnp.float32).reshape(1, Hkv, G, 1, 1), s.shape[:-1] + (1,))
        p = jax.nn.softmax(jnp.concatenate([s, s_sink], axis=-1), axis=-1)[..., :-1]
    o = jnp.einsum('bhgqk,bkhd->bqhgd', p.astype(vc.dtype), vc)
    return o.reshape(B, L, Hq * dh)

def neighborhood_attention(q, k, v, kc, vc, rpb):
    B, T, H, dh = q.shape
    rows = T // GRID_W
    kh = min(NA_KH, rows)
    ncb = GRID_W // NA_QW
    r = np.arange(rows)
    row_idx = np.clip(r - kh // 2, 0, rows - kh)[:, None] + np.arange(kh)[None, :]
    q_cols = np.arange(GRID_W).reshape(ncb, NA_QW)
    win_start = np.clip(q_cols - NA_KW // 2, 0, GRID_W - NA_KW)
    col_idx = np.clip(np.arange(ncb) * NA_QW - NA_KW // 2, 0, GRID_W - NA_CB)[:, None] + np.arange(NA_CB)[None, :]
    key_col = col_idx[:, None, :]
    valid = (key_col >= win_start[:, :, None]) & (key_col < win_start[:, :, None] + NA_KW)
    dr = row_idx - r[:, None] + NA_KH - 1
    dc = np.clip(key_col - q_cols[:, :, None] + NA_KW - 1, 0, 2 * NA_KW - 2)
    bias = rpb.astype(jnp.float32)[:, dr[:, None, None, :, None], dc[None, :, :, None, :]]
    bias = jnp.where(valid[None, None, :, :, None, :], bias, -jnp.inf)

    q_blk = q.reshape(B, rows, ncb, NA_QW, H, dh)
    k_grid = k.reshape(B, rows, GRID_W, H, dh)
    v_grid = v.reshape(B, rows, GRID_W, H, dh)
    ri = row_idx[:, None, :, None]
    ci = col_idx[None, :, None, :]
    k_blk = k_grid[:, ri, ci]
    v_blk = v_grid[:, ri, ci]
    scale = dh ** -0.5
    s_loc = jnp.einsum('brnqhd,brnkchd->bhrnqkc', q_blk, k_blk).astype(jnp.float32) * scale + bias
    n_loc = kh * NA_CB
    s_loc = s_loc.reshape(s_loc.shape[:5] + (n_loc,))
    s_ctx = jnp.einsum('brnqhd,blhd->bhrnql', q_blk, kc).astype(jnp.float32) * scale
    p = jax.nn.softmax(jnp.concatenate([s_loc, s_ctx], axis=-1), axis=-1)
    p_loc = p[..., :n_loc].reshape(p.shape[:5] + (kh, NA_CB)).astype(v.dtype)
    p_ctx = p[..., n_loc:].astype(vc.dtype)
    o = (jnp.einsum('bhrnqkc,brnkchd->brnqhd', p_loc, v_blk)
         + jnp.einsum('bhrnql,blhd->brnqhd', p_ctx, vc))
    return o.reshape(B, T, H * dh)

def sliding_window_attention(q, k, v, kc, vc, sink):
    B, T, Hq, dh = q.shape
    Hkv = k.shape[2]
    G = Hq // Hkv
    bs = SWA_BLOCK
    nb = T // bs
    qb = q.reshape(B, nb, bs, Hkv, G, dh)
    pad = ((0, 0), (bs, bs), (0, 0), (0, 0))
    kp, vp = jnp.pad(k, pad), jnp.pad(v, pad)
    idx = np.arange(nb)[:, None] * bs + np.arange(3 * bs)[None, :]
    kb, vb = kp[:, idx], vp[:, idx]
    kpos = idx - bs
    qpos = np.arange(T).reshape(nb, bs)
    valid = ((np.abs(qpos[:, :, None] - kpos[:, None, :]) <= SWA_WINDOW)
             & (kpos[:, None, :] >= 0) & (kpos[:, None, :] < T))
    scale = dh ** -0.5
    s_loc = jnp.einsum('bnqhgd,bnkhd->bhgnqk', qb, kb).astype(jnp.float32) * scale
    s_loc = jnp.where(valid, s_loc, -jnp.inf)
    s_ctx = jnp.einsum('bnqhgd,blhd->bhgnql', qb, kc).astype(jnp.float32) * scale
    s_sink = jnp.broadcast_to(sink.astype(jnp.float32).reshape(1, Hkv, G, 1, 1, 1), s_loc.shape[:-1] + (1,))
    p = jax.nn.softmax(jnp.concatenate([s_loc, s_ctx, s_sink], axis=-1), axis=-1)
    n_loc = 3 * bs
    L = kc.shape[1]
    p_loc = p[..., :n_loc].astype(v.dtype)
    p_ctx = p[..., n_loc:n_loc + L].astype(vc.dtype)
    o = (jnp.einsum('bhgnqk,bnkhd->bnqhgd', p_loc, vb)
         + jnp.einsum('bhgnql,blhd->bnqhgd', p_ctx, vc))
    return o.reshape(B, T, Hq * dh)

def token_mixers(h, hc, w_in, w_out, wa2_f, ba_f, wa2_b, ba_b, gla_norm, na_rpb, swa_sink, cos, sin, need_ctx_out):
    p = split_cols(h @ w_in)
    pc = split_cols(hc @ w_in)
    y_gla, yc_gla = gla_mixer(p[0:6], pc[0:6], wa2_f, ba_f, wa2_b, ba_b, gla_norm, need_ctx_out)
    nq, nk, nv = (split_heads(a, NA_HEADS) for a in p[6:9])
    nkc, nvc = split_heads(pc[7], NA_HEADS), split_heads(pc[8], NA_HEADS)
    y_na = neighborhood_attention(nq, nk, nv, nkc, nvc, na_rpb)
    sq = apply_rope(split_heads(p[9], SWA_HEADS), cos, sin)
    sk = apply_rope(split_heads(p[10], SWA_KV_HEADS), cos, sin)
    sv = split_heads(p[11], SWA_KV_HEADS)
    skc, svc = split_heads(pc[10], SWA_KV_HEADS), split_heads(pc[11], SWA_KV_HEADS)
    y_swa = sliding_window_attention(sq, sk, sv, skc, svc, swa_sink)
    y = jnp.concatenate([y_gla, y_na, y_swa], axis=-1) @ w_out
    if not need_ctx_out:
        return y, None
    yc_na = context_attention(split_heads(pc[6], NA_HEADS), nkc, nvc, None)
    yc_swa = context_attention(split_heads(pc[9], SWA_HEADS), skc, svc, swa_sink)
    yc = jnp.concatenate([yc_gla, yc_na, yc_swa], axis=-1) @ w_out
    return y, yc

def swiglu(h, w_gate, w_up, w_down):
    return (jax.nn.silu(h @ w_gate) * (h @ w_up)) @ w_down

def first_inputs(seed: int = 0) -> dict:
    key = jax.random.key(seed)
    ks = jax.random.split(key, 24)
    f32 = jnp.float32
    D = D_MODEL

    def nrm(k, shape, s):
        return jax.random.normal(k, shape, f32) * s

    return {
        'x': nrm(ks[0], (BATCH, SEQ, D), 1.0),
        'c': nrm(ks[1], (BATCH, D), 1.0),
        'ctx': nrm(ks[2], (BATCH, CTX_LEN, D), 1.0),
        'c_ctx': nrm(ks[3], (D,), 1.0),
        'w_mod': nrm(ks[4], (DEPTH, D, 6 * D), 0.5 * D ** -0.5),
        'b_mod': nrm(ks[5], (DEPTH, 6 * D), 0.02),
        'norm_mix': 1.0 + nrm(ks[6], (DEPTH, D), 0.05),
        'norm_ffn': 1.0 + nrm(ks[7], (DEPTH, D), 0.05),
        'w_in': nrm(ks[8], (DEPTH, D, IN_WIDTH), D ** -0.5),
        'gla_wa2_f': nrm(ks[9], (DEPTH, GLA_RANK, GLA_W), GLA_RANK ** -0.5),
        'gla_ba_f': nrm(ks[10], (DEPTH, GLA_W), 0.5),
        'gla_wa2_b': nrm(ks[11], (DEPTH, GLA_RANK, GLA_W), GLA_RANK ** -0.5),
        'gla_ba_b': nrm(ks[12], (DEPTH, GLA_W), 0.5),
        'gla_norm': 1.0 + nrm(ks[13], (DEPTH, GLA_W), 0.05),
        'na_rpb': nrm(ks[14], (DEPTH, NA_HEADS, 2 * NA_KH - 1, 2 * NA_KW - 1), 0.1),
        'swa_sink': nrm(ks[15], (DEPTH, SWA_HEADS), 0.5),
        'w_out': nrm(ks[16], (DEPTH, MIX_WIDTH, D), MIX_WIDTH ** -0.5),
        'w_gate': nrm(ks[17], (DEPTH, D, D_FF), D ** -0.5),
        'w_up': nrm(ks[18], (DEPTH, D, D_FF), D ** -0.5),
        'w_down': nrm(ks[19], (DEPTH, D_FF, D), D_FF ** -0.5),
        'final_norm': 1.0 + nrm(ks[20], (D,), 0.05),
    }

def first_block(x, c, ctx, c_ctx, w_mod, b_mod, norm_mix, norm_ffn, w_in, gla_wa2_f, gla_ba_f, gla_wa2_b, gla_ba_b,
              gla_norm, na_rpb, swa_sink, w_out, w_gate, w_up, w_down, final_norm):
    T = x.shape[1]
    cos, sin = axial_rope(T)
    s_lat = jax.nn.silu(c)
    s_ctx = jax.nn.silu(c_ctx)
    xc = ctx
    for i in range(DEPTH):
        need_ctx_out = i < DEPTH - 1
        mod = (s_lat @ w_mod[i] + b_mod[i])[:, None, :]
        mod_c = s_ctx @ w_mod[i] + b_mod[i]
        sh1, sc1, g1, sh2, sc2, g2 = jnp.split(mod, 6, axis=-1)
        sh1c, sc1c, g1c, sh2c, sc2c, g2c = jnp.split(mod_c, 6, axis=-1)
        h = rms_norm(x, norm_mix[i]) * (1.0 + sc1) + sh1
        hc = rms_norm(xc, norm_mix[i]) * (1.0 + sc1c) + sh1c
        y, yc = token_mixers(h, hc, w_in[i], w_out[i], gla_wa2_f[i], gla_ba_f[i], gla_wa2_b[i], gla_ba_b[i],
                             gla_norm[i], na_rpb[i], swa_sink[i], cos, sin, need_ctx_out)
        x = x + g1 * y
        h = rms_norm(x, norm_ffn[i]) * (1.0 + sc2) + sh2
        x = x + g2 * swiglu(h, w_gate[i], w_up[i], w_down[i])
        if need_ctx_out:
            xc = xc + g1c * yc
            hc = rms_norm(xc, norm_ffn[i]) * (1.0 + sc2c) + sh2c
            xc = xc + g2c * swiglu(hc, w_gate[i], w_up[i], w_down[i])
    return rms_norm(x, final_norm)


D_MIX = D_MODEL
ATT_HEADS = 8
ATT_HEAD_DIM = 64
ATT_WIDTH = ATT_HEADS * ATT_HEAD_DIM
MLSTM_HEADS = 4
MLSTM_HEAD_DIM = 128
MLSTM_WIDTH = MLSTM_HEADS * MLSTM_HEAD_DIM
Q_RANK = 256
N_IDX_HEADS = 8
IDX_DIM = 64
INDEX_TOPK = 256
Q_BLOCK = 128
MLSTM_CHUNK = 64
CONV_WIDTH = 4
FFN_HIDDEN = -(-8 * D_MODEL // (3 * 256)) * 256
EPS = 1e-6
IN_SPLITS_2 = (Q_RANK, ATT_WIDTH, ATT_WIDTH, IDX_DIM, N_IDX_HEADS,
             MLSTM_WIDTH, MLSTM_WIDTH, MLSTM_WIDTH, MLSTM_WIDTH, MLSTM_HEADS, MLSTM_HEADS)
IN_COLS = sum(IN_SPLITS_2)


def rms_norm_2(x, w):
    x32 = x.astype(jnp.float32)
    y = x32 * lax.rsqrt(jnp.mean(x32 * x32, axis=-1, keepdims=True) + EPS)
    return (y * w.astype(jnp.float32)).astype(x.dtype)

def rope(x, positions):
    d = x.shape[-1]
    inv_freq = ROPE_THETA ** (-jnp.arange(0, d, 2, dtype=jnp.float32) / d)
    ang = positions.astype(jnp.float32)[..., None] * inv_freq
    cos = jnp.cos(ang)[:, :, None, :]
    sin = jnp.sin(ang)[:, :, None, :]
    x1, x2 = jnp.split(x.astype(jnp.float32), 2, axis=-1)
    return jnp.concatenate([x1 * cos - x2 * sin, x2 * cos + x1 * sin], axis=-1).astype(x.dtype)

def causal_dwconv(x, w, b):
    ch = x.shape[-1]
    y = lax.conv_general_dilated(x, w[:, None, :].astype(x.dtype), window_strides=(1,),
                                 padding=[(CONV_WIDTH - 1, 0)],
                                 dimension_numbers=('NWC', 'WIO', 'NWC'),
                                 feature_group_count=ch)
    return y + b.astype(x.dtype)

def dsa_attention(q, k, v, q_idx, k_idx, w_idx):
    def one_seq(args):
        q_, k_, v_, qi_, ki_, wi_ = args
        seq = q_.shape[0]
        n_sel = min(INDEX_TOPK, seq // 4)
        key_pos = jnp.arange(seq)
        ki32 = ki_.astype(jnp.float32)
        scale = ATT_HEAD_DIM ** -0.5

        def block(i):
            start = i * Q_BLOCK
            t = start + jnp.arange(Q_BLOCK)
            qb = lax.dynamic_slice_in_dim(q_, start, Q_BLOCK, 0)
            qib = lax.dynamic_slice_in_dim(qi_, start, Q_BLOCK, 0).astype(jnp.float32)
            wib = lax.dynamic_slice_in_dim(wi_, start, Q_BLOCK, 0).astype(jnp.float32)
            idx_logits = jnp.einsum('thd,sd->ths', qib, ki32)
            idx_score = jnp.einsum('ths,th->ts', jax.nn.relu(idx_logits), wib)
            idx_score = jnp.where(key_pos[None, :] <= t[:, None], idx_score, -jnp.inf)
            _, sel = lax.top_k(idx_score, n_sel)
            valid = sel <= t[:, None]
            k_sel = k_[sel]
            v_sel = v_[sel]
            logits = jnp.einsum('thd,tkhd->thk', qb, k_sel).astype(jnp.float32) * scale
            logits = jnp.where(valid[:, None, :], logits, -jnp.inf)
            p = jax.nn.softmax(logits, axis=-1)
            return jnp.einsum('thk,tkhd->thd', p.astype(v_.dtype), v_sel)

        out = lax.map(block, jnp.arange(seq // Q_BLOCK))
        return out.reshape((seq,) + q_.shape[1:])

    return lax.map(one_seq, (q, k, v, q_idx, k_idx, w_idx))

def mlstm_chunkwise(q, k, v, ig, lf):
    b_, nh, seq, dk = q.shape
    dv = v.shape[-1]
    nc = seq // MLSTM_CHUNK

    def chunks(a):
        return jnp.moveaxis(a.reshape(a.shape[:2] + (nc, MLSTM_CHUNK) + a.shape[3:]), 2, 0)

    qc, kc, vc, igc, lfc = chunks(q), chunks(k), chunks(v), chunks(ig), chunks(lf)
    bc = jnp.cumsum(lfc, axis=-1)
    causal = jnp.tril(jnp.ones((MLSTM_CHUNK, MLSTM_CHUNK), dtype=bool))

    def step(carry, inp):
        c_s, n_s, m_s = carry
        q_, k_, v_, ig_, b_c = inp
        d_mat = b_c[..., :, None] - b_c[..., None, :] + ig_[..., None, :]
        d_mat = jnp.where(causal, d_mat, -jnp.inf)
        inter = b_c + m_s[..., None]
        m_row = jnp.maximum(inter, jnp.max(d_mat, axis=-1))
        w_intra = jnp.exp(d_mat - m_row[..., None])
        w_inter = jnp.exp(inter - m_row)
        s_mat = jnp.einsum('bhtd,bhsd->bhts', q_, k_) * w_intra
        num = (jnp.einsum('bhts,bhsv->bhtv', s_mat, v_)
               + w_inter[..., None] * jnp.einsum('bhtd,bhdv->bhtv', q_, c_s))
        den = jnp.sum(s_mat, axis=-1) + w_inter * jnp.einsum('bhtd,bhd->bht', q_, n_s)
        h = num / jnp.maximum(jnp.abs(den), jnp.exp(-m_row))[..., None]
        total = b_c[..., -1]
        w_log = total[..., None] - b_c + ig_
        m_new = jnp.maximum(total + m_s, jnp.max(w_log, axis=-1))
        decay = jnp.exp(total + m_s - m_new)
        w_state = jnp.exp(w_log - m_new[..., None])
        c_new = decay[..., None, None] * c_s + jnp.einsum('bhs,bhsd,bhsv->bhdv', w_state, k_, v_)
        n_new = decay[..., None] * n_s + jnp.einsum('bhs,bhsd->bhd', w_state, k_)
        return (c_new, n_new, m_new), h

    init = (jnp.zeros((b_, nh, dk, dv), jnp.float32), jnp.zeros((b_, nh, dk), jnp.float32),
            jnp.zeros((b_, nh), jnp.float32))
    _, hs = lax.scan(step, init, (qc, kc, vc, igc, bc))
    return jnp.moveaxis(hs, 0, 2).reshape(b_, nh, seq, dv)

def hybrid_mixer(h, positions, w_in, q_latent_norm, w_q_up, w_qidx_up, conv_w, conv_b,
                 b_igate, b_fgate, attn_out_norm, mlstm_out_norm, w_out):
    b_, seq, _ = h.shape
    split_pts = [int(s) for s in np.cumsum(IN_SPLITS_2)[:-1]]
    (cq, k_att, v_att, k_idx, w_idx,
     q_m, k_m, v_m, o_m, i_m, f_m) = jnp.split(h @ w_in, split_pts, axis=-1)

    cq = rms_norm_2(cq, q_latent_norm)
    q = rope((cq @ w_q_up).reshape(b_, seq, ATT_HEADS, ATT_HEAD_DIM), positions)
    q_idx = rope((cq @ w_qidx_up).reshape(b_, seq, N_IDX_HEADS, IDX_DIM), positions)
    k = rope(k_att.reshape(b_, seq, ATT_HEADS, ATT_HEAD_DIM), positions)
    v = v_att.reshape(b_, seq, ATT_HEADS, ATT_HEAD_DIM)
    k_idx = rope(k_idx[:, :, None, :], positions)[:, :, 0, :]
    w_idx = w_idx * (N_IDX_HEADS * IDX_DIM) ** -0.5
    att = dsa_attention(q, k, v, q_idx, k_idx, w_idx)
    att = rms_norm_2(att, attn_out_norm.reshape(ATT_HEADS, ATT_HEAD_DIM)).reshape(b_, seq, ATT_WIDTH)

    qk = jax.nn.silu(causal_dwconv(jnp.concatenate([q_m, k_m], axis=-1), conv_w, conv_b))
    q_m, k_m = jnp.split(qk, 2, axis=-1)

    def heads(a):
        return a.reshape(b_, seq, MLSTM_HEADS, MLSTM_HEAD_DIM).transpose(0, 2, 1, 3).astype(jnp.float32)

    ig = (i_m + b_igate).astype(jnp.float32).transpose(0, 2, 1)
    lf = jax.nn.log_sigmoid((f_m + b_fgate).astype(jnp.float32)).transpose(0, 2, 1)
    hm = mlstm_chunkwise(heads(q_m) * MLSTM_HEAD_DIM ** -0.5, heads(k_m), heads(v_m), ig, lf)
    hm = hm.transpose(0, 2, 1, 3).astype(h.dtype)
    hm = rms_norm_2(hm, mlstm_out_norm.reshape(MLSTM_HEADS, MLSTM_HEAD_DIM))
    hm = (jax.nn.sigmoid(o_m).reshape(b_, seq, MLSTM_HEADS, MLSTM_HEAD_DIM) * hm).reshape(b_, seq, MLSTM_WIDTH)

    return jnp.concatenate([att, hm], axis=-1) @ w_out

def swiglu_2(h, w_gate_up, w_down):
    g, u = jnp.split(h @ w_gate_up, 2, axis=-1)
    return (jax.nn.silu(g) * u) @ w_down

def second_inputs(seed: int = 0) -> dict:
    key = jax.random.key(seed)
    ks = jax.random.split(key, 24)
    L = DEPTH

    def nrm(k, shape, scale):
        return jax.random.normal(k, shape, jnp.float32) * scale

    def gain(k, shape):
        return 1.0 + 0.05 * jax.random.normal(k, shape, jnp.float32)

    x = nrm(ks[0], (BATCH, SEQ, D_MODEL), 1.0)
    c = nrm(ks[1], (BATCH, D_MODEL), 1.0)
    offsets = jax.random.randint(ks[2], (BATCH, 1), 0, 1024, dtype=jnp.int32)
    positions = (offsets + jnp.arange(SEQ, dtype=jnp.int32)[None, :]).astype(jnp.int32)
    b_fgate = (jnp.linspace(3.0, 6.0, MLSTM_HEADS, dtype=jnp.float32)[None, :]
               + nrm(ks[14], (L, MLSTM_HEADS), 0.1))
    return {
        "x": x,
        "c": c,
        "positions": positions,
        "w_mod": nrm(ks[3], (L, D_MODEL, 6 * D_MODEL), 0.5 * D_MODEL ** -0.5),
        "b_mod": nrm(ks[4], (L, 6 * D_MODEL), 0.01),
        "mix_norm_pre": gain(ks[5], (L, D_MODEL)),
        "mix_norm_post": gain(ks[6], (L, D_MODEL)),
        "w_in": nrm(ks[7], (L, D_MODEL, IN_COLS), D_MODEL ** -0.5),
        "q_latent_norm": gain(ks[8], (L, Q_RANK)),
        "w_q_up": nrm(ks[9], (L, Q_RANK, ATT_WIDTH), Q_RANK ** -0.5),
        "w_qidx_up": nrm(ks[10], (L, Q_RANK, N_IDX_HEADS * IDX_DIM), Q_RANK ** -0.5),
        "conv_w": nrm(ks[11], (L, CONV_WIDTH, 2 * MLSTM_WIDTH), CONV_WIDTH ** -0.5),
        "conv_b": nrm(ks[12], (L, 2 * MLSTM_WIDTH), 0.01),
        "b_igate": nrm(ks[13], (L, MLSTM_HEADS), 0.1),
        "b_fgate": b_fgate,
        "attn_out_norm": gain(ks[15], (L, ATT_WIDTH)),
        "mlstm_out_norm": gain(ks[16], (L, MLSTM_WIDTH)),
        "w_out": nrm(ks[17], (L, D_MIX, D_MODEL), D_MIX ** -0.5),
        "ffn_norm_pre": gain(ks[18], (L, D_MODEL)),
        "ffn_norm_post": gain(ks[19], (L, D_MODEL)),
        "w_gate_up": nrm(ks[20], (L, D_MODEL, 2 * FFN_HIDDEN), D_MODEL ** -0.5),
        "w_down": nrm(ks[21], (L, FFN_HIDDEN, D_MODEL), FFN_HIDDEN ** -0.5),
    }

def second_block(x, c, positions, w_mod, b_mod, mix_norm_pre, mix_norm_post, w_in, q_latent_norm,
              w_q_up, w_qidx_up, conv_w, conv_b, b_igate, b_fgate, attn_out_norm, mlstm_out_norm,
              w_out, ffn_norm_pre, ffn_norm_post, w_gate_up, w_down):
    c_act = jax.nn.silu(c)
    for l in range(DEPTH):
        mod = c_act @ w_mod[l] + b_mod[l]
        sh_m, sc_m, g_m, sh_f, sc_f, g_f = jnp.split(mod, 6, axis=-1)
        h = rms_norm_2(x, mix_norm_pre[l]) * (1.0 + sc_m[:, None, :]) + sh_m[:, None, :]
        y = hybrid_mixer(h, positions, w_in[l], q_latent_norm[l], w_q_up[l], w_qidx_up[l],
                         conv_w[l], conv_b[l], b_igate[l], b_fgate[l], attn_out_norm[l],
                         mlstm_out_norm[l], w_out[l])
        x = x + g_m[:, None, :] * rms_norm_2(y, mix_norm_post[l])
        h = rms_norm_2(x, ffn_norm_pre[l]) * (1.0 + sc_f[:, None, :]) + sh_f[:, None, :]
        y = swiglu_2(h, w_gate_up[l], w_down[l])
        x = x + g_f[:, None, :] * rms_norm_2(y, ffn_norm_post[l])
    return x


def setup_inputs(seed=0):
    out = dict(first_inputs(seed))
    for name, value in second_inputs(seed + 1).items():
        if name != "x":
            out[name + "_2"] = value
    return out


def reference(
    x, c, ctx, c_ctx, w_mod, b_mod, norm_mix, norm_ffn, w_in, gla_wa2_f, gla_ba_f, gla_wa2_b,
    gla_ba_b, gla_norm, na_rpb, swa_sink, w_out, w_gate, w_up, w_down, final_norm, c_2,
    positions_2, w_mod_2, b_mod_2, mix_norm_pre_2, mix_norm_post_2, w_in_2, q_latent_norm_2,
    w_q_up_2, w_qidx_up_2, conv_w_2, conv_b_2, b_igate_2, b_fgate_2, attn_out_norm_2,
    mlstm_out_norm_2, w_out_2, ffn_norm_pre_2, ffn_norm_post_2, w_gate_up_2, w_down_2,
):
    x = first_block(
        x, c, ctx, c_ctx, w_mod, b_mod, norm_mix, norm_ffn, w_in, gla_wa2_f, gla_ba_f,
        gla_wa2_b, gla_ba_b, gla_norm, na_rpb, swa_sink, w_out, w_gate, w_up, w_down,
        final_norm,
    )
    return second_block(
        x, c_2, positions_2, w_mod_2, b_mod_2, mix_norm_pre_2, mix_norm_post_2, w_in_2,
        q_latent_norm_2, w_q_up_2, w_qidx_up_2, conv_w_2, conv_b_2, b_igate_2, b_fgate_2,
        attn_out_norm_2, mlstm_out_norm_2, w_out_2, ffn_norm_pre_2, ffn_norm_post_2,
        w_gate_up_2, w_down_2,
    )


_drawn_inputs = setup_inputs


def setup_inputs(seed=0):
    import zlib

    import numpy as np

    out = dict(_drawn_inputs(seed))
    spreads = {}
    factors = {'gla_norm': 3.992,
     'na_rpb': 24.297,
     'swa_sink': 64.0,
     'conv_b_2': 22.198,
     'b_igate_2': 64.0,
     'mlstm_out_norm_2': 4.411,
     'q_latent_norm_2': 5.448,
     'attn_out_norm_2': 5.861,
     'ffn_norm_post_2': 2.776}
    for name, (base, spread) in spreads.items():
        noise = np.random.default_rng([zlib.crc32(name.encode()), seed]).standard_normal(out[name].shape)
        drawn = base * np.exp(spread * noise) if base else spread * noise
        out[name] = jnp.asarray(drawn.astype(out[name].dtype))
    for name, factor in factors.items():
        out[name] = (out[name] * factor).astype(out[name].dtype)
    return out
```

```python
from contextlib import ExitStack

import numpy as np

import concourse.bass as bass
from concourse import mybir

F32 = mybir.dt.float32
I32 = mybir.dt.int32
ALU = mybir.AluOpType
ACT = mybir.ActivationFunctionType
AX = mybir.AxisListType.X

PT = 128
D = 1024
KD = D // PT
CTX_T, LAT_T = 2, 4
NT = CTX_T + LAT_T
TOK = NT * PT
FF = 2816
KF = FF // PT
NEG = -1.0e30
TAKEN = -3.0e38
EPS = 1e-6
HD = 64

W1 = 2848
G_Q, G_K, G_V, G_G, G_Z = 0, 256, 512, 768, 1024
N_Q, N_K, N_V = 1056, 1440, 1824
S_Q, S_K, S_V = 2208, 2592, 2720
GLA_H, NA_H, SWA_H = 4, 6, 6
CH = 64
NCH = TOK // CH

W2 = 3408
A_C, A_K, A_V, A_KI, A_WI = 0, 256, 768, 1280, 1344
M_Q, M_K, M_V, M_O, M_I, M_F = 1352, 1864, 2376, 2888, 3400, 3404
ATT_H, ML_H = 8, 4
TOPK = 128

C_ID, C_TRI, C_TRIF, C_ONE, C_SW, C_CAU, C_ROPE, C_FREQ, C_SEL = 0, 128, 640, 768, 896, 1280, 1792, 2048, 2080
C_N = 2080 + 512

SC_N = 14080
HT_N = NT * D
P_N = NT * W1
SLOT = 4096
XN = 6144
YB = 11264
ROWN = 15000

TWO_PI_1 = 6.28125
TWO_PI_2 = float(np.float32(2 * np.pi - TWO_PI_1))
TWO_PI_3 = float(2 * np.pi - TWO_PI_1 - TWO_PI_2)
ROUND = 12582912.0


def shape_constants():
    c = np.zeros((PT, C_N), np.float32)
    i = np.arange(PT)
    s, t = i[:, None], i[None, :]
    same = (s // CH) == (t // CH)
    c[:, C_ID:C_ID + 128] = np.eye(PT)
    for n, m in enumerate([s <= t, s >= t, s > t, s < t]):
        c[:, C_TRI + 128 * n:C_TRI + 128 * (n + 1)] = (m & same) / 16.0
    c[:, C_TRIF:C_TRIF + 128] = s <= t
    c[:, C_ONE:C_ONE + 128] = 1.0
    c[:, C_SW:C_SW + 128] = np.where(t >= s, 0.0, NEG)
    c[:, C_SW + 256:C_SW + 384] = np.where(t <= s, 0.0, NEG)
    c[:, C_CAU + 384:C_CAU + 512] = np.where(t <= s, 0.0, NEG)
    tok = np.arange(LAT_T * PT)
    inv = (np.float32(10000.0) ** (-np.arange(16, dtype=np.float32) / 16)).astype(np.float32)
    row, col = (tok // 64).astype(np.float32), (tok % 64).astype(np.float32)
    ang = np.concatenate([row[:, None] * inv, col[:, None] * inv], -1)
    cs = np.stack([np.cos(ang), np.sin(ang)], 1).reshape(LAT_T, PT, 64)
    c[:, C_ROPE:C_ROPE + 256] = cs.transpose(1, 0, 2).reshape(PT, 256)
    c[:, C_FREQ:C_FREQ + 32] = np.float32(10000.0) ** (-np.arange(0, 64, 2, dtype=np.float32) / 64)
    for h in range(4):
        c[h, C_SEL + 128 * h:C_SEL + 128 * (h + 1)] = 1.0
    oh = np.zeros((32, 64, 2, 64), np.float32)
    for qc in range(64):
        start = min(max(qc - 8, 0), 48)
        for kc in range(64):
            if start <= kc < start + 16:
                oh[kc - qc + 15, kc, :, qc] = 1.0
            else:
                oh[31, kc, :, qc] = NEG
    return c, oh.reshape(32, 64 * 128)


class Banks:

    def __init__(self, ps, filled, emptied):
        self.ps, self.filled, self.emptied = ps, filled, emptied
        self.past, self.count = [], {"a": 0, "d": 0}

    def _next(self, by):
        g = len(self.past)
        self.count[by] += 1
        self.past.append((by, self.count[by]))
        return g

    def fill(self, pe, by):
        g = self._next(by)
        if g >= 8:
            who, n = self.past[g - 8]
            pe.wait_ge(self.emptied[who], n)
        return self.ps[g % 8]

    def empty(self, eng, by, mine):
        g = self._next(by)
        if by != mine:
            return None
        eng.wait_ge(self.filled, g + 1)
        return self.ps[g % 8]

    def filled_so_far(self):
        return len(self.past)

    def emptied_by(self, who):
        return self.count[who]

    def all_emptied(self, eng):
        for who in "ad":
            if self.count[who]:
                eng.wait_ge(self.emptied[who], self.count[who])


def layer(nc, T, w, sems, second, with_ctx, nxt, start_loads=()):
    X, P, SC, WR, CN, GB, SM = T["X"], T["P"], T["SC"], T["W"], T["C"], T["G"], T["SM"]
    PS = T["PS"]
    S = sems
    R = 1 if second else 2
    W = W2 if second else W1
    CW = W // 8
    T0 = CTX_T if second else 0
    O0 = 0 if with_ctx else CTX_T
    IN_T, OUT_T = range(T0, NT), range(O0, NT)
    PW = P[:, 0:(NT - T0) * W].rearrange("p (t n) -> p t n", n=W)

    def pr(t, a, n):
        return PW[:, t - T0, a:a + n]

    XV = X.rearrange("p (t n) -> p t n", n=D)
    HT = SC[:, 0:HT_N].rearrange("p (k n) -> p k n", k=KD)
    ROWS = SC[:, 11776:13312]
    SLM = SC[:, 7680:7680 + SLOT]
    SC32 = SC[:, 13312:13568].rearrange("p (k m) -> p k m", k=KD)
    BR = P[:, 0:1536]
    PO = P[:, 1536:2048]
    XNV = P[:, XN:XN + NT * D].rearrange("p (t n) -> p t n", n=D)
    GTOK = TOK - (CTX_T * PT if second else 0)
    GT = P[:, 0:KF * GTOK].rearrange("p (k n) -> p k n", k=KF)
    GOFF = CTX_T * PT if second else 0
    YBV = P[:, YB:YB + LAT_T * D].rearrange("p (t n) -> p t n", n=D)
    GBV = GB.rearrange("p (s r n) -> p s r n", s=2, r=2)
    ident = CN[:, C_ID:C_ID + 128]
    slots = [WR[:, SLOT * i:SLOT * (i + 1)] for i in range(2)]

    SG = [SC[:, HT_N + 768 * i:HT_N + 768 * (i + 1)] for i in range(2)]

    VR, VT = SM[:, 0:128], SM[:, 128:256]
    MT = SM[:, 272:272 + 32 * R].rearrange("p (s k r) -> p s k r", s=4, r=R)
    AT = SM[:, 336:336 + 16 * R].rearrange("p (s k r) -> p s k r", s=2, r=R)
    ssq, rstd = SM[:, 368:416], SM[:, 416:464]
    nm, rs, rr, fl = SM[:, 464:468], SM[:, 468:472], SM[:, 472:476], SM[:, 476:480]
    DEC = SM[:, 480:528].rearrange("p (d f c) -> p d f c", d=2, f=2)
    SINK = SM[:, 528:534]
    RPR = SM[0:90, 540:571]
    RPT = SM[0:32, 0:128]
    m8 = SM[:, 666:674]
    GIB, GFB = SM[:, 674:678], SM[:, 678:682]
    IG, LF, BC, T16 = (SM[:, 684 + 16 * i:700 + 16 * i].rearrange("p (t h) -> p t h", h=4) for i in range(4))
    WI = SM[:, 748:780].rearrange("p (t h) -> p t h", h=8)
    PF = SM[:, 780:784]
    ones_col = CN[:, C_ONE:C_ONE + 1]
    small = SM[:, 784:912]
    PI32 = T["PI"]

    V_NEXT = 66 if second else 32
    n_next = len(nxt["c"]) if nxt else 0
    nvec = V_NEXT + 8 * n_next
    V_C, V_CC, V_N1, V_N2, V_QL, V_CB, V_CWT = (0, None, 8, 16, 24, 26, 34) if second else (0, 8, 16, 24, None, None, None)

    tiles = []

    def slot_of():
        return slots[len(tiles) % 2]

    def cols(wt, a, n, k0=0, k1=KD):
        src = wt[:, a:a + n].rearrange("(k p) n -> p k n", p=PT)[:, k0:k1]
        dst = slot_of()[:, 0:(k1 - k0) * n].rearrange("p (k n) -> p k n", n=n)
        h = (k1 - k0) // 2
        tiles.append([(dst[:, 0:h], src[:, 0:h]), (dst[:, h:], src[:, h:])])

    if start_loads:
        for j in range(12):
            cols(w["w_mod"], 512 * j, 512)
    for j in range(8):
        cols(w["w_in"], CW * j, CW)
    if second:
        d = slot_of()[:, 0:2048].rearrange("p (m k n) -> p m k n", m=2, k=2)
        tiles.append([(d[:, m], w[n].rearrange("(k p) n -> p k n", p=PT)) for m, n in enumerate(("w_q_up", "w_qidx_up"))])
    else:
        for j in range(2):
            d, s_ = slot_of()[0:32, :], w["onehot"][:, SLOT * j:SLOT * (j + 1)]
            tiles.append([(d[:, 0:2048], s_[:, 0:2048]), (d[:, 2048:], s_[:, 2048:])])
    for j in range(2):
        cols(w["w_out"], 512 * j, 512)
    for j in range(11):
        d = slot_of()[:, :].rearrange("p (m k n) -> p m k n", m=2, k=KD)
        tiles.append([(d[:, m], w[n][:, a + 256 * j:a + 256 * (j + 1)].rearrange("(k p) n -> p k n", p=PT))
                      for m, (n, a) in enumerate(w["gate_up"])])
    DOWN = [(0, 8), (8, 16), (16, 22)]
    for half in range(2):
        for k0, k1 in DOWN:
            cols(w["w_down"], 512 * half, 512, k0, k1)

    def banks():
        return Banks(PS, S["filled"], {"a": S["emptied_act"], "d": S["emptied_dve"]})

    units = []
    if not second:
        QN = SC[:, 0:2304].rearrange("p (f n) -> p f n", n=TOK)
        KN = SC[:, 2304:4608].rearrange("p (f n) -> p f n", n=TOK)
        NB = SC[:, 4608:9984].rearrange("p (h j c) -> p h j c", h=NA_H, j=14)
        SB = [SC[:, 9984 + 776 * i:9984 + 776 * (i + 1)] for i in range(2)]
        PB = [SC[:, 11536 + 768 * i:11536 + 768 * (i + 1)] for i in range(2)]
        RQ = SC[:, 4608:4608 + 1536].rearrange("p (t n) -> p t n", n=384)
        RK = SC[:, 6144:6144 + 1536].rearrange("p (t n) -> p t n", n=256)
        RT = [SC[:, 7680 + 768 * i:7680 + 768 * (i + 1)] for i in range(2)]
        KS = KN[:, 0:2]
        QS = QN
        na_units, sw_units = [], []
        for h in range(NA_H):
            b, f = 64 * (h % 2), h // 2
            for t in OUT_T:
                u = dict(off=b, q=QN[b:b + 64, f, t * 128:(t + 1) * 128], ka=KN[b:b + 64, f, 0:256], kb=None, bias=None,
                         sink=None, v=[(s, N_V + 64 * h) for s in range(CTX_T)], y=pr(t, N_Q + 64 * h, 64))
                if t >= CTX_T:
                    j0 = 7 - 2 * (t - CTX_T) - 1
                    u["kb"] = KN[b:b + 64, f, 256:768]
                    u["bias"] = NB[:, h, j0:j0 + 8, :].rearrange("p j c -> p (j c)")
                    u["v"] += [(s, N_V + 64 * h) for s in range(CTX_T, NT)]
                na_units.append(u)
        for h in range(SWA_H):
            b, f, kv = 64 * (h % 2), h // 2, h // 3
            for t in OUT_T:
                u = dict(off=64 * kv, q=QS[b:b + 64, f, t * 128:(t + 1) * 128], ka=KS[b:b + 64, kv, 0:256], kb=None, bias=None,
                         sink=SINK[:, h:h + 1], v=[(s, S_V + 64 * kv) for s in range(CTX_T)], y=pr(t, S_Q + 64 * h, 64))
                if t >= CTX_T:
                    lo, hi = max(t - 1, CTX_T), min(t + 2, NT)
                    u["kb"] = KS[b:b + 64, kv, lo * 128:hi * 128]
                    u["bias"] = CN[:, C_SW + (lo - t + 1) * 128:C_SW + (hi - t + 1) * 128]
                    u["v"] += [(s, S_V + 64 * kv) for s in range(lo, hi)]
                sw_units.append(u)
        phases = [na_units, sw_units]
    else:
        QQ = SC[:, 0:4096].rearrange("p (t n) -> p t n", n=1024)
        RT = [SC[:, 4096 + 1024 * i:4096 + 1024 * (i + 1)] for i in range(2)]
        CQ = SC[:, 4096:5120].rearrange("p (k n) -> p k n", k=2)
        KID = SC[:, 6144:6656].rearrange("p (t n) -> p t n", n=128)
        QTT = SC[:, 6656:8704].rearrange("p (f n) -> p f n", n=512)
        QIT = SC[:, 8704:10752].rearrange("p (f n) -> p f n", n=512)
        KTT = SC[:, 10752:12800].rearrange("p (f n) -> p f n", n=512)
        KIT = SC[:, 12800:13312]
        SCO, WK = SC[:, 0:512], SC[:, 512:1024]
        RL = [SC[:, 1024 + 512 * i:1536 + 512 * i] for i in range(2)]
        MK = SC[:, 2048:3328]
        MKO = [0, 128, 384, 768]
        SB = [SC[:, 3328 + 520 * i:3328 + 520 * (i + 1)] for i in range(3)]
        PB = [SC[:, 4888 + 512 * i:4888 + 512 * (i + 1)] for i in range(2)]
        CSN = SC[:, 13312:13568].rearrange("p (t c f) -> p t c f", t=4, c=2)
        ANG = [SC[:, 13568 + 128 * i:13696 + 128 * i] for i in range(3)]
        at_units, ml_units = [], []
        for h in range(ATT_H):
            b, f = 64 * (h % 2), h // 2
            for n in range(LAT_T):
                nk = 128 * (n + 1)
                at_units.append(dict(off=b, q=QTT[b:b + 64, f, n * 128:(n + 1) * 128], ka=None, kb=KTT[b:b + 64, f, 0:nk],
                                     bias=MK[:, MKO[n]:MKO[n] + nk], sink=None,
                                     v=[(CTX_T + s, A_V + 64 * h) for s in range(n + 1)],
                                     y=pr(CTX_T + n, A_K + 64 * h, 64)))
        phases = [at_units]
        QK = SC[:, 0:4096].rearrange("p (f n) -> p f n", n=512)
        CP = [SC[:, 4096 + 516 * i:4096 + 516 * (i + 1)] for i in range(2)]
        CT = SC[0:4, 5200:5712]
        SM2 = [SC[:, 5712 + 512 * i:6224 + 512 * i] for i in range(2)]
        SB2 = [SC[:, 7760 + 512 * i:8272 + 512 * i] for i in range(2)]
        PB2 = [SC[:, 6736 + 512 * i:7248 + 512 * i] for i in range(2)]
        for h in range(ML_H):
            for n in range(LAT_T):
                nk = 128 * (n + 1)
                ml_units.append(dict(h=h, n=n, q=QK[:, h, n * 128:(n + 1) * 128], k=QK[:, 4 + h, 0:nk], nk=nk,
                                     v=[(CTX_T + s, M_V + 128 * h) for s in range(n + 1)],
                                     y=pr(CTX_T + n, M_Q + 128 * h, 128)))
    for ph in phases:
        for u in ph:
            u["na"] = 0 if u["ka"] is None else 256
            u["nb"] = 0 if u["kb"] is None else u["kb"].shape[-1]
            u["n"] = u["na"] + u["nb"]
            u["blocks"] = u["n"] // 128

    if not second:
        QI = SC[:, 0:3072].rearrange("p (d f n) -> p d f n", d=2, f=2)
        KI = SC[:, 3072:6144].rearrange("p (d f n) -> p d f n", d=2, f=2)
        LA = SC[:, 6144:9216].rearrange("p (t n) -> p t n", n=512)
        KE = SC[:, 9216:12288].rearrange("p (t d n) -> p t d n", d=2, n=256)
        SE = SC[:, 9216:12288].rearrange("p (d c f e) -> p d c f e", d=2, c=NCH, f=2)
        EB = [SC[:, 12288 + 768 * i:13056 + 768 * i] for i in range(2)]
        ZT = SC[0:33, 12288:13056]
        WZ = SC[0:33, 13056:13568]
        GN = SC[:, 13824:14080]
        AM = [SC[:, 6144 + 1024 * i:7168 + 1024 * i].rearrange("p (d h n) -> p d h n", d=2, h=4) for i in range(2)]
        MN = SC[:, 9216:12288]
        order = [list(range(NCH)), [3, 2, 1, 0] + list(range(NCH - 1, 3, -1))]
        first = [order[0][0], order[1][0]]

    YF = [A_K, A_K + 128, A_K + 256, A_K + 384, M_Q, M_Q + 128, M_Q + 256, M_Q + 384] if second else \
         [G_Q, G_Q + 128, N_Q, N_Q + 128, N_Q + 256, S_Q, S_Q + 128, S_Q + 256]

    def spans(tt):
        out = []
        if tt[0] < CTX_T:
            out.append((0, CTX_T * PT, R - 1))
        return out + [(CTX_T * PT, LAT_T * PT, 0)]

    small_loads = [(VR[a:a + v.shape[-1] // PT, :], v.rearrange("a (f p) -> (a f) p", p=PT)) for a, v in
                   [(V_C, w["c"]), (V_N1, w["norm1"]), (V_N2, w["norm2"])]
                   + ([(V_QL, w["q_latent_norm"]), (V_CB, w["conv_b"])] if second else [(V_CC, w["c_ctx"])])]
    small_loads += [(VR[V_NEXT + 8 * i:V_NEXT + 8 * i + 8, :], c.rearrange("a (f p) -> (a f) p", p=PT))
                    for i, c in enumerate(nxt["c"] if nxt else ())]
    for q in range(4):
        def quarter(v):
            n = v.shape[-1] // 512
            return v.rearrange("a (c q n) -> a q c n", q=4, n=PT)[:, q].broadcast_to([32, n, PT])

        lane = slice(32 * q, 32 * q + 32)
        small_loads.append((BR[lane, :].rearrange("p (c n) -> p c n", n=PT), quarter(w["b_mod"])))
        if second:
            small_loads += [(PO[lane, 256 * i:256 * (i + 1)].rearrange("p (c n) -> p c n", n=PT), quarter(w[n]))
                            for i, n in enumerate(("post1", "post2"))]
    if second:
        small_loads += [(VR[V_CWT:V_CWT + 32, :], w["conv_w"].rearrange("w (f p) -> (w f) p", p=PT)),
                        (P[:, ROWN:ROWN + 512], w["attn_out_norm"].broadcast_to([PT, 512])),
                        (P[:, ROWN + 512:ROWN + 1024], w["mlstm_out_norm"].broadcast_to([PT, 512])),
                        (GIB, w["b_igate"].broadcast_to([PT, 4])), (GFB, w["b_fgate"].broadcast_to([PT, 4])),
                        (PI32[:, :], w["positions"])]
    else:
        small_loads += [(GN, w["gla_norm"].broadcast_to([PT, 256])), (SINK, w["sink"].broadcast_to([PT, SWA_H])),
                        (RPR, w["rpb"].rearrange("h r c -> (h r) c"))]
    z_loads = [] if second else [(WZ[0:16, 0:256], w["wa2_f"]), (WZ[16:32, 256:512], w["wa2_b"]),
                        (WZ[32:33, 0:256], w["ba_f"]), (WZ[32:33, 256:512], w["ba_b"])]
    n_small = 16 * len(small_loads)
    release = []
    mod_release = []
    turn = "ad"

    with nc.Block() as block:

        @block.tensor
        def _(pe):
            B = banks()
            mine = dict(tile=0)

            def load():
                j = mine["tile"]
                mine["tile"] += 1
                pe.wait_ge(S["slot%d" % (j % 2)], 32 * (j // 2 + 1))
                return slots[j % 2]

            def used():
                release.append(("filled", B.filled_so_far()))

            def turn_norm(which):
                tt = OUT_T if which else IN_T
                pe.wait_ge(S["normed%d" % which], len(tt))
                n = 0
                for f in range(KD):
                    for a, cnt, r in spans(tt):
                        bank = B.fill(pe, turn[n % 2])
                        n += 1
                        for i in range(cnt // PT):
                            mm = pe.transpose(bank[:, i * PT:(i + 1) * PT], XNV[:, a // PT + i, f * PT:(f + 1) * PT], ident)
                        mm.then_inc(S["filled"], 1)

            def turn_columns(src, by, tt=None):
                for a, cnt, r in spans(tt or IN_T):
                    bank = B.fill(pe, by[0])
                    by.append(by.pop(0))
                    for i in range(cnt // PT):
                        mm = pe.transpose(bank[:, i * PT:(i + 1) * PT], src(a // PT + i), ident)
                    mm.then_inc(S["filled"], 1)

            pe.wait_ge(S["small"], n_small)
            if start_loads:
                pe.wait_ge(S["start"], 16 * len(start_loads))
            bank = B.fill(pe, "d")
            pe.transpose(bank[:, 0:nvec], VR[0:nvec, :], ident[0:nvec, 0:nvec]).then_inc(S["filled"], 1)

            def mod_chunk(wt):
                bank = B.fill(pe, "d")
                for k in range(KD):
                    for q in range(4):
                        mm = pe.matmul(bank[32 * q:32 * q + 32, 0:PT], SC32[:, k, :], wt[:, k, q * PT:(q + 1) * PT],
                                       start=(k == 0), stop=(k == KD - 1))
                mm.then_inc(S["filled"], 1)

            if start_loads:
                pe.wait_ge(S["silu_c"], 1)
                for j in range(12):
                    mod_chunk(load()[:, :].rearrange("p (k n) -> p k n", k=KD))
                    used()
            pe.wait_ge(S["mod_rows"], 1)
            for chunks in ((0, 1, 2, 3), (6, 7, 8, 9)):
                bank = B.fill(pe, "d")
                for i, c in enumerate(chunks):
                    mm = pe.transpose(bank[:, i * PT:(i + 1) * PT], ROWS[:, c * PT:(c + 1) * PT], ident)
                mm.then_inc(S["filled"], 1)
            for c in (4, 5, 10, 11):
                for r in range(R):
                    bank = B.fill(pe, "a")
                    for q in range(4):
                        pick = ident[:, 32 * q + r:32 * q + r + 1].broadcast_to([PT, PT])
                        mm = pe.matmul(bank[:, q * PT:(q + 1) * PT], pick, ROWS[:, c * PT:(c + 1) * PT], start=True, stop=True)
                    mm.then_inc(S["filled"], 1)

            turn_norm(0)

            B.all_emptied(pe)
            n = 0
            for j in range(8):
                wt = load()[:, 0:KD * CW].rearrange("p (k n) -> p k n", k=KD)
                for t in IN_T:
                    bank = B.fill(pe, turn[n % 2])
                    n += 1
                    for k in range(KD):
                        mm = pe.matmul(bank[:, 0:CW], HT[:, k, t * PT:(t + 1) * PT], wt[:, k, :], start=(k == 0), stop=(k == KD - 1))
                    mm.then_inc(S["filled"], 1)
                used()
            B.all_emptied(pe)

            def attention(name, us, prob, mlstm=False):
                ns = depth(us, mlstm)

                def scores(i):
                    u = us[i]
                    a, b = (PS[2 * (i % 2)], PS[2 * (i % 2) + 1]) if ns == 2 else (None, PS[i % ns])
                    if i >= ns:
                        pe.wait_ge(S[name + ("_prob" if mlstm else "_max")], i - ns + 1)
                    if mlstm:
                        pe.matmul(a[:, 0:u["nk"]], CN[0:4, C_SEL + 128 * u["h"]:C_SEL + 128 * (u["h"] + 1)],
                                  CT[:, 0:u["nk"]], start=True, stop=True)
                        mm = pe.matmul(b[:, 0:u["nk"]], u["q"], u["k"], start=True, stop=True)
                    else:
                        if u["na"]:
                            mm = pe.matmul(a[:, 0:u["na"]], u["q"], u["ka"], start=True, stop=True)
                        if u["nb"]:
                            mm = pe.matmul(b[:, 0:u["nb"]], u["q"], u["kb"], start=True, stop=True)
                    mm.then_inc(S[name + "_scores"], 1)

                def turned(i):
                    u = us[i]
                    nb = len(u["v"])
                    pe.wait_ge(S[name + prob], i + 1)
                    if i >= 1:
                        pe.wait_ge(S[name + "_turned_dve"], i)
                        if n_act(us, i):
                            pe.wait_ge(S[name + "_turned_act"], n_act(us, i))
                    src = (SM2 if mlstm else SB)[i % ns]
                    for j in range(nb):
                        mm = pe.transpose(PS[4 + j // 4][:, (j % 4) * PT:(j % 4 + 1) * PT], src[:, j * PT:(j + 1) * PT], ident)
                    mm.then_inc(S[name + "_turn"], 1)

                def values(i):
                    u = us[i]
                    pe.wait_ge(S[name + "_turned_dve"], i + 1)
                    if n_act(us, i + 1):
                        pe.wait_ge(S[name + "_turned_act"], n_act(us, i + 1))
                    if i >= 2:
                        pe.wait_ge(S[name + "_out"], i - 1)
                    pb = (PB2 if mlstm else PB)[i % 2]
                    for j, (t, c) in enumerate(u["v"]):
                        mm = pe.matmul(PS[6 + i % 2][:, 0:128], pb[:, j * PT:(j + 1) * PT], pr(t, c - u.get("off", 0), 128),
                                       start=(j == 0), stop=(j == len(u["v"]) - 1))
                    mm.then_inc(S[name + "_values"], 1)

                B.all_emptied(pe)
                for i in range(len(us) + ns):
                    if i < len(us):
                        scores(i)
                    if 0 <= i - ns + 1 < len(us):
                        turned(i - ns + 1)
                    if 0 <= i - ns < len(us):
                        values(i - ns)
                pe.wait_ge(S[name + "_out"], len(us))

            if not second:
                for a, cnt, r in spans(IN_T):
                    bank = B.fill(pe, "d")
                    for i in range(cnt // PT):
                        mm = pe.transpose(bank[0:32, i * PT:(i + 1) * PT], pr(a // PT + i, G_Z, 32), ident)
                    mm.then_inc(S["filled"], 1)
                B.all_emptied(pe)
                pe.wait_ge(S["z_ones"], 1)
                pe.wait_ge(S["z_loaded"], 16 * len(z_loads))
                for t in IN_T:
                    bank = B.fill(pe, turn[t % 2])
                    pe.matmul(bank[:, :], ZT[:, t * PT:(t + 1) * PT], WZ, start=True, stop=True).then_inc(S["filled"], 1)
                for f in range(2):
                    turn_columns(lambda t: pr(t, G_Q + 128 * f, 128), ["d"])
                    turn_columns(lambda t: pr(t, G_K + 128 * f, 128), ["d"])
                pe.wait_ge(S["log_decay"], 1)
                for d in (1, 0):
                    for f in range(2):
                        for a, cnt, r in spans(IN_T):
                            bank = B.fill(pe, "a")
                            for i in range(cnt // PT):
                                mm = pe.matmul(bank[:, i * PT:(i + 1) * PT], LA[:, a // PT + i, d * 256 + f * 128:d * 256 + f * 128 + 128],
                                               CN[:, C_TRI + 128 * d:C_TRI + 128 * (d + 1)], start=True, stop=True)
                            mm.then_inc(S["filled"], 1)
                for t in IN_T:
                    bank = B.fill(pe, "a")
                    for d in range(2):
                        mm = pe.matmul(bank[:, 256 * d:256 * (d + 1)], CN[:, C_TRI + 128 * (2 + d):C_TRI + 128 * (3 + d)],
                                       LA[:, t, 256 * d:256 * (d + 1)], start=True, stop=True)
                    mm.then_inc(S["filled"], 1)
                B.all_emptied(pe)
                pe.wait_ge(S["k_end"], 1)
                for d in range(2):
                    for c in range(NCH):
                        par, t, i = c % 2, c // 2, c // 2
                        b = PS[4 * d + 2 * par + i // 4]
                        for h in range(GLA_H):
                            hp, f = h % 2, h // 2
                            at = (i % 4) * 128 + f * 64
                            mm = pe.matmul(b[64 * hp:64 * hp + 64, at:at + 64], KE[64 * par:64 * par + 64, t, d, 64 * h:64 * h + 64],
                                           pr(t, G_V + 64 * h, 64)[64 * par:64 * par + 64, :], start=True, stop=True)
                mm.then_inc(S["chunk_sums"], 1)
                pe.wait_ge(S["states"], 1)
                for n, t in enumerate(OUT_T):
                    if n >= 2:
                        pe.wait_ge(S["masked"], n - 1)
                    for hp in range(2):
                        for d in range(2):
                            for f in range(2):
                                mm = pe.matmul(PS[2 * (n % 2) + hp][:, (d * 2 + f) * 128:(d * 2 + f + 1) * 128],
                                               KI[64 * hp:64 * hp + 64, d, f, t * PT:(t + 1) * PT],
                                               QI[64 * hp:64 * hp + 64, d, f, t * PT:(t + 1) * PT], start=True, stop=True)
                    mm.then_inc(S["products"], 1)
                    if n >= 1:
                        pe.wait_ge(S["gla_out"], n)
                    for hp in range(2):
                        for f in range(2):
                            for par in range(2):
                                c = 2 * t + par
                                dirs = [d for d in range(2) if c != first[d]]
                                for d in dirs:
                                    mm = pe.matmul(PS[6 + hp][64 * par:64 * par + 64, 64 * f:64 * f + 64],
                                                   QI[64 * hp:64 * hp + 64, d, f, c * CH:(c + 1) * CH],
                                                   SE[64 * hp:64 * hp + 64, d, c, f, :], start=(d == dirs[0]), stop=(d == dirs[-1]))
                    pe.wait_ge(S["masked"], n + 1)
                    for h in range(GLA_H):
                        for d in range(2):
                            mm = pe.matmul(PS[4][:, 64 * h:64 * h + 64], AM[n % 2][:, d, h, :], pr(t, G_V + 64 * h, 64),
                                           start=(d == 0), stop=(d == 1))
                    mm.then_inc(S["gla_sums"], 1)
                pe.wait_ge(S["gla_out"], len(OUT_T))

                bank = B.fill(pe, "d")
                pe.transpose(bank[0:31, 0:90], RPR, ident[0:90, 0:90]).then_inc(S["filled"], 1)
                B.all_emptied(pe)
                n = 0
                for j in range(2):
                    oh = load()[0:32, :].rearrange("p (c q) -> p c q", q=PT)
                    for g in range(8):
                        bank = B.fill(pe, turn[n % 2])
                        n += 1
                        for i in range(4):
                            mm = pe.matmul(bank[:, 128 * i:128 * i + 128], oh[:, 4 * g + i, :], RPT, start=True, stop=True)
                        mm.then_inc(S["filled"], 1)
                    used()
                for f in range(3):
                    turn_columns(lambda t: pr(t, N_Q + 128 * f, 128), ["a"], OUT_T)
                    turn_columns(lambda t: pr(t, N_K + 128 * f, 128), ["d"])
                attention("na", na_units, "_exp")

                pe.wait_ge(S["rope"], 1)
                for f in range(3):
                    turn_columns(lambda t: pr(t, S_Q + 128 * f, 128) if t < CTX_T else RQ[:, t - CTX_T, 128 * f:128 * f + 128], ["a"], OUT_T)
                for kv in range(2):
                    turn_columns(lambda t: RK[:, t, 128 * kv:128 * kv + 128], ["d"])
                attention("sw", sw_units, "_exp")
                pe.wait_ge(S["mixed"], 1)
            else:
                pe.wait_ge(S["cq"], 1)
                for k in range(2):
                    turn_columns(lambda t: pr(t, A_C + 128 * k, 128), ["d"])
                B.all_emptied(pe)
                wt = load()[:, 0:2048].rearrange("p (m k n) -> p m k n", m=2, k=2)
                for n in range(LAT_T):
                    for m in range(2):
                        bank = B.fill(pe, turn[m])
                        for k in range(2):
                            mm = pe.matmul(bank[:, :], CQ[:, k, n * PT:(n + 1) * PT], wt[:, m, k, :], start=(k == 0), stop=(k == 1))
                        mm.then_inc(S["filled"], 1)
                used()
                pe.wait_ge(S["rope"], 1)
                for f in range(4):
                    turn_columns(lambda t: QQ[:, t - CTX_T, 128 * f:128 * f + 128], ["a"])
                    turn_columns(lambda t: QQ[:, t - CTX_T, 512 + 128 * f:512 + 128 * f + 128], ["d"])
                    turn_columns(lambda t: pr(t, A_K + 128 * f, 128), ["a"])
                turn_columns(lambda t: KID[:, t - CTX_T, :], ["d"])
                B.all_emptied(pe)
                for n in range(1, LAT_T):
                    for h in range(8):
                        b, f = 64 * (h % 2), h // 2
                        bank = B.fill(pe, "a")
                        pe.matmul(bank[:, 0:128 * (n + 1)], QIT[b:b + 64, f, n * PT:(n + 1) * PT], KIT[b:b + 64, 0:128 * (n + 1)],
                                  start=True, stop=True).then_inc(S["filled"], 1)
                attention("at", at_units, "_exp")

                for f in range(8):
                    turn_columns(lambda t: pr(t, M_Q + 128 * f, 128), ["a"])
                pe.wait_ge(S["log_forget"], 1)
                bank = B.fill(pe, "d")
                for n in range(LAT_T):
                    for m in range(n + 1):
                        mm = pe.matmul(bank[:, 4 * n:4 * n + 4], CN[:, C_TRIF:C_TRIF + 128] if m == n else CN[:, C_ONE:C_ONE + 128],
                                       LF[:, m, :], start=(m == 0), stop=(m == n))
                mm.then_inc(S["filled"], 1)
                pe.wait_ge(S["gate_cols"], 1)
                bank = B.fill(pe, "d")
                for n in range(LAT_T):
                    mm = pe.transpose(bank[0:4, n * PT:(n + 1) * PT], T16[:, n, :], ident)
                mm.then_inc(S["filled"], 1)
                pe.wait_ge(S["conv_silu"], 1)
                attention("ml", ml_units, "_prob", mlstm=True)
                pe.wait_ge(S["mixed"], 1)

            n = 0
            for f in range(KD):
                for a, cnt, r in spans(OUT_T):
                    bank = B.fill(pe, turn[n % 2])
                    n += 1
                    for i in range(cnt // PT):
                        mm = pe.transpose(bank[:, i * PT:(i + 1) * PT], pr(a // PT + i, YF[f], 128), ident)
                    mm.then_inc(S["filled"], 1)
            B.all_emptied(pe)
            n = 0
            for j in range(2):
                wt = load()[:, :].rearrange("p (k n) -> p k n", k=KD)
                for t in OUT_T:
                    bank = B.fill(pe, turn[n % 2] if second else "d")
                    n += 1
                    for k in range(KD):
                        mm = pe.matmul(bank[:, :], HT[:, k, t * PT:(t + 1) * PT], wt[:, k, :], start=(k == 0), stop=(k == KD - 1))
                    mm.then_inc(S["filled"], 1)
                used()

            turn_norm(1)

            B.all_emptied(pe)

            def mod_beside(j):
                if j == 0:
                    pe.wait_ge(S["silu_next"], 1)
                pe.wait_ge(S["mod_landed"], 32 * (j + 1))
                mod_chunk(SLM.rearrange("p (k n) -> p k n", k=KD))
                mod_release.append(B.filled_so_far())

            for j in range(11):
                wt = load()[:, :].rearrange("p (m k n) -> p m k n", m=2, k=KD)
                for sub in range(2):
                    for a, cnt, r in spans(OUT_T):
                        for m in range(2):
                            bank = B.fill(pe, turn[m])
                            for k in range(KD):
                                mm = pe.matmul(bank[:, 0:cnt], wt[:, m, k, sub * 128:(sub + 1) * 128], HT[:, k, a:a + cnt],
                                               start=(k == 0), stop=(k == KD - 1))
                            mm.then_inc(S["filled"], 1)
                used()
                if nxt:
                    mod_beside(j)
            if nxt:
                mod_beside(11)
            B.all_emptied(pe)
            for half in range(2):
                for piece, (k0, k1) in enumerate(DOWN):
                    wt = load()[:, 0:(k1 - k0) * 512].rearrange("p (k n) -> p k n", n=512)
                    if piece == 0:
                        out_banks = [B.fill(pe, turn[t % 2] if second else "d") for t in OUT_T]
                    for t, bank in zip(OUT_T, out_banks):
                        for k in range(k0, k1):
                            mm = pe.matmul(bank[:, :], GT[:, k, t * PT - GOFF:(t + 1) * PT - GOFF], wt[:, k - k0, :],
                                           start=(k == 0), stop=(k == KF - 1))
                        if piece == 2:
                            mm.then_inc(S["filled"], 1)
                    if piece == 2:
                        used()
                    else:
                        mm.then_inc(S["down_part"], 1)
                        release.append(("down_part", 2 * half + piece + 1))
            assert mine["tile"] == len(tiles)

        @block.sync
        def _(sp):
            for dst, src in start_loads:
                sp.dma_start(dst, src).then_inc(S["start"], 16)
            for dst, src in small_loads:
                sp.dma_start(dst, src).then_inc(S["small"], 16)
            first_ffn = len(tiles) - 17
            for j, parts in enumerate(tiles):
                if j == first_ffn - 8 and z_loads:
                    sp.wait_ge(S["zeroed"], 1)
                    for dst, src in z_loads:
                        sp.dma_start(dst, src).then_inc(S["z_loaded"], 16)
                if j >= 2:
                    name, n = release[j - 2]
                    sp.wait_ge(S[name], n)
                for dst, src in parts:
                    sp.dma_start(dst, src).then_inc(S["slot%d" % (j % 2)], 16)
                c = j - first_ffn
                if nxt and 0 <= c < 12:
                    if c == 0:
                        sp.wait_ge(S["mod_room"], 1)
                    else:
                        sp.wait_ge(S["filled"], mod_release[c - 1])
                    src = nxt["w_mod"][:, 512 * c:512 * (c + 1)].rearrange("(k p) n -> p k n", p=PT)
                    dst = SLM.rearrange("p (k n) -> p k n", k=KD)
                    for h in (slice(0, 4), slice(4, 8)):
                        sp.dma_start(dst[:, h], src[:, h]).then_inc(S["mod_landed"], 16)

        @block.gpsimd
        def _(pool):
            if not second:
                pool.wait_ge(S["rows_read"], 1)
                pool.memset(WZ, 0.0).then_inc(S["zeroed"], 1)
                pool.wait_ge(S["zeroed"], 1)
                pool.memset(ZT[32:33, :], 1.0).then_inc(S["z_ones"], 1)

        @block.scalar
        def _(act):
            B = banks()
            steps = [0]

            def step(ins):
                steps[0] += 1
                ins.then_inc(S["act_step"], 1)
                act.wait_ge(S["act_step"], steps[0])

            def copy_out(bank, dst):
                act.activation(dst, bank, ACT.Copy).then_inc(S["emptied_act"], 1)

            nroot = [0]

            def modulate(which, tt):
                n = 0
                for f in range(KD):
                    for a, cnt, r in spans(tt):
                        bank = B.empty(act, turn[n % 2], "a")
                        n += 1
                        if bank is not None:
                            act.activation(HT[:, f, a:a + cnt], bank[:, 0:cnt], ACT.Identity, scale=AT[:, which, f, r:r + 1],
                                           bias=MT[:, 2 * which, f, r:r + 1]).then_inc(S["emptied_act"], 1)

            def roots(n):
                nroot[0] += 1
                act.wait_ge(S["mean_sq"], nroot[0])
                act.activation(ssq[:, 0:n], ssq[:, 0:n], ACT.Sqrt).then_inc(S["root"], 1)

            def columns(dst, by, tt=None):
                for a, cnt, r in spans(tt or IN_T):
                    bank = B.empty(act, by, "a")
                    if bank is not None:
                        copy_out(bank[:, 0:cnt], dst(a, cnt))

            def attention(name, us, scale, mlstm=False):
                sb, pb = (SB2, PB2) if mlstm else (SB, PB)
                ns = depth(us, mlstm)
                for i in range(len(us) + ns - 1):
                    if i < len(us):
                        u = us[i]
                        if not mlstm and u["na"]:
                            act.wait_ge(S[name + "_scores"], i + 1)
                            if i >= 2:
                                act.wait_ge(S[name + "_turn"], i - 1)
                            ins = act.activation(sb[i % 2][:, 0:256], PS[2 * (i % 2)][:, 0:256], ACT.Copy, scale=scale)
                            if u["sink"] is not None:
                                ins = act.activation(sb[i % 2][:, u["n"]:u["n"] + 1], u["sink"], ACT.Copy)
                            ins.then_inc(S[name + "_ctx"], 1)
                        act.wait_ge(S[name + "_max"], i + 1)
                        c = i % 4
                        if mlstm:
                            act.activation(sb[i % 2][:, 0:u["nk"]], sb[i % 2][:, 0:u["nk"]], ACT.Exp, bias=nm[:, c:c + 1])
                            act.activation(fl[:, c:c + 1], BC[:, u["n"], u["h"]:u["h"] + 1], ACT.Exp, scale=-1.0,
                                           bias=nm[:, c:c + 1]).then_inc(S[name + "_exp"], 1)
                        else:
                            m = u["n"] + (u["sink"] is not None)
                            act.activation(sb[i % ns][:, 0:m], sb[i % ns][:, 0:m], ACT.Exp, bias=nm[:, c:c + 1],
                                           accum_out=rs[:, c:c + 1]).then_inc(S[name + "_exp"], 1)
                    if i >= ns - 1:
                        k = i - ns + 1
                        nb = len(us[k]["v"])
                        if nb > 4:
                            act.wait_ge(S[name + "_turn"], k + 1)
                            if k >= 2:
                                act.wait_ge(S[name + "_values"], k - 1)
                            act.activation(pb[k % 2][:, 512:128 * nb], PS[5][:, 0:128 * (nb - 4)], ACT.Copy).then_inc(S[name + "_turned_act"], 1)

            def silu_rows(at, event):
                out = SC32.rearrange("p k (m r) -> p k m r", r=len(at))
                for r, v in enumerate(at):
                    ins = act.activation(out[:, :, :, r], VT[:, v:v + 8].unsqueeze(2).broadcast_to([PT, KD, 32 // len(at)]), ACT.Silu)
                ins.then_inc(S[event], 1)

            act.wait_ge(S["vectors"], 1)
            B.empty(act, "d", "a")
            if start_loads:
                silu_rows([V_C, V_CC], "silu_c")
                for j in range(12):
                    B.empty(act, "d", "a")
            for _ in range(2):
                B.empty(act, "d", "a")
            for s_ in range(2):
                for half in range(2):
                    for r in range(R):
                        bank = B.empty(act, "a", "a")
                        copy_out(bank[:, :], GBV[:, s_, r, half * 512:(half + 1) * 512])
            act.sem_inc(S["rows_read"], 1)
            roots(len(IN_T))
            modulate(0, IN_T)

            n = 0
            for j in range(8):
                for t in IN_T:
                    bank = B.empty(act, turn[n % 2], "a")
                    n += 1
                    if bank is not None:
                        copy_out(bank[:, 0:CW], pr(t, CW * j, CW))

            if not second:
                for _ in spans(IN_T):
                    B.empty(act, "d", "a")
                for t in IN_T:
                    bank = B.empty(act, turn[t % 2], "a")
                    if bank is not None:
                        copy_out(bank[:, :], LA[:, t, :])
                for f in range(2):
                    columns(None, "d")
                    columns(None, "d")
                la = SC[:, 6144:9216]
                act.wait_ge(S["abs_z"], 1)
                step(act.activation(la, la, ACT.Exp, scale=-1.0))
                act.activation(la, la, ACT.Ln, bias=ones_col).then_inc(S["ln_z"], 1)
                k = 0
                for d in (1, 0):
                    for f in range(2):
                        for i, (a, cnt, r) in enumerate(spans(IN_T)):
                            bank = B.empty(act, "a", "a")
                            if k and i == 0:
                                act.wait_ge(S["decay_used"], k)
                            act.activation(EB[0][:, a:a + cnt], bank[:, 0:cnt], ACT.Exp)
                            act.activation(EB[1][:, a:a + cnt], bank[:, 0:cnt], ACT.Exp, scale=-1.0).then_inc(S["emptied_act"], 1)
                        k += 1
                for t in IN_T:
                    bank = B.empty(act, "a", "a")
                    act.activation(KE[:, t].rearrange("p d n -> p (d n)"), bank[:, :], ACT.Exp).then_inc(S["emptied_act"], 1)
                gg = PW[:, O0 - T0:, G_G:G_G + 256]
                act.activation(gg, gg, ACT.Silu).then_inc(S["gate_act"], 1)
                roots(len(OUT_T) * GLA_H)
                B.empty(act, "d", "a")
                n = 0
                for g in range(16):
                    bank = B.empty(act, turn[n % 2], "a")
                    n += 1
                    if bank is not None:
                        for half in range(2):
                            ins = act.activation(nb_part(NB, g, half), bank_part(bank, half), ACT.Copy)
                        ins.then_inc(S["emptied_act"], 1)
                for f in range(3):
                    columns(lambda a, cnt: QN[:, f, a:a + cnt], "a", OUT_T)
                    columns(None, "d")
                attention("na", na_units, 0.125)
                for f in range(3):
                    columns(lambda a, cnt: QS[:, f, a:a + cnt], "a", OUT_T)
                for kv in range(2):
                    columns(None, "d")
                attention("sw", sw_units, 0.125)
            else:
                act.wait_ge(S["angles"], 1)
                act.activation(CSN[:, :, 1, :], ANG[0].rearrange("p (t f) -> p t f", t=4), ACT.Sin)
                act.activation(CSN[:, :, 0, :], ANG[1].rearrange("p (t f) -> p t f", t=4), ACT.Sin).then_inc(S["cos_sin"], 1)
                roots(LAT_T)
                for k in range(2):
                    columns(None, "d")
                for n in range(LAT_T):
                    for m in range(2):
                        bank = B.empty(act, turn[m], "a")
                        if bank is not None:
                            copy_out(bank[:, :], QQ[:, n, m * 512:(m + 1) * 512])
                for f in range(4):
                    columns(lambda a, cnt: QTT[:, f, :], "a")
                    columns(None, "d")
                    columns(lambda a, cnt: KTT[:, f, :], "a")
                columns(None, "d")
                g = 0
                act.wait_ge(S["turned_all"], 1)
                for n in range(1, LAT_T):
                    for h in range(8):
                        bank = B.empty(act, "a", "a")
                        if g >= 2:
                            act.wait_ge(S["index_sum"], g - 1)
                        act.activation(RL[g % 2][:, 0:128 * (n + 1)], bank[:, 0:128 * (n + 1)], ACT.Relu).then_inc(S["emptied_act"], 1)
                        g += 1
                attention("at", at_units, 0.125)
                roots(LAT_T * ATT_H)
                for f in range(8):
                    bank = B.empty(act, "a", "a")
                    if f >= 2:
                        act.wait_ge(S["conv"], f - 1)
                    copy_out(bank[:, :], CP[f % 2][:, 3:515])
                act.wait_ge(S["abs_f"], 1)
                step(act.activation(T16[:, :, :], T16[:, :, :], ACT.Exp, scale=-1.0))
                act.activation(T16[:, :, :], T16[:, :, :], ACT.Ln, bias=ones_col).then_inc(S["ln_f"], 1)
                act.wait_ge(S["conv"], 8)
                act.activation(SC[:, 0:4096], SC[:, 0:4096], ACT.Silu).then_inc(S["conv_silu"], 1)
                og = PW[:, :, M_O:M_O + 512]
                act.activation(og, og, ACT.Sigmoid).then_inc(S["gate_act"], 1)
                B.empty(act, "d", "a")
                B.empty(act, "d", "a")
                attention("ml", ml_units, None, mlstm=True)
                roots(LAT_T * ML_H)

            n = 0
            for f in range(KD):
                for a, cnt, r in spans(OUT_T):
                    bank = B.empty(act, turn[n % 2], "a")
                    n += 1
                    if bank is not None:
                        copy_out(bank[:, 0:cnt], HT[:, f, a:a + cnt])
            n = 0
            for j in range(2):
                for t in OUT_T:
                    bank = B.empty(act, turn[n % 2] if second else "d", "a")
                    n += 1
                    if bank is not None:
                        copy_out(bank[:, :], YBV[:, t - CTX_T, 512 * j:512 * (j + 1)])
            if second:
                roots(LAT_T)
            roots(len(OUT_T))
            modulate(1, OUT_T)

            if nxt:
                act.wait_ge(S["mod_room"], 1)
                silu_rows([V_NEXT + 8 * i for i in range(n_next)], "silu_next")
            q, read = 0, []
            for j in range(22):
                for a, cnt, r in spans(OUT_T):
                    bank = B.empty(act, "a", "a")
                    if q >= 2:
                        act.wait_ge(S["emptied_dve"], read[q - 2])
                    act.activation(SG[q % 2][:, 0:cnt], bank[:, 0:cnt], ACT.Silu).then_inc(S["emptied_act"], 1)
                    B.empty(act, "d", "a")
                    read.append(B.emptied_by("d"))
                    q += 1
                if nxt and j % 2:
                    B.empty(act, "d", "a")
            if nxt:
                B.empty(act, "d", "a")
            for half in range(2):
                for t in OUT_T:
                    bank = B.empty(act, turn[t % 2] if second else "d", "a")
                    if bank is not None:
                        copy_out(bank[:, :], YBV[:, t - CTX_T, 512 * half:512 * (half + 1)])
            if second:
                roots(LAT_T)

        @block.vector
        def _(dve):
            B = banks()
            steps = [0]

            def step(ins):
                steps[0] += 1
                ins.then_inc(S["dve_step"], 1)
                dve.wait_ge(S["dve_step"], steps[0])

            def copy_out(bank, dst):
                dve.tensor_copy(dst, bank).then_inc(S["emptied_dve"], 1)

            nroot = [0]

            def inverse_root(n, width, dst=None):
                dve.tensor_scalar(ssq[:, 0:n], ssq[:, 0:n], 1.0 / width, EPS, ALU.mult, ALU.add).then_inc(S["mean_sq"], 1)
                nroot[0] += 1
                dve.wait_ge(S["root"], nroot[0])
                step(dve.reciprocal(rstd[:, 0:n], ssq[:, 0:n]))

            def square_sums(src, junk, cols_):
                for i in range(len(src)):
                    ins = dve.tensor_tensor_reduce(junk[i], src[i], src[i], 1.0, 0.0, ALU.mult, ALU.add, ssq[:, i:i + 1])
                step(ins)

            def norm(which, tt):
                square_sums([XV[:, t, :] for t in tt], [XNV[:, t, :] for t in tt], None)
                inverse_root(len(tt), D)
                for i, t in enumerate(tt):
                    dve.tensor_scalar(XNV[:, t, :], XV[:, t, :], rstd[:, i:i + 1], None, ALU.mult).then_inc(S["normed%d" % which], 1)

            def modulate(which, tt):
                n = 0
                for f in range(KD):
                    for a, cnt, r in spans(tt):
                        bank = B.empty(dve, turn[n % 2], "d")
                        n += 1
                        if bank is not None:
                            dve.tensor_scalar(HT[:, f, a:a + cnt], bank[:, 0:cnt], AT[:, which, f, r:r + 1],
                                              MT[:, 2 * which, f, r:r + 1], ALU.mult, ALU.add).then_inc(S["emptied_dve"], 1)

            def columns(dst, by, tt=None):
                for a, cnt, r in spans(tt or IN_T):
                    bank = B.empty(dve, by, "d")
                    if bank is not None:
                        copy_out(bank[:, 0:cnt], dst(a, cnt))

            def head_norm(y, nt, H, dh, gain, gate):
                n = H * dh
                sq = SC[:, 0:nt * n].rearrange("p (t n) -> p t n", n=n)
                step(dve.tensor_tensor(sq, y, y, ALU.mult))
                step(dve.tensor_reduce(ssq[:, 0:nt * H].rearrange("p (t h) -> p t h", h=H),
                                       sq.rearrange("p t (h d) -> p t h d", h=H), AX, ALU.add))
                inverse_root(nt * H, dh)
                r4 = rstd[:, 0:nt * H].rearrange("p (t h) -> p t h", h=H).unsqueeze(3).broadcast_to([PT, nt, H, dh])
                y4 = y.rearrange("p t (h d) -> p t h d", h=H)
                step(dve.tensor_tensor(y4, y4, r4, ALU.mult))
                step(dve.tensor_tensor(y, y, gain.unsqueeze(1).broadcast_to([PT, nt, n]), ALU.mult))
                if gate is not None:
                    dve.wait_ge(S["gate_act"], 1)
                    step(dve.tensor_tensor(y, y, gate, ALU.mult))

            def rotate(x, dst, H, cos, sin, tmp):
                c = cos.unsqueeze(2).broadcast_to([PT, 4, H, 32])
                s_ = sin.unsqueeze(2).broadcast_to([PT, 4, H, 32])
                x1, x2, d1, d2 = x[:, :, :, 0:32], x[:, :, :, 32:64], dst[:, :, :, 0:32], dst[:, :, :, 32:64]
                t1, t2 = (z[:, 0:4 * H * 32].rearrange("p (t h f) -> p t h f", t=4, h=H) for z in tmp)
                dve.tensor_tensor(t1, x1, s_, ALU.mult)
                step(dve.tensor_tensor(t2, x2, s_, ALU.mult))
                dve.tensor_tensor(d1, x1, c, ALU.mult)
                step(dve.tensor_tensor(d2, x2, c, ALU.mult))
                dve.tensor_tensor(d1, d1, t2, ALU.subtract)
                return dve.tensor_tensor(d2, d2, t1, ALU.add)

            def attention(name, us, scale, mlstm=False):
                pb = PB2 if mlstm else PB
                ns = depth(us, mlstm)
                n_ctx = [0]

                def weigh(i):
                    u, s_, c = us[i], (SB2 if mlstm else SB)[i % ns], i % 4
                    a, b = (PS[2 * (i % 2)], PS[2 * (i % 2) + 1]) if ns == 2 else (None, PS[i % ns])
                    dve.wait_ge(S[name + "_scores"], i + 1)
                    if mlstm:
                        nk = u["nk"]
                        step(dve.tensor_tensor(s_[:, 0:nk], a[:, 0:nk], CN[:, C_CAU + 512 - nk:C_CAU + 512], ALU.add))
                        step(dve.reduce_max(nm[:, c:c + 1], s_[:, 0:nk], AX))
                        dve.tensor_scalar(nm[:, c:c + 1], nm[:, c:c + 1], 0.0, -1.0, ALU.max, ALU.mult).then_inc(S[name + "_max"], 1)
                        dve.wait_ge(S[name + "_exp"], i + 1)
                        if i >= 2:
                            dve.wait_ge(S[name + "_turn"], i - 1)
                        dve.scalar_tensor_tensor(SM2[i % 2][:, 0:nk], b[:, 0:nk], float(np.float32(128 ** -0.5)), s_[:, 0:nk],
                                                 ALU.mult, ALU.mult, accum_out=rs[:, c:c + 1]).then_inc(S[name + "_prob"], 1)
                        return
                    if i >= ns:
                        dve.wait_ge(S[name + "_turn"], i - ns + 1)
                    na, nb = u["na"], u["nb"]
                    if nb:
                        step(dve.scalar_tensor_tensor(s_[:, na:na + nb], b[:, 0:nb], scale, u["bias"], ALU.mult, ALU.add))
                    if na:
                        n_ctx[0] += 1
                        dve.wait_ge(S[name + "_ctx"], n_ctx[0])
                    m = u["n"] + (u["sink"] is not None)
                    dve.reduce_max(nm[:, c:c + 1], s_[:, 0:m], AX, negate=True).then_inc(S[name + "_max"], 1)

                def turned(i):
                    nb = min(len(us[i]["v"]), 4)
                    dve.wait_ge(S[name + "_turn"], i + 1)
                    if i >= 2:
                        dve.wait_ge(S[name + "_values"], i - 1)
                    dve.tensor_copy(pb[i % 2][:, 0:128 * nb], PS[4][:, 0:128 * nb]).then_inc(S[name + "_turned_dve"], 1)

                def output(i):
                    u, c = us[i], i % 4
                    dve.wait_ge(S[name + "_exp"], i + 1)
                    if mlstm:
                        dve.wait_ge(S[name + "_prob"], i + 1)
                        step(dve.scalar_tensor_tensor(rr[:, c:c + 1], rs[:, c:c + 1], -1.0, rs[:, c:c + 1], ALU.mult, ALU.max))
                        step(dve.tensor_tensor(rr[:, c:c + 1], rr[:, c:c + 1], fl[:, c:c + 1], ALU.max))
                        step(dve.reciprocal(rr[:, c:c + 1], rr[:, c:c + 1]))
                    else:
                        step(dve.reciprocal(rr[:, c:c + 1], rs[:, c:c + 1]))
                    dve.wait_ge(S[name + "_values"], i + 1)
                    dv, off = u["y"].shape[-1], u.get("off", 0)
                    dve.tensor_scalar(u["y"], PS[6 + i % 2][:, off:off + dv], rr[:, c:c + 1], None, ALU.mult).then_inc(S[name + "_out"], 1)

                for i in range(len(us) + ns):
                    if i < len(us):
                        weigh(i)
                    if 0 <= i - ns + 1 < len(us):
                        turned(i - ns + 1)
                    if 0 <= i - ns < len(us):
                        output(i - ns)
                dve.wait_ge(S[name + "_out"], len(us))

            dve.wait_ge(S["small"], n_small)
            if start_loads:
                dve.wait_ge(S["start"], 16 * len(start_loads))
            bank = B.empty(dve, "d", "d")
            dve.tensor_copy(VT[:, 0:nvec], bank[:, 0:nvec]).then_inc(S["emptied_dve"], 1)
            dve.wait_ge(S["emptied_dve"], 1)
            dve.sem_inc(S["vectors"], 1)

            def mod_chunk(c):
                bank = B.empty(dve, "d", "d")
                copy_out(bank[:, 0:PT], ROWS[:, c * PT:(c + 1) * PT])

            if start_loads:
                for c in range(12):
                    mod_chunk(c)
                dve.wait_ge(S["emptied_dve"], B.emptied_by("d"))
            if second:
                step(dve.tensor_tensor(ROWS, ROWS, BR, ALU.add))
                for i in range(2):
                    g = ROWS[:, (4 + 6 * i) * PT:(6 + 6 * i) * PT]
                    ins = dve.tensor_tensor(g, g, PO[:, 256 * i:256 * (i + 1)], ALU.mult)
                ins.then_inc(S["mod_rows"], 1)
            else:
                dve.tensor_tensor(ROWS, ROWS, BR, ALU.add).then_inc(S["mod_rows"], 1)
            for i in range(2):
                bank = B.empty(dve, "d", "d")
                dve.tensor_copy(MT[:, 2 * i:2 * i + 2].rearrange("p s k r -> p (s k) r"),
                                bank.rearrange("p (k m) -> p k m", m=32)[:, :, 0:R]).then_inc(S["emptied_dve"], 1)
            dve.wait_ge(S["emptied_dve"], B.emptied_by("d"))
            for s_, v in ((0, V_N1), (1, V_N2)):
                for r in range(R):
                    ins = dve.scalar_tensor_tensor(AT[:, s_, :, r], MT[:, 2 * s_ + 1, :, r], 1.0, VT[:, v:v + 8], ALU.add, ALU.mult)
            step(ins)
            for _ in range(4 * R):
                B.empty(dve, "a", "d")
            norm(0, IN_T)
            modulate(0, IN_T)

            n = 0
            for j in range(8):
                for t in IN_T:
                    bank = B.empty(dve, turn[n % 2], "d")
                    n += 1
                    if bank is not None:
                        copy_out(bank[:, 0:CW], pr(t, CW * j, CW))

            if not second:
                for a, cnt, r in spans(IN_T):
                    bank = B.empty(dve, "d", "d")
                    copy_out(bank[0:32, 0:cnt], ZT[0:32, a:a + cnt])
                for t in IN_T:
                    bank = B.empty(dve, turn[t % 2], "d")
                    if bank is not None:
                        copy_out(bank[:, :], LA[:, t, :])
                B.all_emptied(dve)
                la = SC[:, 6144:9216]
                dve.tensor_scalar(MN, la, 0.0, None, ALU.min)
                dve.scalar_tensor_tensor(la, la, -1.0, la, ALU.mult, ALU.max).then_inc(S["abs_z"], 1)
                for f in range(2):
                    columns(lambda a, cnt: QI[:, 0, f, a:a + cnt], "d")
                    columns(lambda a, cnt: KI[:, 0, f, a:a + cnt], "d")
                dve.wait_ge(S["emptied_dve"], B.emptied_by("d"))
                dve.wait_ge(S["ln_z"], 1)
                dve.tensor_tensor(la, MN, la, ALU.subtract).then_inc(S["log_decay"], 1)
                for d in (1, 0):
                    for f in range(2):
                        for _ in spans(IN_T):
                            B.empty(dve, "a", "d")
                        dve.wait_ge(S["emptied_act"], B.emptied_by("a"))
                        edge = EB[0].rearrange("p (c s) -> p c s", s=CH)[:, :, CH - 1 if d == 0 else 0]
                        dve.tensor_copy(DEC[:, d, f, :], edge)
                        dve.scalar_tensor_tensor(QI[:, d, f, :], EB[0], HD ** -0.5, QI[:, 0, f, :], ALU.mult, ALU.mult)
                        dve.tensor_tensor(KI[:, d, f, :], EB[1], KI[:, 0, f, :], ALU.mult).then_inc(S["decay_used"], 1)
                for _ in IN_T:
                    B.empty(dve, "a", "d")
                dve.wait_ge(S["emptied_act"], B.emptied_by("a"))
                for d in range(2):
                    ins = dve.tensor_tensor(KE[:, :, d, :], KE[:, :, d, :], PW[:, :, G_K:G_K + 256], ALU.mult)
                ins.then_inc(S["k_end"], 1)
                dve.wait_ge(S["chunk_sums"], 1)
                for k in range(NCH - 1):
                    for d in range(2):
                        c, after = order[d][k], order[d][k + 1]
                        i = c // 2
                        sums = PS[4 * d + 2 * (c % 2) + i // 4][:, (i % 4) * 128:(i % 4 + 1) * 128]
                        for f in range(2):
                            if k == 0:
                                ins = dve.tensor_copy(SE[:, d, after, f, :], sums[:, 64 * f:64 * f + 64])
                            else:
                                ins = dve.scalar_tensor_tensor(SE[:, d, after, f, :], SE[:, d, c, f, :], DEC[:, d, f, c:c + 1],
                                                               sums[:, 64 * f:64 * f + 64], ALU.mult, ALU.add)
                    step(ins)
                dve.sem_inc(S["states"], 1)
                for n, t in enumerate(OUT_T):
                    dve.wait_ge(S["products"], n + 1)
                    if n >= 2:
                        dve.wait_ge(S["gla_sums"], n - 1)
                    for hp in range(2):
                        b4 = PS[2 * (n % 2) + hp].rearrange("p (d f n) -> p d f n", d=2, f=2)
                        for d in range(2):
                            tri = CN[:, C_TRI + 128 * d:C_TRI + 128 * (d + 1)].unsqueeze(1).broadcast_to([PT, 2, PT])
                            ins = dve.scalar_tensor_tensor(AM[n % 2].rearrange("p d (f q) n -> p d f q n", q=2)[:, d, :, hp, :],
                                                           b4[:, d], 16.0, tri, ALU.mult, ALU.mult)
                    ins.then_inc(S["masked"], 1)
                    dve.wait_ge(S["gla_sums"], n + 1)
                    y = pr(t, G_Q, 256)
                    step(dve.tensor_copy(y, PS[4][:, 0:256]))
                    y4 = y.rearrange("p (f q e) -> p f q e", f=2, q=2)
                    for hp in range(2):
                        ins = dve.tensor_tensor(y4[:, :, hp, :], y4[:, :, hp, :], PS[6 + hp][:, 0:128].rearrange("p (f e) -> p f e", f=2), ALU.add)
                    ins.then_inc(S["gla_out"], 1)
                dve.wait_ge(S["gla_out"], len(OUT_T))
                head_norm(PW[:, O0 - T0:, G_Q:G_Q + 256], len(OUT_T), GLA_H, HD, GN, PW[:, O0 - T0:, G_G:G_G + 256])

                step(dve.memset(RPT, 1.0))
                bank = B.empty(dve, "d", "d")
                copy_out(bank[0:31, 0:90], RPT[0:31, 0:90])
                n = 0
                for g in range(16):
                    bank = B.empty(dve, turn[n % 2], "d")
                    n += 1
                    if bank is not None:
                        for half in range(2):
                            ins = dve.tensor_copy(nb_part(NB, g, half), bank_part(bank, half))
                        ins.then_inc(S["emptied_dve"], 1)
                for f in range(3):
                    columns(None, "a", OUT_T)
                    columns(lambda a, cnt: KN[:, f, a:a + cnt], "d")
                B.all_emptied(dve)
                attention("na", na_units, 0.125)

                cs = CN[:, C_ROPE:C_ROPE + 256].rearrange("p (t c f) -> p t c f", t=4, c=2)
                lat = PW[:, CTX_T:, :]
                step(rotate(lat[:, :, S_Q:S_Q + 384].rearrange("p t (h e) -> p t h e", e=64), RQ.rearrange("p t (h e) -> p t h e", e=64),
                            6, cs[:, :, 0, :], cs[:, :, 1, :], RT))
                rk = RK.rearrange("p t (k q e) -> p t k q e", k=2, q=2)
                step(rotate(lat[:, :, S_K:S_K + 128].rearrange("p t (h e) -> p t h e", e=64), rk[:, CTX_T:, :, 0, :],
                            2, cs[:, :, 0, :], cs[:, :, 1, :], RT))
                dve.tensor_copy(rk[:, CTX_T:, :, 1, :], rk[:, CTX_T:, :, 0, :])
                for q in range(2):
                    ins = dve.tensor_copy(rk[:, 0:CTX_T, :, q, :], PW[:, 0:CTX_T, S_K:S_K + 128].rearrange("p t (h e) -> p t h e", e=64))
                ins.then_inc(S["rope"], 1)
                for f in range(3):
                    columns(None, "a", OUT_T)
                for kv in range(2):
                    columns(lambda a, cnt: KS[:, kv, a:a + cnt], "d")
                attention("sw", sw_units, 0.125)
                dve.sem_inc(S["mixed"], 1)
            else:
                step(dve.tensor_copy(PF, PI32[:, :]))
                for t in range(LAT_T):
                    ins = dve.tensor_scalar(ANG[0][:, 32 * t:32 * t + 32], CN[:, C_FREQ:C_FREQ + 32], PF[:, t:t + 1], None, ALU.mult)
                step(ins)
                step(dve.tensor_scalar(ANG[1], ANG[0], float(1 / (2 * np.pi)), ROUND, ALU.mult, ALU.add))
                step(dve.tensor_scalar(ANG[1], ANG[1], ROUND, None, ALU.subtract))
                for c in (TWO_PI_1, TWO_PI_2, TWO_PI_3):
                    step(dve.scalar_tensor_tensor(ANG[0], ANG[1], -c, ANG[0], ALU.mult, ALU.add))
                step(dve.tensor_scalar(ANG[0], ANG[0], 3.1415925, -3.1415925, ALU.min, ALU.max))
                step(dve.scalar_tensor_tensor(ANG[1], ANG[0], -1.0, ANG[0], ALU.mult, ALU.max))
                dve.tensor_scalar(ANG[1], ANG[1], -1.0, float(np.pi / 2), ALU.mult, ALU.add).then_inc(S["angles"], 1)
                B.all_emptied(dve)
                junk = RT[0]
                for t in range(LAT_T):
                    c = pr(CTX_T + t, A_C, 256)
                    ins = dve.tensor_tensor_reduce(junk[:, 0:256], c, c, 1.0, 0.0, ALU.mult, ALU.add, ssq[:, t:t + 1])
                    step(ins)
                inverse_root(LAT_T, 256)
                for t in range(LAT_T):
                    c = pr(CTX_T + t, A_C, 256)
                    ins = dve.tensor_scalar(c, c, rstd[:, t:t + 1], None, ALU.mult)
                ins.then_inc(S["cq"], 1)
                for k in range(2):
                    bank = B.empty(dve, "d", "d")
                    dve.tensor_scalar(CQ[:, k, :], bank[:, :], VT[:, V_QL + k:V_QL + k + 1], None, ALU.mult).then_inc(S["emptied_dve"], 1)
                for n in range(LAT_T):
                    for m in range(2):
                        bank = B.empty(dve, turn[m], "d")
                        if bank is not None:
                            copy_out(bank[:, :], QQ[:, n, m * 512:(m + 1) * 512])
                B.all_emptied(dve)
                dve.wait_ge(S["cos_sin"], 1)
                cos, sin = CSN[:, :, 0, :], CSN[:, :, 1, :]
                for x in (QQ[:, :, 0:512], QQ[:, :, 512:1024], PW[:, :, A_K:A_K + 512]):
                    x4 = x.rearrange("p t (h e) -> p t h e", e=64)
                    step(rotate(x4, x4, 8, cos, sin, RT))
                ki = PW[:, :, A_KI:A_KI + 64].rearrange("p t (h e) -> p t h e", e=64)
                kid = KID.rearrange("p t (h e) -> p t h e", e=64)
                step(rotate(ki, kid[:, :, 0:1, :], 1, cos, sin, RT))
                dve.tensor_scalar(WI, PW[:, :, A_WI:A_WI + 8], float(np.float32(512 ** -0.5)), None, ALU.mult)
                dve.tensor_copy(kid[:, :, 1:2, :], kid[:, :, 0:1, :]).then_inc(S["rope"], 1)
                dve.wait_ge(S["rope"], 1)
                for f in range(4):
                    columns(None, "a")
                    columns(lambda a, cnt: QIT[:, f, :], "d")
                    columns(None, "a")
                columns(lambda a, cnt: KIT, "d")
                B.all_emptied(dve)
                dve.sem_inc(S["turned_all"], 1)
                g = 0
                cau = CN[:, C_CAU + 384:C_CAU + 512]
                dve.tensor_copy(MK[:, 0:128], cau)
                for n in range(1, LAT_T):
                    nk = 128 * (n + 1)
                    for h in range(8):
                        B.empty(dve, "a", "d")
                        dve.wait_ge(S["emptied_act"], B.emptied_by("a"))
                        if h == 0:
                            dve.tensor_scalar(SCO[:, 0:nk], RL[g % 2][:, 0:nk], WI[:, n, h:h + 1], None, ALU.mult).then_inc(S["index_sum"], 1)
                        else:
                            dve.scalar_tensor_tensor(SCO[:, 0:nk], RL[g % 2][:, 0:nk], WI[:, n, h:h + 1], SCO[:, 0:nk],
                                                     ALU.mult, ALU.add).then_inc(S["index_sum"], 1)
                        g += 1
                        dve.wait_ge(S["index_sum"], g)
                    step(dve.tensor_tensor(SCO[:, nk - 128:nk], SCO[:, nk - 128:nk], cau, ALU.add))
                    for r in range(TOPK // 8):
                        src = (SCO if r == 0 else WK)[:, 0:nk]
                        step(dve.max(m8, src))
                        step(dve.match_replace(WK[:, 0:nk], m8, src, TAKEN))
                    step(dve.tensor_tensor(WK[:, 0:nk], WK[:, 0:nk], SCO[:, 0:nk], ALU.is_equal))
                    mk = MK[:, MKO[n]:MKO[n] + nk]
                    step(dve.tensor_scalar(mk, WK[:, 0:nk], NEG, None, ALU.mult))
                    step(dve.tensor_tensor(mk[:, nk - 128:nk], mk[:, nk - 128:nk], cau, ALU.add))
                attention("at", at_units, 0.125)
                head_norm(PW[:, :, A_K:A_K + 512], LAT_T, ATT_H, HD, P[:, ROWN:ROWN + 512], None)

                dve.tensor_tensor(IG, PW[:, :, M_I:M_I + 4], GIB.unsqueeze(1).broadcast_to([PT, 4, 4]), ALU.add)
                step(dve.tensor_tensor(BC, PW[:, :, M_F:M_F + 4], GFB.unsqueeze(1).broadcast_to([PT, 4, 4]), ALU.add))
                dve.tensor_scalar(LF, BC, 0.0, None, ALU.min)
                dve.scalar_tensor_tensor(T16, BC, -1.0, BC, ALU.mult, ALU.max).then_inc(S["abs_f"], 1)
                for i in range(2):
                    ins = dve.memset(CP[i][:, 0:3], 0.0)
                step(ins)
                cw = VT[:, V_CWT:V_CWT + 32].rearrange("p (j f) -> p j f", j=4)
                for f in range(8):
                    B.empty(dve, "a", "d")
                    dve.wait_ge(S["emptied_act"], B.emptied_by("a"))
                    x = CP[f % 2]
                    step(dve.tensor_scalar(QK[:, f, :], x[:, 0:512], cw[:, 0, f:f + 1], VT[:, V_CB + f:V_CB + f + 1], ALU.mult, ALU.add))
                    for j in (1, 2):
                        step(dve.scalar_tensor_tensor(QK[:, f, :], x[:, j:j + 512], cw[:, j, f:f + 1], QK[:, f, :], ALU.mult, ALU.add))
                    dve.scalar_tensor_tensor(QK[:, f, :], x[:, 3:515], cw[:, 3, f:f + 1], QK[:, f, :], ALU.mult, ALU.add).then_inc(S["conv"], 1)
                dve.wait_ge(S["ln_f"], 1)
                dve.tensor_tensor(LF, LF, T16, ALU.subtract).then_inc(S["log_forget"], 1)
                bank = B.empty(dve, "d", "d")
                dve.tensor_copy(BC.rearrange("p t h -> p (t h)"), bank[:, 0:16]).then_inc(S["emptied_dve"], 1)
                dve.wait_ge(S["emptied_dve"], B.emptied_by("d"))
                dve.tensor_tensor(T16, IG, BC, ALU.subtract).then_inc(S["gate_cols"], 1)
                bank = B.empty(dve, "d", "d")
                copy_out(bank[0:4, :], CT)
                attention("ml", ml_units, None, mlstm=True)
                head_norm(PW[:, :, M_Q:M_Q + 512], LAT_T, ML_H, 128, P[:, ROWN + 512:ROWN + 1024], PW[:, :, M_O:M_O + 512])
                dve.sem_inc(S["mixed"], 1)

            n = 0
            for f in range(KD):
                for a, cnt, r in spans(OUT_T):
                    bank = B.empty(dve, turn[n % 2], "d")
                    n += 1
                    if bank is not None:
                        copy_out(bank[:, 0:cnt], HT[:, f, a:a + cnt])

            def add_gated(which, bank, t, half):
                r = 1 if t < CTX_T else 0
                a = 512 * half
                dve.tensor_tensor(SG[half][:, 0:512], bank[:, :], GBV[:, which, r, a:a + 512], ALU.mult).then_inc(S["emptied_dve"], 1)
                dve.wait_ge(S["emptied_dve"], B.emptied_by("d"))
                step(dve.tensor_tensor(XV[:, t, a:a + 512], XV[:, t, a:a + 512], SG[half][:, 0:512], ALU.add))

            def add_normed(which):
                B.all_emptied(dve)
                square_sums([YBV[:, t, :] for t in range(LAT_T)], [P[:, D * t:D * (t + 1)] for t in range(LAT_T)], None)
                inverse_root(LAT_T, D)
                for t in range(LAT_T):
                    ins = dve.scalar_tensor_tensor(YBV[:, t, :], YBV[:, t, :], rstd[:, t:t + 1], GBV[:, which, 0, :], ALU.mult, ALU.mult)
                step(ins)
                for t in range(LAT_T):
                    ins = dve.tensor_tensor(XV[:, CTX_T + t, :], XV[:, CTX_T + t, :], YBV[:, t, :], ALU.add)
                step(ins)

            n = 0
            for j in range(2):
                for t in OUT_T:
                    bank = B.empty(dve, turn[n % 2] if second else "d", "d")
                    n += 1
                    if bank is not None:
                        if second:
                            copy_out(bank[:, :], YBV[:, t - CTX_T, 512 * j:512 * (j + 1)])
                        else:
                            add_gated(0, bank, t, j)
            if second:
                add_normed(0)
            norm(1, OUT_T)
            dve.sem_inc(S["mod_room"], 1)
            modulate(1, OUT_T)

            q = 0
            for j in range(22):
                for a, cnt, r in spans(OUT_T):
                    B.empty(dve, "a", "d")
                    bank = B.empty(dve, "d", "d")
                    dve.wait_ge(S["emptied_act"], B.emptied_by("a"))
                    dve.tensor_tensor(GT[:, j, a - GOFF:a - GOFF + cnt], SG[q % 2][:, 0:cnt], bank[:, 0:cnt], ALU.mult).then_inc(S["emptied_dve"], 1)
                    q += 1
                if nxt and j % 2:
                    mod_chunk(j // 2)
            if nxt:
                mod_chunk(11)
            for half in range(2):
                for t in OUT_T:
                    bank = B.empty(dve, turn[t % 2] if second else "d", "d")
                    if bank is not None:
                        if second:
                            copy_out(bank[:, :], YBV[:, t - CTX_T, 512 * half:512 * (half + 1)])
                        else:
                            add_gated(1, bank, t, half)
            if second:
                add_normed(1)


def depth(us, mlstm):
    return 2 if mlstm or any(u["na"] for u in us) else 3


def n_act(us, i):
    return sum(len(u["v"]) > 4 for u in us[:i])


def nb_part(NB, g, half):
    return NB[64 * half:64 * half + 64, :, :, 4 * g:4 * g + 4].rearrange("p h j c -> p c h j")


def bank_part(bank, half):
    a = 1 - half
    return bank[64 * half:64 * half + 64, :].rearrange("p (c n) -> p c n", c=4)[:, :, 0:90].rearrange("p c (h r) -> p c h r", h=NA_H)[:, :, :, a:a + 14]


FIRST = ["x", "c", "ctx", "c_ctx", "w_mod", "b_mod", "norm_mix", "norm_ffn", "w_in", "gla_wa2_f", "gla_ba_f",
         "gla_wa2_b", "gla_ba_b", "gla_norm", "na_rpb", "swa_sink", "w_out", "w_gate", "w_up", "w_down", "final_norm"]
SECOND = ["c", "positions", "w_mod", "b_mod", "mix_norm_pre", "mix_norm_post", "w_in", "q_latent_norm", "w_q_up",
          "w_qidx_up", "conv_w", "conv_b", "b_igate", "b_fgate", "attn_out_norm", "mlstm_out_norm", "w_out",
          "ffn_norm_pre", "ffn_norm_post", "w_gate_up", "w_down"]


class Semaphores(dict):

    def __init__(self, nc, stack):
        super().__init__()
        self.nc, self.stack = nc, stack

    def __missing__(self, name):
        self[name] = self.stack.enter_context(self.nc.semaphore(name))
        return self[name]

    def all(self):
        nums = sorted(s.num for s in self.values())
        assert nums == list(range(nums[0], nums[-1] + 1))
        return range(nums[0], nums[-1] + 1)


def program(nc, a, out):
    with ExitStack() as stack:
        def sb(name, n, dt=F32):
            return stack.enter_context(nc.sbuf_tensor(name, [PT, n], dt))[:, :]

        T = dict(X=sb("x_res", NT * D), P=sb("projected", P_N), SC=sb("scratch", SC_N), W=sb("weights", 2 * SLOT),
                 C=sb("constants", C_N), G=sb("gates", 4 * D), SM=sb("small", 928), PI=sb("positions_sb", 4, I32))
        T["PS"] = [stack.enter_context(nc.psum_tensor("bank%d" % i, [PT, 512], F32))[:, :] for i in range(8)]
        S = Semaphores(nc, stack)
        X, P = T["X"], T["P"]
        XV = X.rearrange("p (t n) -> p t n", n=D)

        def end_of_layer():
            nc.all_engine_barrier(sems_to_clear=S.all())

        start = [(T["C"], a["constants"]),
                 (XV[:, 0:CTX_T], a["ctx"].rearrange("a (t p) n -> p (a t) n", p=PT)),
                 (XV[:, CTX_T:], a["x"].rearrange("a (t p) n -> p (a t) n", p=PT))]
        for l in range(2):
            def row(name):
                return a[name][l:l + 1]

            w = dict(w_mod=a["w_mod"][l], b_mod=row("b_mod"), c=a["c"], c_ctx=a["c_ctx"].rearrange("(a n) -> a n", a=1),
                     norm1=row("norm_mix"), norm2=row("norm_ffn"), w_in=a["w_in"][l], wa2_f=a["gla_wa2_f"][l],
                     wa2_b=a["gla_wa2_b"][l], ba_f=row("gla_ba_f"), ba_b=row("gla_ba_b"), gla_norm=row("gla_norm"),
                     rpb=a["na_rpb"][l], sink=row("swa_sink"), w_out=a["w_out"][l], w_down=a["w_down"][l],
                     gate=a["w_gate"][l], up=a["w_up"][l], gate_up=(("gate", 0), ("up", 0)), onehot=a["onehot"])
            if l == 0:
                nxt = dict(w_mod=a["w_mod"][1], c=[a["c"], w["c_ctx"]])
            else:
                nxt = dict(w_mod=a["w_mod_2"][0], c=[a["c_2"]])
            layer(nc, T, w, S, False, l == 0, nxt, start if l == 0 else ())
            end_of_layer()

        ssq, rstd = T["SM"][:, 368:372], T["SM"][:, 416:420]
        gain = P[:, 0:D]
        with nc.Block() as block:
            @block.sync
            def _(sp):
                sp.dma_start(gain, a["final_norm"].rearrange("(a n) -> a n", a=1).broadcast_to([PT, D])).then_inc(S["small"], 16)

            @block.vector
            def _(dve):
                for t in range(LAT_T):
                    x = XV[:, CTX_T + t, :]
                    ins = dve.tensor_tensor_reduce(P[:, D * (t + 1):D * (t + 2)], x, x, 1.0, 0.0, ALU.mult, ALU.add, ssq[:, t:t + 1])
                ins.then_inc(S["dve_step"], 1)
                dve.wait_ge(S["dve_step"], 1)
                dve.tensor_scalar(ssq, ssq, 1.0 / D, EPS, ALU.mult, ALU.add).then_inc(S["mean_sq"], 1)
                dve.wait_ge(S["root"], 1)
                dve.reciprocal(rstd, ssq).then_inc(S["dve_step"], 1)
                dve.wait_ge(S["dve_step"], 2)
                dve.wait_ge(S["small"], 16)
                for t in range(LAT_T):
                    x = XV[:, CTX_T + t, :]
                    dve.scalar_tensor_tensor(x, x, rstd[:, t:t + 1], gain, ALU.mult, ALU.mult)

            @block.scalar
            def _(act):
                act.wait_ge(S["mean_sq"], 1)
                act.activation(ssq, ssq, ACT.Sqrt).then_inc(S["root"], 1)
        end_of_layer()

        b = {n: a[n + "_2"] for n in SECOND}
        for l in range(2):
            def row(name):
                return b[name][l:l + 1]

            def mat(name):
                return b[name][l]

            w = dict(w_mod=mat("w_mod"), b_mod=row("b_mod"), c=b["c"], norm1=row("mix_norm_pre"), norm2=row("ffn_norm_pre"),
                     w_in=mat("w_in"), w_q_up=mat("w_q_up"), w_qidx_up=mat("w_qidx_up"), w_out=mat("w_out"),
                     w_down=mat("w_down"), gate=mat("w_gate_up"), gate_up=(("gate", 0), ("gate", FF)),
                     q_latent_norm=row("q_latent_norm"), conv_b=row("conv_b"), conv_w=mat("conv_w"),
                     post1=row("mix_norm_post"), post2=row("ffn_norm_post"), attn_out_norm=row("attn_out_norm"),
                     mlstm_out_norm=row("mlstm_out_norm"), b_igate=row("b_igate"), b_fgate=row("b_fgate"),
                     positions=b["positions"])
            layer(nc, T, w, S, True, False, dict(w_mod=b["w_mod"][1], c=[b["c"]]) if l == 0 else None)
            end_of_layer()

        with nc.Block() as block:
            @block.sync
            def _(sp):
                sp.dma_start(out.rearrange("a (t p) n -> p (a t) n", p=PT), XV[:, CTX_T:]).then_inc(S["stored"], 16)
                sp.wait_ge(S["stored"], 16)


def kernel(**inputs):
    import concourse.bacc as bacc
    from concourse.bass_utils import run_bass_kernel_spmd

    nc = bacc.Bacc("TRN2", target_bir_lowering=False, num_devices=1)
    constants, onehot = shape_constants()
    inputs = {**inputs, "positions_2": np.asarray(inputs["positions_2"]).reshape(LAT_T, PT).T}
    arrays, args = {}, {}
    given = {n: inputs[n] for n in FIRST} | {n + "_2": inputs[n + "_2"] for n in SECOND}
    for name, v in {**given, "constants": constants, "onehot": onehot}.items():
        v = np.ascontiguousarray(v)
        arrays["in_" + name] = v
        args[name] = nc.dram_tensor("in_" + name, v.shape, mybir.dt.from_np(v.dtype), kind="ExternalInput").ap()
    out = nc.dram_tensor("out", (1, LAT_T * PT, D), F32, kind="ExternalOutput").ap()
    program(nc, args, out)
    r = run_bass_kernel_spmd(nc, [arrays], core_ids=[0])
    return r.results[0]["out"]
```

```python
from contextlib import ExitStack

import numpy as np

import concourse.bass as bass
from concourse import mybir

F32 = mybir.dt.float32
F32R = mybir.dt.float32r
I32 = mybir.dt.int32
ALU = mybir.AluOpType
ACT = mybir.ActivationFunctionType
AX = mybir.AxisListType.X

PT = 128
D = 1024
KD = D // PT
CTX_T, LAT_T = 2, 4
NT = CTX_T + LAT_T
TOK = NT * PT
FF = 2816
KF = FF // PT
NEG = -1.0e30
TAKEN = -3.0e38
EPS = 1e-6
HD = 64

W1 = 2848
G_Q, G_K, G_V, G_G, G_Z = 0, 256, 512, 768, 1024
N_Q, N_K, N_V = 1056, 1440, 1824
S_Q, S_K, S_V = 2208, 2592, 2720
GLA_H, NA_H, SWA_H = 4, 6, 6
CH = 64
NCH = TOK // CH

W2 = 3408
A_C, A_K, A_V, A_KI, A_WI = 0, 256, 768, 1280, 1344
M_Q, M_K, M_V, M_O, M_I, M_F = 1352, 1864, 2376, 2888, 3400, 3404
ATT_H, ML_H = 8, 4
TOPK = 128

C_ID, C_TRI, C_TRIF, C_ONE, C_SW, C_CAU, C_ROPE, C_FREQ, C_SEL = 0, 128, 640, 768, 896, 1280, 1792, 2048, 2080
C_N = 2080 + 512

SC_N = 14080
H_N = NT * D
P_N = NT * W1
UNIT = 1024
LAND = 4
PARTS = [(0, 8), (8, 15), (15, 22)]
XN = 6144
YB = 8192
ROWN = 15000

TWO_PI_1 = 6.28125
TWO_PI_2 = float(np.float32(2 * np.pi - TWO_PI_1))
TWO_PI_3 = float(2 * np.pi - TWO_PI_1 - TWO_PI_2)
ROUND = 12582912.0


def shape_constants():
    c = np.zeros((PT, C_N), np.float32)
    i = np.arange(PT)
    s, t = i[:, None], i[None, :]
    same = (s // CH) == (t // CH)
    c[:, C_ID:C_ID + 128] = np.eye(PT)
    for n, m in enumerate([s <= t, s >= t, s > t, s < t]):
        c[:, C_TRI + 128 * n:C_TRI + 128 * (n + 1)] = (m & same) / 16.0
    c[:, C_TRIF:C_TRIF + 128] = s <= t
    c[:, C_ONE:C_ONE + 128] = 1.0
    c[:, C_SW:C_SW + 128] = np.where(t >= s, 0.0, NEG)
    c[:, C_SW + 256:C_SW + 384] = np.where(t <= s, 0.0, NEG)
    c[:, C_CAU + 384:C_CAU + 512] = np.where(t <= s, 0.0, NEG)
    tok = np.arange(LAT_T * PT)
    inv = (np.float32(10000.0) ** (-np.arange(16, dtype=np.float32) / 16)).astype(np.float32)
    row, col = (tok // 64).astype(np.float32), (tok % 64).astype(np.float32)
    ang = np.concatenate([row[:, None] * inv, col[:, None] * inv], -1)
    cs = np.stack([np.cos(ang), np.sin(ang)], 1).reshape(LAT_T, PT, 64)
    c[:, C_ROPE:C_ROPE + 256] = cs.transpose(1, 0, 2).reshape(PT, 256)
    c[:, C_FREQ:C_FREQ + 32] = np.float32(10000.0) ** (-np.arange(0, 64, 2, dtype=np.float32) / 64)
    for h in range(4):
        c[h, C_SEL + 128 * h:C_SEL + 128 * (h + 1)] = 1.0
    oh = np.zeros((32, 64, 2, 64), np.float32)
    for qc in range(64):
        start = min(max(qc - 8, 0), 48)
        for kc in range(64):
            if start <= kc < start + 16:
                oh[kc - qc + 15, kc, :, qc] = 1.0
            else:
                oh[31, kc, :, qc] = NEG
    return c, oh.reshape(32, 64 * 128)


class Banks:

    def __init__(self, ps, filled, emptied):
        self.ps, self.filled, self.emptied = ps, filled, emptied
        self.past, self.count = [], {"a": 0, "d": 0}

    def _next(self, by):
        g = len(self.past)
        self.count[by] += 1
        self.past.append((by, self.count[by]))
        return g

    def fill(self, pe, by):
        g = self._next(by)
        if g >= 8:
            who, n = self.past[g - 8]
            pe.wait_ge(self.emptied[who], n)
        return self.ps[g % 8]

    def empty(self, eng, by, mine):
        g = self._next(by)
        if by != mine:
            return None
        eng.wait_ge(self.filled, g + 1)
        return self.ps[g % 8]

    def filled_so_far(self):
        return len(self.past)

    def emptied_by(self, who):
        return self.count[who]

    def share(self, eng):
        g = self._next("d")
        eng.wait_ge(self.filled, g + 1)
        return self.ps[g % 8]

    def all_emptied(self, eng):
        for who in "ad":
            if self.count[who]:
                eng.wait_ge(self.emptied[who], self.count[who])


def layer(nc, T, w, sems, second, with_ctx, nxt, start_loads=()):
    X, P, SC, WR, CN, GB, SM = T["X"], T["P"], T["SC"], T["W"], T["C"], T["G"], T["SM"]
    PS = T["PS"]
    S = sems
    R = 1 if second else 2
    W = W2 if second else W1
    CW = W // 8
    T0 = CTX_T if second else 0
    O0 = 0 if with_ctx else CTX_T
    IN_T, OUT_T = range(T0, NT), range(O0, NT)
    PW = P[:, 0:(NT - T0) * W].rearrange("p (t n) -> p t n", n=W)

    def pr(t, a, n):
        return PW[:, t - T0, a:a + n]

    XV = X.rearrange("p (t n) -> p t n", n=D)
    HH, HL = (T[n].rearrange("p (k n) -> p k n", k=KD) for n in ("h_high", "h_low"))
    GH, GL = (T[n + ("_2" if second else "_1")].rearrange("p (k n) -> p k n", k=8) for n in ("hidden_high", "hidden_low"))
    ROWS = SC[:, 2 * H_N:2 * H_N + 1536]
    TMP = [SC[:, 2 * H_N + 512 * i:2 * H_N + 512 * (i + 1)] for i in range(2)]
    SLM = [P[:, 12288 + 2048 * i:12288 + 2048 * (i + 1)].rearrange("p (k n) -> p k n", k=4) for i in range(2)]
    SC32 = SC[:, 13824:14080].rearrange("p (k m) -> p k m", k=KD)
    BR = P[:, 0:1536]
    PO = P[:, 1536:2048]
    XNV = P[:, XN:XN + NT * D].rearrange("p (t n) -> p t n", n=D)
    GOFF = CTX_T * PT if second else 0
    YBV = P[:, YB:YB + LAT_T * D].rearrange("p (t n) -> p t n", n=D)
    GBV = GB.rearrange("p (s r n) -> p s r n", s=2, r=2)
    ident = CN[:, C_ID:C_ID + 128]
    slots = [WR[:, UNIT * i:UNIT * (i + 1)] for i in range(LAND)]
    WH, WL = ([T[n][:, UNIT * i:UNIT * (i + 1)] for i in range(2)] for n in ("weights_high", "weights_low"))

    SG = [P[:, 14336 + 512 * i:14336 + 512 * (i + 1)] for i in range(2)]
    FT = P[:, 15872:16384]

    VR, VT = SM[:, 0:128], SM[:, 128:256]
    MT = SM[:, 272:272 + 32 * R].rearrange("p (s k r) -> p s k r", s=4, r=R)
    AT = SM[:, 336:336 + 16 * R].rearrange("p (s k r) -> p s k r", s=2, r=R)
    ssq, rstd = SM[:, 368:416], SM[:, 416:464]
    nm, rs, rr, fl = SM[:, 464:468], SM[:, 468:472], SM[:, 472:476], SM[:, 476:480]
    DEC = SM[:, 480:528].rearrange("p (d f c) -> p d f c", d=2, f=2)
    SINK = SM[:, 528:534]
    RPR = SM[0:90, 540:571]
    RPT = SM[0:32, 0:128]
    m8 = SM[:, 666:674]
    GIB, GFB = SM[:, 674:678], SM[:, 678:682]
    IG, LF, BC, T16 = (SM[:, 684 + 16 * i:700 + 16 * i].rearrange("p (t h) -> p t h", h=4) for i in range(4))
    WI = SM[:, 748:780].rearrange("p (t h) -> p t h", h=8)
    PF = SM[:, 780:784]
    ROPE = CN[:, C_ROPE:C_ROPE + 256].rearrange("p (t c f) -> p t c f", t=4, c=2)
    ones_col = CN[:, C_ONE:C_ONE + 1]
    small = SM[:, 784:912]
    PI32 = T["PI"]

    V_NEXT = 66 if second else 32
    n_next = len(nxt["c"]) if nxt else 0
    nvec = V_NEXT + 8 * n_next
    V_C, V_CC, V_N1, V_N2, V_QL, V_CB, V_CWT = (0, None, 8, 16, 24, 26, 34) if second else (0, 8, 16, 24, None, None, None)

    weight_units = []
    split_of = []
    beside = {}

    def unit(src, k, n, split=True):
        if split:
            split_of.append(len(weight_units))
        slot = slots[len(weight_units) % LAND]
        dst = slot[0:src.shape[0], 0:n] if k == 1 else slot[:, 0:k * n].rearrange("p (k n) -> p k n", n=n)
        weight_units.append((dst, src, (k, n), split))

    def cols(wt, a, n, k0, k1, split=True):
        unit(wt[:, a:a + n].rearrange("(k p) n -> p k n", p=PT)[:, k0:k1], k1 - k0, n, split)

    for j in range(8):
        for k in range(0, KD, 2):
            cols(w["w_in"], CW * j, CW, k, k + 2)
    if second:
        for n in ("w_q_up", "w_qidx_up"):
            cols(w[n], 0, 512, 0, 2, split=False)
    else:
        for j in range(8):
            unit(w["onehot"][:, UNIT * j:UNIT * (j + 1)], 1, UNIT, split=False)
    for j in range(2):
        for k in range(0, KD, 2):
            cols(w["w_out"], 512 * j, 512, k, k + 2)
    for m0, m1 in PARTS:
        for m in range(m0, m1):
            for n, a in w["gate_up"]:
                cols(w[n], a + PT * m, PT, 0, KD)
            beside[len(weight_units) - 1] = m
        for half in range(2):
            for k in range(m0, m1, 2):
                cols(w["w_down"], 512 * half, 512, k, min(k + 2, m1))
            if m1 == KF:
                beside[len(weight_units) - 1] = KF + half
    n_of = {j: s_ for s_, j in enumerate(split_of)}

    def mod_source(w_mod, i):
        return w_mod[512 * (i % 2):512 * (i % 2 + 1), 512 * (i // 2):512 * (i // 2 + 1)].rearrange("(k p) n -> p k n", p=PT)

    def banks():
        return Banks(PS, S["filled"], {"a": S["emptied_act"], "d": S["emptied_dve"]})

    units = []
    if not second:
        QN = SC[:, 0:2304].rearrange("p (f n) -> p f n", n=TOK)
        KN = SC[:, 2304:4608].rearrange("p (f n) -> p f n", n=TOK)
        NB = SC[:, 4608:9984].rearrange("p (h j c) -> p h j c", h=NA_H, j=14)
        SB = [SC[:, 9984 + 776 * i:9984 + 776 * (i + 1)] for i in range(2)]
        PB = [SC[:, 11536 + 768 * i:11536 + 768 * (i + 1)] for i in range(2)]
        RK = SC[:, 6144:6144 + 1536].rearrange("p (t n) -> p t n", n=256)
        RT = [SC[:, 12288 + 768 * i:12288 + 768 * (i + 1)] for i in range(2)]
        KS = KN[:, 0:2]
        QS = QN
        na_units, sw_units = [], []
        for h in range(NA_H):
            b, f = 64 * (h % 2), h // 2
            for t in OUT_T:
                u = dict(off=b, q=QN[b:b + 64, f, t * 128:(t + 1) * 128], ka=KN[b:b + 64, f, 0:256], kb=None, bias=None,
                         sink=None, v=[(s, N_V + 64 * h) for s in range(CTX_T)], y=pr(t, N_Q + 64 * h, 64))
                if t >= CTX_T:
                    j0 = 7 - 2 * (t - CTX_T) - 1
                    u["kb"] = KN[b:b + 64, f, 256:768]
                    u["bias"] = NB[:, h, j0:j0 + 8, :].rearrange("p j c -> p (j c)")
                    u["v"] += [(s, N_V + 64 * h) for s in range(CTX_T, NT)]
                na_units.append(u)
        for h in range(SWA_H):
            b, f, kv = 64 * (h % 2), h // 2, h // 3
            for t in OUT_T:
                u = dict(off=64 * kv, q=QS[b:b + 64, f, t * 128:(t + 1) * 128], ka=KS[b:b + 64, kv, 0:256], kb=None, bias=None,
                         sink=SINK[:, h:h + 1], v=[(s, S_V + 64 * kv) for s in range(CTX_T)], y=pr(t, S_Q + 64 * h, 64))
                if t >= CTX_T:
                    lo, hi = max(t - 1, CTX_T), min(t + 2, NT)
                    u["kb"] = KS[b:b + 64, kv, lo * 128:hi * 128]
                    u["bias"] = CN[:, C_SW + (lo - t + 1) * 128:C_SW + (hi - t + 1) * 128]
                    u["v"] += [(s, S_V + 64 * kv) for s in range(lo, hi)]
                sw_units.append(u)
        phases = [na_units, sw_units]
    else:
        QQ = SC[:, 0:4096].rearrange("p (t n) -> p t n", n=1024)
        RT = [X[:, 1024 * i:1024 * (i + 1)] for i in range(2)]
        CQ = SC[:, 4096:5120].rearrange("p (k n) -> p k n", k=2)
        KID = P[:, 13696:14208].rearrange("p (t n) -> p t n", n=128)
        QTT = SC[:, 6656:8704].rearrange("p (f n) -> p f n", n=512)
        QIT = SC[:, 8704:10752].rearrange("p (f n) -> p f n", n=512)
        KTT = SC[:, 10752:12800].rearrange("p (f n) -> p f n", n=512)
        KIT = SC[:, 12800:13312]
        SCO, WK = SC[:, 0:512], SC[:, 512:1024]
        RL = [SC[:, 1024 + 512 * i:1536 + 512 * i] for i in range(2)]
        MK = SC[:, 2048:3328]
        MKO = [0, 128, 384, 768]
        SB = [SC[:, 3328 + 520 * i:3328 + 520 * (i + 1)] for i in range(3)]
        PB = [SC[:, 4888 + 512 * i:4888 + 512 * (i + 1)] for i in range(2)]
        CSN = SC[:, 13312:13568].rearrange("p (t c f) -> p t c f", t=4, c=2)
        ANG = [SC[:, 13568 + 128 * i:13696 + 128 * i] for i in range(3)]
        at_units, ml_units = [], []
        for h in range(ATT_H):
            b, f = 64 * (h % 2), h // 2
            for n in range(LAT_T):
                nk = 128 * (n + 1)
                at_units.append(dict(off=b, q=QTT[b:b + 64, f, n * 128:(n + 1) * 128], ka=None, kb=KTT[b:b + 64, f, 0:nk],
                                     bias=MK[:, MKO[n]:MKO[n] + nk], sink=None,
                                     v=[(CTX_T + s, A_V + 64 * h) for s in range(n + 1)],
                                     y=pr(CTX_T + n, A_K + 64 * h, 64)))
        phases = [at_units]
        QK = SC[:, 0:4096].rearrange("p (f n) -> p f n", n=512)
        CP = [SC[:, 4096 + 516 * i:4096 + 516 * (i + 1)] for i in range(2)]
        CT = SC[0:4, 5200:5712]
        SM2 = [SC[:, 5712 + 512 * i:6224 + 512 * i] for i in range(2)]
        SB2 = [SC[:, 7760 + 512 * i:8272 + 512 * i] for i in range(2)]
        PB2 = [SC[:, 6736 + 512 * i:7248 + 512 * i] for i in range(2)]
        for h in range(ML_H):
            for n in range(LAT_T):
                nk = 128 * (n + 1)
                ml_units.append(dict(h=h, n=n, q=QK[:, h, n * 128:(n + 1) * 128], k=QK[:, 4 + h, 0:nk], nk=nk,
                                     v=[(CTX_T + s, M_V + 128 * h) for s in range(n + 1)],
                                     y=pr(CTX_T + n, M_Q + 128 * h, 128)))
    for ph in phases:
        for u in ph:
            u["na"] = 0 if u["ka"] is None else 256
            u["nb"] = 0 if u["kb"] is None else u["kb"].shape[-1]
            u["n"] = u["na"] + u["nb"]
            u["blocks"] = u["n"] // 128

    if not second:
        QI = SC[:, 0:3072].rearrange("p (d f n) -> p d f n", d=2, f=2)
        KI = SC[:, 3072:6144].rearrange("p (d f n) -> p d f n", d=2, f=2)
        LA = SC[:, 6144:9216].rearrange("p (t n) -> p t n", n=512)
        KE = SC[:, 9216:12288].rearrange("p (t d n) -> p t d n", d=2, n=256)
        SE = SC[:, 9216:12288].rearrange("p (d c f e) -> p d c f e", d=2, c=NCH, f=2)
        EB = [SC[:, 12288 + 768 * i:13056 + 768 * i] for i in range(2)]
        ZT = SC[0:33, 12288:13056]
        WZ = SC[0:33, 13056:13568]
        GN = SC[:, 13824:14080]
        AM = [SC[:, 6144 + 1024 * i:7168 + 1024 * i].rearrange("p (d h n) -> p d h n", d=2, h=4) for i in range(2)]
        MN = SC[:, 9216:12288]
        order = [list(range(NCH)), [3, 2, 1, 0] + list(range(NCH - 1, 3, -1))]
        first = [order[0][0], order[1][0]]

    YF = [A_K, A_K + 128, A_K + 256, A_K + 384, M_Q, M_Q + 128, M_Q + 256, M_Q + 384] if second else \
         [G_Q, G_Q + 128, N_Q, N_Q + 128, N_Q + 256, S_Q, S_Q + 128, S_Q + 256]

    def spans(tt):
        out = []
        if tt[0] < CTX_T:
            out.append((0, CTX_T * PT, R - 1))
        return out + [(CTX_T * PT, LAT_T * PT, 0)]

    small_loads = [(VR[a:a + v.shape[-1] // PT, :], v.rearrange("a (f p) -> (a f) p", p=PT)) for a, v in
                   [(V_C, w["c"]), (V_N1, w["norm1"]), (V_N2, w["norm2"])]
                   + ([(V_QL, w["q_latent_norm"]), (V_CB, w["conv_b"])] if second else [(V_CC, w["c_ctx"])])]
    small_loads += [(VR[V_NEXT + 8 * i:V_NEXT + 8 * i + 8, :], c.rearrange("a (f p) -> (a f) p", p=PT))
                    for i, c in enumerate(nxt["c"] if nxt else ())]
    for q in range(4):
        def quarter(v):
            n = v.shape[-1] // 512
            return v.rearrange("a (c q n) -> a q c n", q=4, n=PT)[:, q].broadcast_to([32, n, PT])

        lane = slice(32 * q, 32 * q + 32)
        small_loads.append((BR[lane, :].rearrange("p (c n) -> p c n", n=PT), quarter(w["b_mod"])))
        if second:
            small_loads += [(PO[lane, 256 * i:256 * (i + 1)].rearrange("p (c n) -> p c n", n=PT), quarter(w[n]))
                            for i, n in enumerate(("post1", "post2"))]
    if second:
        small_loads += [(VR[V_CWT:V_CWT + 32, :], w["conv_w"].rearrange("w (f p) -> (w f) p", p=PT))]
        late_loads = [(P[:, ROWN:ROWN + 512], w["attn_out_norm"].broadcast_to([PT, 512])),
                        (P[:, ROWN + 512:ROWN + 1024], w["mlstm_out_norm"].broadcast_to([PT, 512])),
                        (GIB, w["b_igate"].broadcast_to([PT, 4])), (GFB, w["b_fgate"].broadcast_to([PT, 4])),
                        (PI32[:, :], w["positions"])]
    else:
        late_loads = [(SINK, w["sink"].broadcast_to([PT, SWA_H])),
                        (RPR, w["rpb"].rearrange("h r c -> (h r) c"))]
    z_loads = [] if second else [(WZ[0:16, 0:256], w["wa2_f"]), (WZ[16:32, 256:512], w["wa2_b"]),
                        (WZ[32:33, 0:256], w["ba_f"]), (WZ[32:33, 256:512], w["ba_b"]),
                        (GN, w["gla_norm"].broadcast_to([PT, 256]))]
    n_small, n_late = 16 * len(small_loads), 16 * len(late_loads)
    release = []
    first_mod_release = []
    mod_release = []
    turn = "ad"

    with nc.Block() as block:

        @block.tensor
        def _(pe):
            B = banks()
            mine = dict(part=0)

            def next_unit():
                j = len(release)
                _, _, (k, n), split = weight_units[j]
                if not split:
                    pe.wait_ge(S["landed%d" % (j % LAND)], 16 * (j // LAND + 1))
                    return slots[j % LAND][:, 0:k * n].rearrange("p (k n) -> p k n", n=n)
                s_ = n_of[j]
                pe.wait_ge(S["w_low"], s_ + 1)
                return [v[s_ % 2][:, 0:k * n].rearrange("p (k n) -> p k n", n=n) for v in (WH, WL)]

            def used():
                release.append(("filled", B.filled_so_far()))

            def part_used(mm):
                mm.then_inc(S["unit_part"], 1)
                mine["part"] += 1
                release.append(("unit_part", mine["part"]))

            def product(ah, al, tt, off, n, k0, k1, by, ready=None):
                out_banks = {}
                for k in range(k0, k1, 2):
                    kn = min(k + 2, k1)
                    wh, wl = next_unit()
                    if ready:
                        pe.wait_ge(S["emptied_dve"], ready[kn - 1])
                    for i, t in enumerate(tt):
                        if k == k0:
                            out_banks[t] = B.fill(pe, by(i))
                        at = slice(t * PT - off[1], (t + 1) * PT - off[1])
                        for kk in range(k, kn):
                            for q, (x, wt) in enumerate(((ah, wh), (ah, wl), (al, wh))):
                                mm = pe.matmul(out_banks[t][:, 0:n], x[:, kk - off[0], at], wt[:, kk - k, :],
                                               start=(kk == k0 and q == 0), stop=(kk == k1 - 1 and q == 2))
                        if kn == k1:
                            mm.then_inc(S["filled"], 1)
                    if kn == k1:
                        used()
                    else:
                        part_used(mm)

            def turn_norm(which):
                there = {}
                tt = OUT_T if which else IN_T
                pe.wait_ge(S["normed%d" % which], (len(tt) + 1) // 2)
                pe.wait_ge(S["normed_act%d" % which], len(tt) // 2)
                for f in range(KD):
                    for a, cnt, r in spans(tt):
                        bank = B.fill(pe, "d")
                        for i in range(cnt // PT):
                            mm = pe.transpose(bank[:, i * PT:(i + 1) * PT], XNV[:, a // PT + i, f * PT:(f + 1) * PT], ident)
                        mm.then_inc(S["filled"], 1)
                    there[f] = B.emptied_by("d")
                return there

            def turn_columns(src, by, tt=None):
                for a, cnt, r in spans(tt or IN_T):
                    bank = B.fill(pe, by[0])
                    by.append(by.pop(0))
                    for i in range(cnt // PT):
                        mm = pe.transpose(bank[:, i * PT:(i + 1) * PT], src(a // PT + i), ident)
                    mm.then_inc(S["filled"], 1)

            pe.wait_ge(S["small"], n_small)
            if start_loads:
                pe.wait_ge(S["start"], 16 * len(start_loads))
            bank = B.fill(pe, "d")
            pe.transpose(bank[:, 0:nvec], VR[0:nvec, :], ident[0:nvec, 0:nvec]).then_inc(S["filled"], 1)

            def mod_tile(i, wt):
                bank = B.fill(pe, "d")
                for k in range(4):
                    for q in range(4):
                        mm = pe.matmul(bank[32 * q:32 * q + 32, 0:PT], SC32[:, 4 * (i % 2) + k, :], wt[:, k, q * PT:(q + 1) * PT],
                                       start=(k == 0), stop=(k == 3))
                mm.then_inc(S["filled"], 1)

            if start_loads:
                pe.wait_ge(S["silu_c"], 1)
                for i in range(24):
                    pe.wait_ge(S["mod_first%d" % (i % 2)], 16 * (i // 2 + 1))
                    mod_tile(i, SLM[i % 2])
                    first_mod_release.append(B.filled_so_far())
            pe.wait_ge(S["mod_rows"], 1)
            for chunks in ((0, 1, 2, 3), (6, 7, 8, 9)):
                bank = B.fill(pe, "d")
                for i, c in enumerate(chunks):
                    mm = pe.transpose(bank[:, i * PT:(i + 1) * PT], ROWS[:, c * PT:(c + 1) * PT], ident)
                mm.then_inc(S["filled"], 1)
            for c in (4, 5, 10, 11):
                for r in range(R):
                    bank = B.fill(pe, "a")
                    for q in range(4):
                        pick = ident[:, 32 * q + r:32 * q + r + 1].broadcast_to([PT, PT])
                        mm = pe.matmul(bank[:, q * PT:(q + 1) * PT], pick, ROWS[:, c * PT:(c + 1) * PT], start=True, stop=True)
                    mm.then_inc(S["filled"], 1)

            there = turn_norm(0)

            for j in range(8):
                product(HH, HL, IN_T, (0, 0), CW, 0, KD, lambda i: turn[i % 2], None if j else there)
            B.all_emptied(pe)

            def attention(name, us, prob, mlstm=False):
                ns = depth(us, mlstm)

                def scores(i):
                    u = us[i]
                    a, b = (PS[2 * (i % 2)], PS[2 * (i % 2) + 1]) if ns == 2 else (None, PS[i % ns])
                    if i >= ns:
                        pe.wait_ge(S[name + ("_prob" if mlstm else "_max")], i - ns + 1)
                    if mlstm:
                        pe.matmul(a[:, 0:u["nk"]], CN[0:4, C_SEL + 128 * u["h"]:C_SEL + 128 * (u["h"] + 1)],
                                  CT[:, 0:u["nk"]], start=True, stop=True)
                        mm = pe.matmul(b[:, 0:u["nk"]], u["q"], u["k"], start=True, stop=True)
                    else:
                        if u["na"]:
                            mm = pe.matmul(a[:, 0:u["na"]], u["q"], u["ka"], start=True, stop=True)
                        if u["nb"]:
                            mm = pe.matmul(b[:, 0:u["nb"]], u["q"], u["kb"], start=True, stop=True)
                    mm.then_inc(S[name + "_scores"], 1)

                def turned(i):
                    u = us[i]
                    nb = len(u["v"])
                    pe.wait_ge(S[name + prob], i + 1)
                    if i >= 1:
                        pe.wait_ge(S[name + "_turned_dve"], i)
                        if n_act(us, i):
                            pe.wait_ge(S[name + "_turned_act"], n_act(us, i))
                    src = (SM2 if mlstm else SB)[i % ns]
                    for j in range(nb):
                        mm = pe.transpose(PS[4 + j // 4][:, (j % 4) * PT:(j % 4 + 1) * PT], src[:, j * PT:(j + 1) * PT], ident)
                    mm.then_inc(S[name + "_turn"], 1)

                def values(i):
                    u = us[i]
                    pe.wait_ge(S[name + "_turned_dve"], i + 1)
                    if n_act(us, i + 1):
                        pe.wait_ge(S[name + "_turned_act"], n_act(us, i + 1))
                    if i >= 2:
                        pe.wait_ge(S[name + "_out"], i - 1)
                    pb = (PB2 if mlstm else PB)[i % 2]
                    for j, (t, c) in enumerate(u["v"]):
                        mm = pe.matmul(PS[6 + i % 2][:, 0:128], pb[:, j * PT:(j + 1) * PT], pr(t, c - u.get("off", 0), 128),
                                       start=(j == 0), stop=(j == len(u["v"]) - 1))
                    mm.then_inc(S[name + "_values"], 1)

                B.all_emptied(pe)
                for i in range(len(us) + ns):
                    if i < len(us):
                        scores(i)
                    if 0 <= i - ns + 1 < len(us):
                        turned(i - ns + 1)
                    if 0 <= i - ns < len(us):
                        values(i - ns)
                pe.wait_ge(S[name + "_out"], len(us))

            if not second:
                for a, cnt, r in spans(IN_T):
                    bank = B.fill(pe, "d")
                    for i in range(cnt // PT):
                        mm = pe.transpose(bank[0:32, i * PT:(i + 1) * PT], pr(a // PT + i, G_Z, 32), ident)
                    mm.then_inc(S["filled"], 1)
                B.all_emptied(pe)
                pe.wait_ge(S["z_ones"], 1)
                pe.wait_ge(S["z_loaded"], 16 * len(z_loads))
                for t in IN_T:
                    bank = B.fill(pe, turn[t % 2])
                    pe.matmul(bank[:, :], ZT[:, t * PT:(t + 1) * PT], WZ, start=True, stop=True).then_inc(S["filled"], 1)
                for f in range(2):
                    turn_columns(lambda t: pr(t, G_Q + 128 * f, 128), ["d"])
                    turn_columns(lambda t: pr(t, G_K + 128 * f, 128), ["d"])
                pe.wait_ge(S["log_decay"], 1)
                for d in (1, 0):
                    for f in range(2):
                        for a, cnt, r in spans(IN_T):
                            bank = B.fill(pe, "a")
                            for i in range(cnt // PT):
                                mm = pe.matmul(bank[:, i * PT:(i + 1) * PT], LA[:, a // PT + i, d * 256 + f * 128:d * 256 + f * 128 + 128],
                                               CN[:, C_TRI + 128 * d:C_TRI + 128 * (d + 1)], start=True, stop=True)
                            mm.then_inc(S["filled"], 1)
                for t in IN_T:
                    bank = B.fill(pe, "a")
                    for d in range(2):
                        mm = pe.matmul(bank[:, 256 * d:256 * (d + 1)], CN[:, C_TRI + 128 * (2 + d):C_TRI + 128 * (3 + d)],
                                       LA[:, t, 256 * d:256 * (d + 1)], start=True, stop=True)
                    mm.then_inc(S["filled"], 1)
                B.all_emptied(pe)
                pe.wait_ge(S["k_end"], 1)
                for d in range(2):
                    for c in range(NCH):
                        par, t, i = c % 2, c // 2, c // 2
                        b = PS[4 * d + 2 * par + i // 4]
                        for h in range(GLA_H):
                            hp, f = h % 2, h // 2
                            at = (i % 4) * 128 + f * 64
                            mm = pe.matmul(b[64 * hp:64 * hp + 64, at:at + 64], KE[64 * par:64 * par + 64, t, d, 64 * h:64 * h + 64],
                                           pr(t, G_V + 64 * h, 64)[64 * par:64 * par + 64, :], start=True, stop=True)
                mm.then_inc(S["chunk_sums"], 1)
                pe.wait_ge(S["states"], 1)
                for n, t in enumerate(OUT_T):
                    if n >= 2:
                        pe.wait_ge(S["masked"], n - 1)
                    for hp in range(2):
                        for d in range(2):
                            for f in range(2):
                                mm = pe.matmul(PS[2 * (n % 2) + hp][:, (d * 2 + f) * 128:(d * 2 + f + 1) * 128],
                                               KI[64 * hp:64 * hp + 64, d, f, t * PT:(t + 1) * PT],
                                               QI[64 * hp:64 * hp + 64, d, f, t * PT:(t + 1) * PT], start=True, stop=True)
                    mm.then_inc(S["products"], 1)
                    if n >= 1:
                        pe.wait_ge(S["gla_out"], n)
                    for hp in range(2):
                        for f in range(2):
                            for par in range(2):
                                c = 2 * t + par
                                dirs = [d for d in range(2) if c != first[d]]
                                for d in dirs:
                                    mm = pe.matmul(PS[6 + hp][64 * par:64 * par + 64, 64 * f:64 * f + 64],
                                                   QI[64 * hp:64 * hp + 64, d, f, c * CH:(c + 1) * CH],
                                                   SE[64 * hp:64 * hp + 64, d, c, f, :], start=(d == dirs[0]), stop=(d == dirs[-1]))
                    pe.wait_ge(S["masked"], n + 1)
                    for h in range(GLA_H):
                        for d in range(2):
                            mm = pe.matmul(PS[4][:, 64 * h:64 * h + 64], AM[n % 2][:, d, h, :], pr(t, G_V + 64 * h, 64),
                                           start=(d == 0), stop=(d == 1))
                    mm.then_inc(S["gla_sums"], 1)
                pe.wait_ge(S["gla_out"], len(OUT_T))

                pe.wait_ge(S["late"], n_late)
                bank = B.fill(pe, "d")
                pe.transpose(bank[0:31, 0:90], RPR, ident[0:90, 0:90]).then_inc(S["filled"], 1)
                B.all_emptied(pe)
                n = 0
                for j in range(8):
                    oh = next_unit()[0:32, 0, :].rearrange("p (c q) -> p c q", q=PT)
                    for g in range(2):
                        bank = B.fill(pe, turn[n % 2])
                        n += 1
                        for i in range(4):
                            mm = pe.matmul(bank[:, 128 * i:128 * i + 128], oh[:, 4 * g + i, :], RPT, start=True, stop=True)
                        mm.then_inc(S["filled"], 1)
                    used()
                for f in range(3):
                    turn_columns(lambda t: pr(t, N_Q + 128 * f, 128), ["a"], OUT_T)
                    turn_columns(lambda t: pr(t, N_K + 128 * f, 128), ["d"])
                attention("na", na_units, "_exp")

                pe.wait_ge(S["rope"], 1)
                for f in range(3):
                    turn_columns(lambda t: pr(t, S_Q + 128 * f, 128), ["a"], OUT_T)
                for kv in range(2):
                    turn_columns(lambda t: RK[:, t, 128 * kv:128 * kv + 128], ["d"])
                attention("sw", sw_units, "_exp")
                pe.wait_ge(S["mixed"], 1)
            else:
                pe.wait_ge(S["cq"], 1)
                for k in range(2):
                    turn_columns(lambda t: pr(t, A_C + 128 * k, 128), ["d"])
                B.all_emptied(pe)
                for m in range(2):
                    wt = next_unit()
                    for n in range(LAT_T):
                        bank = B.fill(pe, turn[n % 2])
                        for k in range(2):
                            mm = pe.matmul(bank[:, :], CQ[:, k, n * PT:(n + 1) * PT], wt[:, k, :], start=(k == 0), stop=(k == 1))
                        mm.then_inc(S["filled"], 1)
                    used()
                pe.wait_ge(S["key_rope"], 1)
                for f in range(4):
                    turn_columns(lambda t: pr(t, A_K + 128 * f, 128), ["a"])
                turn_columns(lambda t: KID[:, t - CTX_T, :], ["a"])
                for m in range(2):
                    pe.wait_ge(S["rope"], m + 1)
                    for f in range(4):
                        turn_columns(lambda t: QQ[:, t - CTX_T, 512 * m + 128 * f:512 * m + 128 * f + 128], ["a"])
                B.all_emptied(pe)
                for n in range(1, LAT_T):
                    for h in range(8):
                        b, f = 64 * (h % 2), h // 2
                        bank = B.fill(pe, "a")
                        pe.matmul(bank[:, 0:128 * (n + 1)], QIT[b:b + 64, f, n * PT:(n + 1) * PT], KIT[b:b + 64, 0:128 * (n + 1)],
                                  start=True, stop=True).then_inc(S["filled"], 1)
                attention("at", at_units, "_exp")

                for f in range(8):
                    turn_columns(lambda t: pr(t, M_Q + 128 * f, 128), ["a"])
                pe.wait_ge(S["log_forget"], 1)
                bank = B.fill(pe, "d")
                for n in range(LAT_T):
                    for m in range(n + 1):
                        mm = pe.matmul(bank[:, 4 * n:4 * n + 4], CN[:, C_TRIF:C_TRIF + 128] if m == n else CN[:, C_ONE:C_ONE + 128],
                                       LF[:, m, :], start=(m == 0), stop=(m == n))
                mm.then_inc(S["filled"], 1)
                pe.wait_ge(S["gate_cols"], 1)
                bank = B.fill(pe, "d")
                for n in range(LAT_T):
                    mm = pe.transpose(bank[0:4, n * PT:(n + 1) * PT], T16[:, n, :], ident)
                mm.then_inc(S["filled"], 1)
                pe.wait_ge(S["conv_silu"], 1)
                attention("ml", ml_units, "_prob", mlstm=True)
                pe.wait_ge(S["mixed"], 1)

            for f in range(KD):
                for a, cnt, r in spans(OUT_T):
                    bank = B.fill(pe, "d")
                    for i in range(cnt // PT):
                        mm = pe.transpose(bank[:, i * PT:(i + 1) * PT], pr(a // PT + i, YF[f], 128), ident)
                    mm.then_inc(S["filled"], 1)
                there[f] = B.emptied_by("d")
            for j in range(2):
                product(HH, HL, OUT_T, (0, 0), 512, 0, KD, lambda i: "d", None if j else there)

            there = turn_norm(1)


            def mod_beside(i):
                if i == 0:
                    pe.wait_ge(S["silu_next"], 1)
                pe.wait_ge(S["mod_landed"], 16 * (i + 1))
                mod_tile(i, SLM[0])
                mod_release.append(B.filled_so_far())

            for m0, m1 in PARTS:
                ready = {}
                for m in range(m0, m1):
                    for by in "ad":
                        wh, wl = next_unit()
                        for a, cnt, r in spans(OUT_T):
                            bank = B.fill(pe, by)
                            for k in range(KD):
                                if m == 0 and by == "a":
                                    pe.wait_ge(S["emptied_dve"], there[k])
                                for q, (wt, x) in enumerate(((wh, HH), (wh, HL), (wl, HH))):
                                    mm = pe.matmul(bank[:, 0:cnt], wt[:, k, :], x[:, k, a:a + cnt],
                                                   start=(k == 0 and q == 0), stop=(k == KD - 1 and q == 2))
                            mm.then_inc(S["filled"], 1)
                        used()
                    ready[m] = B.emptied_by("d")
                    if nxt:
                        mod_beside(m)
                for half in range(2):
                    product(GH, GL, OUT_T, (m0, GOFF), 512, m0, m1, lambda i: "d", ready)
                    if nxt and m1 == KF:
                        mod_beside(KF + half)
            assert len(release) == len(weight_units)

        @block.sync
        def _(sp):
            for dst, src in start_loads:
                sp.dma_start(dst, src).then_inc(S["start"], 16)
            for dst, src in small_loads:
                sp.dma_start(dst, src).then_inc(S["small"], 16)
            if start_loads:
                for i in range(24):
                    if i >= 2:
                        sp.wait_ge(S["filled"], first_mod_release[i - 2])
                    sp.dma_start(SLM[i % 2], mod_source(w["w_mod"], i)).then_inc(S["mod_first%d" % (i % 2)], 16)
            for j, (dst, src, _, _) in enumerate(weight_units):
                if j == LAND:
                    for d_, s_ in late_loads:
                        sp.dma_start(d_, s_).then_inc(S["late"], 16)
                if j == LAND and z_loads:
                    sp.wait_ge(S["zeroed"], 1)
                    for d_, s_ in z_loads:
                        sp.dma_start(d_, s_).then_inc(S["z_loaded"], 16)
                if j >= LAND:
                    if weight_units[j - LAND][3]:
                        sp.wait_ge(S["w_low"], n_of[j - LAND] + 1)
                    else:
                        name, n = release[j - LAND]
                        sp.wait_ge(S[name], n)
                sp.dma_start(dst, src).then_inc(S["landed%d" % (j % LAND)], 16)
                if nxt and j in beside:
                    i = beside[j]
                    if i == 0:
                        sp.wait_ge(S["mod_room"], 1)
                    else:
                        sp.wait_ge(S["filled"], mod_release[i - 1])
                    sp.dma_start(SLM[0], mod_source(nxt["w_mod"], i)).then_inc(S["mod_landed"], 16)

        @block.gpsimd
        def _(pool):
            if not second:
                pool.wait_ge(S["h_ready"], 1)
                pool.memset(WZ, 0.0).then_inc(S["zeroed"], 1)
                pool.wait_ge(S["zeroed"], 1)
                pool.memset(ZT[32:33, :], 1.0).then_inc(S["z_ones"], 1)

        @block.scalar
        def _(act):
            B = banks()
            steps = [0]

            def step(ins):
                steps[0] += 1
                ins.then_inc(S["act_step"], 1)
                act.wait_ge(S["act_step"], steps[0])

            def copy_out(bank, dst):
                act.activation(dst, bank, ACT.Copy).then_inc(S["emptied_act"], 1)

            nroot = [0]
            nsplit = [0]

            def split():
                s_ = nsplit[0]
                nsplit[0] += 1
                j = split_of[s_]
                _, _, (k, n), _ = weight_units[j]
                act.wait_ge(S["landed%d" % (j % LAND)], 16 * (j // LAND + 1))
                if s_ >= 2:
                    act.wait_ge(S[release[split_of[s_ - 2]][0]], release[split_of[s_ - 2]][1])
                act.activation(WH[s_ % 2][:, 0:k * n], slots[j % LAND][:, 0:k * n], ACT.Copy).then_inc(S["w_high"], 1)

            def modulate(which, tt):
                for f in range(KD):
                    for a, cnt, r in spans(tt):
                        bank = B.share(act)
                        act.activation(HH[:, f, a:a + cnt], bank[:, 0:cnt], ACT.Identity, scale=AT[:, which, f, r:r + 1],
                                       bias=MT[:, 2 * which, f, r:r + 1]).then_inc(S["h_high"], 1)

            def roots(n):
                nroot[0] += 1
                act.wait_ge(S["mean_sq"], nroot[0])
                act.activation(ssq[:, 0:n], ssq[:, 0:n], ACT.Sqrt).then_inc(S["root"], 1)

            def norm(which, tt):
                for i, t in enumerate(tt):
                    if which:
                        act.wait_ge(S["x_done"], i + 1)
                    if which or i % 2:
                        ins = act.activation(XNV[:, t, :], XV[:, t, :], ACT.Square, accum_out=ssq[:, i:i + 1])
                ins.then_inc(S["squared"], 1)
                roots(len(tt))
                act.wait_ge(S["inverse%d" % which], 1)
                for i, t in enumerate(tt):
                    if i % 2:
                        act.activation(XNV[:, t, :], XV[:, t, :], ACT.Copy, scale=rstd[:, i:i + 1]).then_inc(S["normed_act%d" % which], 1)

            def output_squares(junk):
                for t in range(LAT_T):
                    B.empty(act, "d", "a")
                    act.wait_ge(S["emptied_dve"], B.emptied_by("d"))
                    ins = act.activation(junk[:, D * t:D * (t + 1)], YBV[:, t, :], ACT.Square, accum_out=ssq[:, t:t + 1])
                ins.then_inc(S["squared"], 1)
                roots(LAT_T)

            def columns(dst, by, tt=None):
                for a, cnt, r in spans(tt or IN_T):
                    bank = B.empty(act, by, "a")
                    if bank is not None:
                        copy_out(bank[:, 0:cnt], dst(a, cnt))

            def attention(name, us, scale, mlstm=False):
                sb, pb = (SB2, PB2) if mlstm else (SB, PB)
                ns = depth(us, mlstm)
                for i in range(len(us) + ns - 1):
                    if i < len(us):
                        u = us[i]
                        if not mlstm and u["na"]:
                            act.wait_ge(S[name + "_scores"], i + 1)
                            if i >= 2:
                                act.wait_ge(S[name + "_turn"], i - 1)
                            ins = act.activation(sb[i % 2][:, 0:256], PS[2 * (i % 2)][:, 0:256], ACT.Copy, scale=scale)
                            if u["sink"] is not None:
                                ins = act.activation(sb[i % 2][:, u["n"]:u["n"] + 1], u["sink"], ACT.Copy)
                            ins.then_inc(S[name + "_ctx"], 1)
                        act.wait_ge(S[name + "_max"], i + 1)
                        c = i % 4
                        if mlstm:
                            act.activation(sb[i % 2][:, 0:u["nk"]], sb[i % 2][:, 0:u["nk"]], ACT.Exp, bias=nm[:, c:c + 1])
                            act.activation(fl[:, c:c + 1], BC[:, u["n"], u["h"]:u["h"] + 1], ACT.Exp, scale=-1.0,
                                           bias=nm[:, c:c + 1]).then_inc(S[name + "_exp"], 1)
                        else:
                            m = u["n"] + (u["sink"] is not None)
                            act.activation(sb[i % ns][:, 0:m], sb[i % ns][:, 0:m], ACT.Exp, bias=nm[:, c:c + 1],
                                           accum_out=rs[:, c:c + 1]).then_inc(S[name + "_exp"], 1)
                    if i >= ns - 1:
                        k = i - ns + 1
                        nb = len(us[k]["v"])
                        if nb > 4:
                            act.wait_ge(S[name + "_turn"], k + 1)
                            if k >= 2:
                                act.wait_ge(S[name + "_values"], k - 1)
                            act.activation(pb[k % 2][:, 512:128 * nb], PS[5][:, 0:128 * (nb - 4)], ACT.Copy).then_inc(S[name + "_turned_act"], 1)

            def silu_rows(at, event):
                out = SC32.rearrange("p k (m r) -> p k m r", r=len(at))
                for r, v in enumerate(at):
                    ins = act.activation(out[:, :, :, r], VT[:, v:v + 8].unsqueeze(2).broadcast_to([PT, KD, 32 // len(at)]), ACT.Silu)
                ins.then_inc(S[event], 1)

            if not start_loads:
                norm(0, IN_T)
            act.wait_ge(S["vectors"], 1)
            B.empty(act, "d", "a")
            if start_loads:
                silu_rows([V_C, V_CC], "silu_c")
                for _ in range(24):
                    B.empty(act, "d", "a")
            for _ in range(2):
                B.empty(act, "d", "a")
            for s_ in range(2):
                for half in range(2):
                    for r in range(R):
                        bank = B.empty(act, "a", "a")
                        copy_out(bank[:, :], GBV[:, s_, r, half * 512:(half + 1) * 512])
            if start_loads:
                norm(0, IN_T)
            split()
            split()
            act.wait_ge(S["scales"], 1)
            modulate(0, IN_T)

            for j in range(8):
                for i in range(4 if j < 7 else 3):
                    if (j, i) != (0, 0):
                        split()
                    if second and (j, i) == (1, 1):
                        act.wait_ge(S["angles"], 1)
                        act.activation(CSN[:, :, 1, :], ANG[0].rearrange("p (t f) -> p t f", t=4), ACT.Sin)
                        act.activation(CSN[:, :, 0, :], ANG[1].rearrange("p (t f) -> p t f", t=4), ACT.Sin).then_inc(S["cos_sin"], 1)
                    if second and (j, i) == (3, 0):
                        roots(LAT_T)
                for i, t in enumerate(IN_T):
                    bank = B.empty(act, turn[i % 2], "a")
                    if bank is not None:
                        copy_out(bank[:, 0:CW], pr(t, CW * j, CW))

            if not second:
                for _ in spans(IN_T):
                    B.empty(act, "d", "a")
                for t in IN_T:
                    bank = B.empty(act, turn[t % 2], "a")
                    if bank is not None:
                        copy_out(bank[:, :], LA[:, t, :])
                for f in range(2):
                    columns(None, "d")
                    columns(None, "d")
                la = SC[:, 6144:9216]
                act.wait_ge(S["abs_z"], 1)
                step(act.activation(la, la, ACT.Exp, scale=-1.0))
                act.activation(la, la, ACT.Ln, bias=ones_col).then_inc(S["ln_z"], 1)
                k = 0
                for d in (1, 0):
                    for f in range(2):
                        for i, (a, cnt, r) in enumerate(spans(IN_T)):
                            bank = B.empty(act, "a", "a")
                            if k and i == 0:
                                act.wait_ge(S["decay_used"], k)
                            act.activation(EB[0][:, a:a + cnt], bank[:, 0:cnt], ACT.Exp)
                            act.activation(EB[1][:, a:a + cnt], bank[:, 0:cnt], ACT.Exp, scale=-1.0).then_inc(S["emptied_act"], 1)
                        k += 1
                for t in IN_T:
                    bank = B.empty(act, "a", "a")
                    act.activation(KE[:, t].rearrange("p d n -> p (d n)"), bank[:, :], ACT.Exp).then_inc(S["emptied_act"], 1)
                gg = PW[:, O0 - T0:, G_G:G_G + 256]
                act.activation(gg, gg, ACT.Silu).then_inc(S["gate_act"], 1)
                roots(len(OUT_T) * GLA_H)
                B.empty(act, "d", "a")
                n = 0
                for g in range(16):
                    bank = B.empty(act, turn[n % 2], "a")
                    n += 1
                    if bank is not None:
                        for half in range(2):
                            ins = act.activation(nb_part(NB, g, half), bank_part(bank, half), ACT.Copy)
                        ins.then_inc(S["emptied_act"], 1)
                for f in range(3):
                    columns(lambda a, cnt: QN[:, f, a:a + cnt], "a", OUT_T)
                    columns(None, "d")
                attention("na", na_units, 0.125)
                for f in range(3):
                    columns(lambda a, cnt: QS[:, f, a:a + cnt], "a", OUT_T)
                for kv in range(2):
                    columns(None, "d")
                act.wait_ge(S["late"], n_late)
                attention("sw", sw_units, 0.125)
            else:
                for k in range(2):
                    columns(None, "d")
                for m in range(2):
                    for n in range(LAT_T):
                        bank = B.empty(act, turn[n % 2], "a")
                        if bank is not None:
                            copy_out(bank[:, :], QQ[:, n, m * 512:(m + 1) * 512])
                for f in range(4):
                    columns(lambda a, cnt: KTT[:, f, :], "a")
                columns(lambda a, cnt: KIT, "a")
                for dst in (QTT, QIT):
                    for f in range(4):
                        columns(lambda a, cnt: dst[:, f, :], "a")
                g = 0
                act.wait_ge(S["turned_all"], 1)
                for n in range(1, LAT_T):
                    for h in range(8):
                        bank = B.empty(act, "a", "a")
                        if g >= 2:
                            act.wait_ge(S["index_sum"], g - 1)
                        act.activation(RL[g % 2][:, 0:128 * (n + 1)], bank[:, 0:128 * (n + 1)], ACT.Relu).then_inc(S["emptied_act"], 1)
                        g += 1
                attention("at", at_units, 0.125)
                roots(LAT_T * ATT_H)
                for f in range(8):
                    bank = B.empty(act, "a", "a")
                    if f >= 2:
                        act.wait_ge(S["conv"], f - 1)
                    act.activation(CP[f % 2][:, 3:515], bank[:, :], ACT.Copy)
                    cw, cb = VT[:, V_CWT + f:V_CWT + f + 1], VT[:, V_CB + f:V_CB + f + 1]
                    act.activation(QK[:, f, 0:3], cb.broadcast_to([PT, 3]), ACT.Copy)
                    act.activation(QK[:, f, 3:512], bank[:, 0:509], ACT.Identity, scale=cw, bias=cb).then_inc(S["emptied_act"], 1)
                act.wait_ge(S["abs_f"], 1)
                step(act.activation(T16[:, :, :], T16[:, :, :], ACT.Exp, scale=-1.0))
                act.activation(T16[:, :, :], T16[:, :, :], ACT.Ln, bias=ones_col).then_inc(S["ln_f"], 1)
                act.wait_ge(S["conv"], 8)
                act.activation(SC[:, 0:4096], SC[:, 0:4096], ACT.Silu).then_inc(S["conv_silu"], 1)
                og = PW[:, :, M_O:M_O + 512]
                act.activation(og, og, ACT.Sigmoid).then_inc(S["gate_act"], 1)
                B.empty(act, "d", "a")
                B.empty(act, "d", "a")
                attention("ml", ml_units, None, mlstm=True)
                roots(LAT_T * ML_H)

            split()
            split()
            for f in range(KD):
                for a, cnt, r in spans(OUT_T):
                    bank = B.share(act)
                    act.activation(HH[:, f, a:a + cnt], bank[:, 0:cnt], ACT.Copy).then_inc(S["h_high"], 1)
            for j in range(2):
                for _ in range(3):
                    split()
                if second and j:
                    output_squares(P[:, 0:LAT_T * D])
                    continue
                for _ in OUT_T:
                    B.empty(act, "d", "a")
            split()
            split()
            norm(1, OUT_T)
            modulate(1, OUT_T)

            if nxt:
                act.wait_ge(S["mod_room"], 1)
                silu_rows([V_NEXT + 8 * i for i in range(n_next)], "silu_next")

            def ahead():
                if nsplit[0] < len(split_of):
                    split()

            q, read = 0, []
            for m0, m1 in PARTS:
                for m in range(m0, m1):
                    if m:
                        ahead()
                    for a, cnt, r in spans(OUT_T):
                        bank = B.empty(act, "a", "a")
                        if q >= 2:
                            act.wait_ge(S["emptied_dve"], read[q - 2])
                        act.activation(SG[q % 2][:, 0:cnt], bank[:, 0:cnt], ACT.Silu).then_inc(S["emptied_act"], 1)
                        q += 1
                    ahead()
                    for _ in spans(OUT_T):
                        B.empty(act, "d", "a")
                        read.append(B.emptied_by("d"))
                    if nxt:
                        B.empty(act, "d", "a")
                for half in range(2):
                    for k in range(m0, m1, 2):
                        ahead()
                    if second and half and m1 == KF:
                        output_squares(SC[:, 0:LAT_T * D])
                    else:
                        for _ in OUT_T:
                            B.empty(act, "d", "a")
                    if nxt and m1 == KF:
                        B.empty(act, "d", "a")

        @block.vector
        def _(dve):
            B = banks()
            steps = [0]

            def step(ins):
                steps[0] += 1
                ins.then_inc(S["dve_step"], 1)
                dve.wait_ge(S["dve_step"], steps[0])

            def copy_out(bank, dst):
                dve.tensor_copy(dst, bank).then_inc(S["emptied_dve"], 1)

            nroot = [0]

            def inverse_root(n, width, dst=None):
                dve.tensor_scalar(ssq[:, 0:n], ssq[:, 0:n], 1.0 / width, EPS, ALU.mult, ALU.add).then_inc(S["mean_sq"], 1)
                nroot[0] += 1
                dve.wait_ge(S["root"], nroot[0])
                step(dve.reciprocal(rstd[:, 0:n], ssq[:, 0:n]))

            nsquared = [0]

            def squared():
                nsquared[0] += 1
                dve.wait_ge(S["squared"], nsquared[0])

            def norm(which, tt):
                if which:
                    dve.wait_ge(S["x_done"], len(tt))
                else:
                    for i, t in list(enumerate(tt))[::2]:
                        ins = dve.tensor_tensor_reduce(XNV[:, t, :], XV[:, t, :], XV[:, t, :], 1.0, 0.0, ALU.mult, ALU.add, ssq[:, i:i + 1])
                    step(ins)
                squared()
                inverse_root(len(tt), D)
                dve.sem_inc(S["inverse%d" % which], 1)
                for i, t in list(enumerate(tt))[::2]:
                    dve.tensor_scalar(XNV[:, t, :], XV[:, t, :], rstd[:, i:i + 1], None, ALU.mult).then_inc(S["normed%d" % which], 1)

            nsplit, nhigh = [0], [0]

            def split():
                s_ = nsplit[0]
                nsplit[0] += 1
                _, _, (k, n), _ = weight_units[split_of[s_]]
                dve.wait_ge(S["w_high"], s_ + 1)
                dve.tensor_tensor(WL[s_ % 2][:, 0:k * n], slots[split_of[s_] % LAND][:, 0:k * n],
                                  WH[s_ % 2][:, 0:k * n].bitcast(F32), ALU.subtract).then_inc(S["w_low"], 1)

            def after_high():
                bank = B.share(dve)
                nhigh[0] += 1
                dve.wait_ge(S["h_high"], nhigh[0])
                return bank

            def low(f, a, cnt, src):
                dve.tensor_tensor(HL[:, f, a:a + cnt], src, HH[:, f, a:a + cnt].bitcast(F32), ALU.subtract).then_inc(S["emptied_dve"], 1)

            def modulate(which, tt):
                n = 0
                for f in range(KD):
                    for a, cnt, r in spans(tt):
                        bank, tmp = after_high(), TMP[n % 2]
                        if n >= 2:
                            dve.wait_ge(S["emptied_dve"], B.emptied_by("d") - 2)
                        n += 1
                        step(dve.tensor_scalar(tmp[:, 0:cnt], bank[:, 0:cnt], AT[:, which, f, r:r + 1],
                                               MT[:, 2 * which, f, r:r + 1], ALU.mult, ALU.add))
                        low(f, a, cnt, tmp[:, 0:cnt])

            def columns(dst, by, tt=None):
                for a, cnt, r in spans(tt or IN_T):
                    bank = B.empty(dve, by, "d")
                    if bank is not None:
                        copy_out(bank[:, 0:cnt], dst(a, cnt))

            def head_norm(y, nt, H, dh, gain, gate):
                n = H * dh
                sq = SC[:, 0:nt * n].rearrange("p (t n) -> p t n", n=n)
                step(dve.tensor_tensor(sq, y, y, ALU.mult))
                step(dve.tensor_reduce(ssq[:, 0:nt * H].rearrange("p (t h) -> p t h", h=H),
                                       sq.rearrange("p t (h d) -> p t h d", h=H), AX, ALU.add))
                inverse_root(nt * H, dh)
                r4 = rstd[:, 0:nt * H].rearrange("p (t h) -> p t h", h=H).unsqueeze(3).broadcast_to([PT, nt, H, dh])
                y4 = y.rearrange("p t (h d) -> p t h d", h=H)
                step(dve.tensor_tensor(y4, y4, r4, ALU.mult))
                step(dve.tensor_tensor(y, y, gain.unsqueeze(1).broadcast_to([PT, nt, n]), ALU.mult))
                if gate is not None:
                    dve.wait_ge(S["gate_act"], 1)
                    step(dve.tensor_tensor(y, y, gate, ALU.mult))

            def rotate(x, dst, H, cos, sin, tmp):
                nt = x.shape[1]
                c = cos.unsqueeze(2).broadcast_to([PT, nt, H, 32])
                s_ = sin.unsqueeze(2).broadcast_to([PT, nt, H, 32])
                x1, x2, d1, d2 = x[:, :, :, 0:32], x[:, :, :, 32:64], dst[:, :, :, 0:32], dst[:, :, :, 32:64]
                t1, t2 = (z[:, 0:nt * H * 32].rearrange("p (t h f) -> p t h f", t=nt, h=H) for z in tmp)
                dve.tensor_tensor(t1, x1, s_, ALU.mult)
                step(dve.tensor_tensor(t2, x2, s_, ALU.mult))
                dve.tensor_tensor(d1, x1, c, ALU.mult)
                step(dve.tensor_tensor(d2, x2, c, ALU.mult))
                dve.tensor_tensor(d1, d1, t2, ALU.subtract)
                return dve.tensor_tensor(d2, d2, t1, ALU.add)

            def attention(name, us, scale, mlstm=False):
                pb = PB2 if mlstm else PB
                ns = depth(us, mlstm)
                n_ctx = [0]

                def weigh(i):
                    u, s_, c = us[i], (SB2 if mlstm else SB)[i % ns], i % 4
                    a, b = (PS[2 * (i % 2)], PS[2 * (i % 2) + 1]) if ns == 2 else (None, PS[i % ns])
                    dve.wait_ge(S[name + "_scores"], i + 1)
                    if mlstm:
                        nk = u["nk"]
                        step(dve.tensor_tensor(s_[:, 0:nk], a[:, 0:nk], CN[:, C_CAU + 512 - nk:C_CAU + 512], ALU.add))
                        step(dve.reduce_max(nm[:, c:c + 1], s_[:, 0:nk], AX))
                        dve.tensor_scalar(nm[:, c:c + 1], nm[:, c:c + 1], 0.0, -1.0, ALU.max, ALU.mult).then_inc(S[name + "_max"], 1)
                        dve.wait_ge(S[name + "_exp"], i + 1)
                        if i >= 2:
                            dve.wait_ge(S[name + "_turn"], i - 1)
                        dve.scalar_tensor_tensor(SM2[i % 2][:, 0:nk], b[:, 0:nk], float(np.float32(128 ** -0.5)), s_[:, 0:nk],
                                                 ALU.mult, ALU.mult, accum_out=rs[:, c:c + 1]).then_inc(S[name + "_prob"], 1)
                        return
                    if i >= ns:
                        dve.wait_ge(S[name + "_turn"], i - ns + 1)
                    na, nb = u["na"], u["nb"]
                    if nb:
                        step(dve.scalar_tensor_tensor(s_[:, na:na + nb], b[:, 0:nb], scale, u["bias"], ALU.mult, ALU.add))
                    if na:
                        n_ctx[0] += 1
                        dve.wait_ge(S[name + "_ctx"], n_ctx[0])
                    m = u["n"] + (u["sink"] is not None)
                    dve.reduce_max(nm[:, c:c + 1], s_[:, 0:m], AX, negate=True).then_inc(S[name + "_max"], 1)

                def turned(i):
                    nb = min(len(us[i]["v"]), 4)
                    dve.wait_ge(S[name + "_turn"], i + 1)
                    if i >= 2:
                        dve.wait_ge(S[name + "_values"], i - 1)
                    dve.tensor_copy(pb[i % 2][:, 0:128 * nb], PS[4][:, 0:128 * nb]).then_inc(S[name + "_turned_dve"], 1)

                def output(i):
                    u, c = us[i], i % 4
                    dve.wait_ge(S[name + "_exp"], i + 1)
                    if mlstm:
                        dve.wait_ge(S[name + "_prob"], i + 1)
                        step(dve.scalar_tensor_tensor(rr[:, c:c + 1], rs[:, c:c + 1], -1.0, rs[:, c:c + 1], ALU.mult, ALU.max))
                        step(dve.tensor_tensor(rr[:, c:c + 1], rr[:, c:c + 1], fl[:, c:c + 1], ALU.max))
                        step(dve.reciprocal(rr[:, c:c + 1], rr[:, c:c + 1]))
                    else:
                        step(dve.reciprocal(rr[:, c:c + 1], rs[:, c:c + 1]))
                    dve.wait_ge(S[name + "_values"], i + 1)
                    dv, off = u["y"].shape[-1], u.get("off", 0)
                    dve.tensor_scalar(u["y"], PS[6 + i % 2][:, off:off + dv], rr[:, c:c + 1], None, ALU.mult).then_inc(S[name + "_out"], 1)

                for i in range(len(us) + ns):
                    if i < len(us):
                        weigh(i)
                    if 0 <= i - ns + 1 < len(us):
                        turned(i - ns + 1)
                    if 0 <= i - ns < len(us):
                        output(i - ns)
                dve.wait_ge(S[name + "_out"], len(us))

            if not start_loads:
                norm(0, IN_T)
            dve.wait_ge(S["small"], n_small)
            if start_loads:
                dve.wait_ge(S["start"], 16 * len(start_loads))
            bank = B.empty(dve, "d", "d")
            dve.tensor_copy(VT[:, 0:nvec], bank[:, 0:nvec]).then_inc(S["emptied_dve"], 1)
            dve.wait_ge(S["emptied_dve"], 1)
            dve.sem_inc(S["vectors"], 1)

            mod_first = [0]

            def mod_tile(i):
                bank = B.empty(dve, "d", "d")
                rows = ROWS[:, (i // 2) * PT:(i // 2 + 1) * PT]
                if i % 2 == 0:
                    copy_out(bank[:, 0:PT], rows)
                    mod_first[0] = B.emptied_by("d")
                else:
                    dve.wait_ge(S["emptied_dve"], mod_first[0])
                    dve.tensor_tensor(rows, rows, bank[:, 0:PT], ALU.add).then_inc(S["emptied_dve"], 1)

            if start_loads:
                for i in range(24):
                    mod_tile(i)
                dve.wait_ge(S["emptied_dve"], B.emptied_by("d"))
            if second:
                step(dve.tensor_tensor(ROWS, ROWS, BR, ALU.add))
                for i in range(2):
                    g = ROWS[:, (4 + 6 * i) * PT:(6 + 6 * i) * PT]
                    ins = dve.tensor_tensor(g, g, PO[:, 256 * i:256 * (i + 1)], ALU.mult)
                ins.then_inc(S["mod_rows"], 1)
            else:
                dve.tensor_tensor(ROWS, ROWS, BR, ALU.add).then_inc(S["mod_rows"], 1)
            for i in range(2):
                bank = B.empty(dve, "d", "d")
                dve.tensor_copy(MT[:, 2 * i:2 * i + 2].rearrange("p s k r -> p (s k) r"),
                                bank.rearrange("p (k m) -> p k m", m=32)[:, :, 0:R]).then_inc(S["emptied_dve"], 1)
            dve.wait_ge(S["emptied_dve"], B.emptied_by("d"))
            for s_, v in ((0, V_N1), (1, V_N2)):
                for r in range(R):
                    ins = dve.scalar_tensor_tensor(AT[:, s_, :, r], MT[:, 2 * s_ + 1, :, r], 1.0, VT[:, v:v + 8], ALU.add, ALU.mult)
            step(ins)
            for _ in range(4 * R):
                B.empty(dve, "a", "d")
            dve.sem_inc(S["scales"], 1)
            if start_loads:
                norm(0, IN_T)
            split()
            split()
            modulate(0, IN_T)
            dve.wait_ge(S["emptied_dve"], B.emptied_by("d"))
            dve.sem_inc(S["h_ready"], 1)

            def angles():
                dve.wait_ge(S["late"], n_late)
                step(dve.tensor_copy(PF, PI32[:, :]))
                for t in range(LAT_T):
                    ins = dve.tensor_scalar(ANG[0][:, 32 * t:32 * t + 32], CN[:, C_FREQ:C_FREQ + 32], PF[:, t:t + 1], None, ALU.mult)
                step(ins)
                step(dve.tensor_scalar(ANG[1], ANG[0], float(1 / (2 * np.pi)), ROUND, ALU.mult, ALU.add))
                step(dve.tensor_scalar(ANG[1], ANG[1], ROUND, None, ALU.subtract))
                for c in (TWO_PI_1, TWO_PI_2, TWO_PI_3):
                    step(dve.scalar_tensor_tensor(ANG[0], ANG[1], -c, ANG[0], ALU.mult, ALU.add))
                step(dve.tensor_scalar(ANG[0], ANG[0], 3.1415925, -3.1415925, ALU.min, ALU.max))
                step(dve.scalar_tensor_tensor(ANG[1], ANG[0], -1.0, ANG[0], ALU.mult, ALU.max))
                dve.tensor_scalar(ANG[1], ANG[1], -1.0, float(np.pi / 2), ALU.mult, ALU.add).then_inc(S["angles"], 1)

            def beside_projection(j, i):
                t = CTX_T + i
                if i == 0:
                    B.all_emptied(dve)
                if (j, i) == (1, 0):
                    angles()
                elif j == 2:
                    c = pr(t, A_C, 256)
                    step(dve.tensor_tensor_reduce(SC[:, 2 * H_N:2 * H_N + 256], c, c, 1.0, 0.0, ALU.mult, ALU.add, ssq[:, i:i + 1]))
                elif (j, i) == (3, 0):
                    inverse_root(LAT_T, 256)
                    for k in range(LAT_T):
                        c = pr(CTX_T + k, A_C, 256)
                        ins = dve.tensor_scalar(c, c, rstd[:, k:k + 1], None, ALU.mult)
                    ins.then_inc(S["cq"], 1)
                elif j in (4, 5):
                    if (j, i) == (4, 0):
                        dve.wait_ge(S["cos_sin"], 1)
                    cos, sin = CSN[:, i:i + 1, 0, :], CSN[:, i:i + 1, 1, :]
                    if j == 4:
                        x = pr(t, A_K, 512).rearrange("p (t h e) -> p t h e", t=1, e=64)
                        step(rotate(x, x, 8, cos, sin, RT))
                    else:
                        x = pr(t, A_KI, 64).rearrange("p (t h e) -> p t h e", t=1, e=64)
                        step(rotate(x, KID[:, i, 0:64].rearrange("p (t h e) -> p t h e", t=1, e=64), 1, cos, sin, RT))
                elif (j, i) == (6, 0):
                    dve.tensor_scalar(WI, PW[:, :, A_WI:A_WI + 8], float(np.float32(512 ** -0.5)), None, ALU.mult)
                    dve.tensor_copy(KID[:, :, 64:128], KID[:, :, 0:64]).then_inc(S["key_rope"], 1)

            for j in range(8):
                for i in range(4 if j < 7 else 3):
                    if (j, i) != (0, 0):
                        split()
                    if second:
                        beside_projection(j, i)
                for i, t in enumerate(IN_T):
                    bank = B.empty(dve, turn[i % 2], "d")
                    if bank is not None:
                        copy_out(bank[:, 0:CW], pr(t, CW * j, CW))

            if not second:
                for a, cnt, r in spans(IN_T):
                    bank = B.empty(dve, "d", "d")
                    copy_out(bank[0:32, 0:cnt], ZT[0:32, a:a + cnt])
                for t in IN_T:
                    bank = B.empty(dve, turn[t % 2], "d")
                    if bank is not None:
                        copy_out(bank[:, :], LA[:, t, :])
                B.all_emptied(dve)
                la = SC[:, 6144:9216]
                dve.tensor_scalar(MN, la, 0.0, None, ALU.min)
                dve.scalar_tensor_tensor(la, la, -1.0, la, ALU.mult, ALU.max).then_inc(S["abs_z"], 1)
                for f in range(2):
                    columns(lambda a, cnt: QI[:, 0, f, a:a + cnt], "d")
                    columns(lambda a, cnt: KI[:, 0, f, a:a + cnt], "d")
                dve.wait_ge(S["emptied_dve"], B.emptied_by("d"))
                dve.wait_ge(S["ln_z"], 1)
                dve.tensor_tensor(la, MN, la, ALU.subtract).then_inc(S["log_decay"], 1)
                for d in (1, 0):
                    for f in range(2):
                        for _ in spans(IN_T):
                            B.empty(dve, "a", "d")
                        dve.wait_ge(S["emptied_act"], B.emptied_by("a"))
                        edge = EB[0].rearrange("p (c s) -> p c s", s=CH)[:, :, CH - 1 if d == 0 else 0]
                        dve.tensor_copy(DEC[:, d, f, :], edge)
                        dve.scalar_tensor_tensor(QI[:, d, f, :], EB[0], HD ** -0.5, QI[:, 0, f, :], ALU.mult, ALU.mult)
                        dve.tensor_tensor(KI[:, d, f, :], EB[1], KI[:, 0, f, :], ALU.mult).then_inc(S["decay_used"], 1)
                for _ in IN_T:
                    B.empty(dve, "a", "d")
                dve.wait_ge(S["emptied_act"], B.emptied_by("a"))
                for d in range(2):
                    ins = dve.tensor_tensor(KE[:, :, d, :], KE[:, :, d, :], PW[:, :, G_K:G_K + 256], ALU.mult)
                ins.then_inc(S["k_end"], 1)
                dve.wait_ge(S["chunk_sums"], 1)
                for k in range(NCH - 1):
                    for d in range(2):
                        c, after = order[d][k], order[d][k + 1]
                        i = c // 2
                        sums = PS[4 * d + 2 * (c % 2) + i // 4][:, (i % 4) * 128:(i % 4 + 1) * 128]
                        for f in range(2):
                            if k == 0:
                                ins = dve.tensor_copy(SE[:, d, after, f, :], sums[:, 64 * f:64 * f + 64])
                            else:
                                ins = dve.scalar_tensor_tensor(SE[:, d, after, f, :], SE[:, d, c, f, :], DEC[:, d, f, c:c + 1],
                                                               sums[:, 64 * f:64 * f + 64], ALU.mult, ALU.add)
                    step(ins)
                dve.sem_inc(S["states"], 1)
                for n, t in enumerate(OUT_T):
                    dve.wait_ge(S["products"], n + 1)
                    if n >= 2:
                        dve.wait_ge(S["gla_sums"], n - 1)
                    for hp in range(2):
                        b4 = PS[2 * (n % 2) + hp].rearrange("p (d f n) -> p d f n", d=2, f=2)
                        for d in range(2):
                            tri = CN[:, C_TRI + 128 * d:C_TRI + 128 * (d + 1)].unsqueeze(1).broadcast_to([PT, 2, PT])
                            ins = dve.scalar_tensor_tensor(AM[n % 2].rearrange("p d (f q) n -> p d f q n", q=2)[:, d, :, hp, :],
                                                           b4[:, d], 16.0, tri, ALU.mult, ALU.mult)
                    ins.then_inc(S["masked"], 1)
                    dve.wait_ge(S["gla_sums"], n + 1)
                    y = pr(t, G_Q, 256)
                    step(dve.tensor_copy(y, PS[4][:, 0:256]))
                    y4 = y.rearrange("p (f q e) -> p f q e", f=2, q=2)
                    for hp in range(2):
                        ins = dve.tensor_tensor(y4[:, :, hp, :], y4[:, :, hp, :], PS[6 + hp][:, 0:128].rearrange("p (f e) -> p f e", f=2), ALU.add)
                    ins.then_inc(S["gla_out"], 1)
                    if t >= CTX_T:
                        i = t - CTX_T
                        for a, H in ((S_Q, SWA_H), (S_K, 2)):
                            x = pr(t, a, 64 * H).rearrange("p (t h e) -> p t h e", t=1, e=64)
                            step(rotate(x, x, H, ROPE[:, i:i + 1, 0, :], ROPE[:, i:i + 1, 1, :], RT))
                dve.wait_ge(S["gla_out"], len(OUT_T))
                dve.wait_ge(S["z_loaded"], 16 * len(z_loads))
                head_norm(PW[:, O0 - T0:, G_Q:G_Q + 256], len(OUT_T), GLA_H, HD, GN, PW[:, O0 - T0:, G_G:G_G + 256])

                step(dve.memset(RPT, 1.0))
                bank = B.empty(dve, "d", "d")
                copy_out(bank[0:31, 0:90], RPT[0:31, 0:90])
                n = 0
                for g in range(16):
                    bank = B.empty(dve, turn[n % 2], "d")
                    n += 1
                    if bank is not None:
                        for half in range(2):
                            ins = dve.tensor_copy(nb_part(NB, g, half), bank_part(bank, half))
                        ins.then_inc(S["emptied_dve"], 1)
                for f in range(3):
                    columns(None, "a", OUT_T)
                    columns(lambda a, cnt: KN[:, f, a:a + cnt], "d")
                B.all_emptied(dve)
                attention("na", na_units, 0.125)

                for q in range(2):
                    ins = dve.tensor_copy(RK.rearrange("p t (k q e) -> p t k q e", k=2, q=2)[:, :, :, q, :],
                                          PW[:, :, S_K:S_K + 128].rearrange("p t (h e) -> p t h e", e=64))
                ins.then_inc(S["rope"], 1)
                for f in range(3):
                    columns(None, "a", OUT_T)
                for kv in range(2):
                    columns(lambda a, cnt: KS[:, kv, a:a + cnt], "d")
                attention("sw", sw_units, 0.125)
                dve.sem_inc(S["mixed"], 1)
            else:
                for k in range(2):
                    bank = B.empty(dve, "d", "d")
                    dve.tensor_scalar(CQ[:, k, :], bank[:, :], VT[:, V_QL + k:V_QL + k + 1], None, ALU.mult).then_inc(S["emptied_dve"], 1)
                for m in range(2):
                    for n in range(LAT_T):
                        bank = B.empty(dve, turn[n % 2], "d")
                        if bank is not None:
                            copy_out(bank[:, :], QQ[:, n, m * 512:(m + 1) * 512])
                for _ in range(5):
                    columns(None, "a")
                B.all_emptied(dve)
                for m in range(2):
                    x4 = QQ[:, :, 512 * m:512 * (m + 1)].rearrange("p t (h e) -> p t h e", e=64)
                    step(rotate(x4, x4, 8, CSN[:, :, 0, :], CSN[:, :, 1, :], RT))
                    dve.sem_inc(S["rope"], 1)
                for _ in range(8):
                    columns(None, "a")
                B.all_emptied(dve)
                dve.sem_inc(S["turned_all"], 1)
                g = 0
                cau = CN[:, C_CAU + 384:C_CAU + 512]
                dve.tensor_copy(MK[:, 0:128], cau)
                for n in range(1, LAT_T):
                    nk = 128 * (n + 1)
                    for h in range(8):
                        B.empty(dve, "a", "d")
                        dve.wait_ge(S["emptied_act"], B.emptied_by("a"))
                        if h == 0:
                            dve.tensor_scalar(SCO[:, 0:nk], RL[g % 2][:, 0:nk], WI[:, n, h:h + 1], None, ALU.mult).then_inc(S["index_sum"], 1)
                        else:
                            dve.scalar_tensor_tensor(SCO[:, 0:nk], RL[g % 2][:, 0:nk], WI[:, n, h:h + 1], SCO[:, 0:nk],
                                                     ALU.mult, ALU.add).then_inc(S["index_sum"], 1)
                        g += 1
                        dve.wait_ge(S["index_sum"], g)
                    step(dve.tensor_tensor(SCO[:, nk - 128:nk], SCO[:, nk - 128:nk], cau, ALU.add))
                    for r in range(TOPK // 8):
                        src = (SCO if r == 0 else WK)[:, 0:nk]
                        step(dve.max(m8, src))
                        step(dve.match_replace(WK[:, 0:nk], m8, src, TAKEN))
                    mk = MK[:, MKO[n]:MKO[n] + nk]
                    step(dve.tensor_scalar(mk, WK[:, 0:nk], TAKEN, NEG, ALU.is_gt, ALU.mult))
                    step(dve.tensor_tensor(mk[:, nk - 128:nk], mk[:, nk - 128:nk], cau, ALU.add))
                attention("at", at_units, 0.125)
                head_norm(PW[:, :, A_K:A_K + 512], LAT_T, ATT_H, HD, P[:, ROWN:ROWN + 512], None)

                dve.tensor_tensor(IG, PW[:, :, M_I:M_I + 4], GIB.unsqueeze(1).broadcast_to([PT, 4, 4]), ALU.add)
                step(dve.tensor_tensor(BC, PW[:, :, M_F:M_F + 4], GFB.unsqueeze(1).broadcast_to([PT, 4, 4]), ALU.add))
                dve.tensor_scalar(LF, BC, 0.0, None, ALU.min)
                dve.scalar_tensor_tensor(T16, BC, -1.0, BC, ALU.mult, ALU.max).then_inc(S["abs_f"], 1)
                for i in range(2):
                    ins = dve.memset(CP[i][:, 0:3], 0.0)
                step(ins)
                cw = VT[:, V_CWT:V_CWT + 32].rearrange("p (j f) -> p j f", j=4)
                for f in range(8):
                    B.empty(dve, "a", "d")
                    dve.wait_ge(S["emptied_act"], B.emptied_by("a"))
                    x = CP[f % 2]
                    for j in (1, 2):
                        step(dve.scalar_tensor_tensor(QK[:, f, :], x[:, j:j + 512], cw[:, j, f:f + 1], QK[:, f, :], ALU.mult, ALU.add))
                    dve.scalar_tensor_tensor(QK[:, f, :], x[:, 3:515], cw[:, 3, f:f + 1], QK[:, f, :], ALU.mult, ALU.add).then_inc(S["conv"], 1)
                dve.wait_ge(S["ln_f"], 1)
                dve.tensor_tensor(LF, LF, T16, ALU.subtract).then_inc(S["log_forget"], 1)
                bank = B.empty(dve, "d", "d")
                dve.tensor_copy(BC.rearrange("p t h -> p (t h)"), bank[:, 0:16]).then_inc(S["emptied_dve"], 1)
                dve.wait_ge(S["emptied_dve"], B.emptied_by("d"))
                dve.tensor_tensor(T16, IG, BC, ALU.subtract).then_inc(S["gate_cols"], 1)
                bank = B.empty(dve, "d", "d")
                copy_out(bank[0:4, :], CT)
                attention("ml", ml_units, None, mlstm=True)
                head_norm(PW[:, :, M_Q:M_Q + 512], LAT_T, ML_H, 128, P[:, ROWN + 512:ROWN + 1024], PW[:, :, M_O:M_O + 512])
                dve.sem_inc(S["mixed"], 1)

            split()
            split()
            for f in range(KD):
                for a, cnt, r in spans(OUT_T):
                    low(f, a, cnt, after_high()[:, 0:cnt])

            def add_gated(which, bank, t, half):
                r = 1 if t < CTX_T else 0
                a = 512 * half
                dve.tensor_tensor(FT, bank[:, :], GBV[:, which, r, a:a + 512], ALU.mult).then_inc(S["emptied_dve"], 1)
                dve.wait_ge(S["emptied_dve"], B.emptied_by("d"))
                step(dve.tensor_tensor(XV[:, t, a:a + 512], XV[:, t, a:a + 512], FT, ALU.add))
                if which == 0 and half == 1:
                    dve.sem_inc(S["x_done"], 1)

            def add_normed(which):
                dve.wait_ge(S["emptied_dve"], B.emptied_by("d"))
                squared()
                inverse_root(LAT_T, D)
                for t in range(LAT_T):
                    step(dve.scalar_tensor_tensor(YBV[:, t, :], YBV[:, t, :], rstd[:, t:t + 1], GBV[:, which, 0, :], ALU.mult, ALU.mult))
                    dve.tensor_tensor(XV[:, CTX_T + t, :], XV[:, CTX_T + t, :], YBV[:, t, :], ALU.add).then_inc(S["x_done" if which == 0 else "x_final"], 1)

            def outputs(which, half, more=False):
                if more:
                    dve.wait_ge(S["emptied_dve"], B.emptied_by("d"))
                for t in OUT_T:
                    bank = B.empty(dve, "d", "d")
                    if not second:
                        add_gated(which, bank, t, half)
                        continue
                    y = YBV[:, t - CTX_T, 512 * half:512 * (half + 1)]
                    if more:
                        dve.tensor_tensor(y, y, bank[:, :], ALU.add).then_inc(S["emptied_dve"], 1)
                    else:
                        copy_out(bank[:, :], y)

            for j in range(2):
                for _ in range(3):
                    split()
                outputs(0, j)
            if second:
                add_normed(0)
            norm(1, OUT_T)
            dve.sem_inc(S["mod_room"], 1)
            split()
            split()
            modulate(1, OUT_T)

            def ahead():
                if nsplit[0] < len(split_of):
                    split()

            q = 0
            for m0, m1 in PARTS:
                for m in range(m0, m1):
                    if m:
                        ahead()
                    for _ in spans(OUT_T):
                        B.empty(dve, "a", "d")
                    gated = B.emptied_by("a") - len(spans(OUT_T))
                    ahead()
                    for a, cnt, r in spans(OUT_T):
                        dve.wait_ge(S["emptied_dve"], B.emptied_by("d"))
                        bank = B.empty(dve, "d", "d")
                        gated += 1
                        dve.wait_ge(S["emptied_act"], gated)
                        at = slice(a - GOFF, a - GOFF + cnt)
                        dve.tensor_tensor(FT[:, 0:cnt], SG[q % 2][:, 0:cnt], bank[:, 0:cnt], ALU.mult)
                        step(dve.tensor_tensor(GH[:, m - m0, at], SG[q % 2][:, 0:cnt], bank[:, 0:cnt], ALU.mult))
                        dve.tensor_tensor(GL[:, m - m0, at], FT[:, 0:cnt], GH[:, m - m0, at].bitcast(F32), ALU.subtract).then_inc(S["emptied_dve"], 1)
                        q += 1
                    if nxt:
                        mod_tile(m)
                for half in range(2):
                    for k in range(m0, m1, 2):
                        ahead()
                    outputs(1, half, more=m0 > 0)
                    if nxt and m1 == KF:
                        mod_tile(KF + half)
            if second:
                add_normed(1)


def depth(us, mlstm):
    return 2 if mlstm or any(u["na"] for u in us) else 3


def n_act(us, i):
    return sum(len(u["v"]) > 4 for u in us[:i])


def nb_part(NB, g, half):
    return NB[64 * half:64 * half + 64, :, :, 4 * g:4 * g + 4].rearrange("p h j c -> p c h j")


def bank_part(bank, half):
    a = 1 - half
    return bank[64 * half:64 * half + 64, :].rearrange("p (c n) -> p c n", c=4)[:, :, 0:90].rearrange("p c (h r) -> p c h r", h=NA_H)[:, :, :, a:a + 14]


FIRST = ["x", "c", "ctx", "c_ctx", "w_mod", "b_mod", "norm_mix", "norm_ffn", "w_in", "gla_wa2_f", "gla_ba_f",
         "gla_wa2_b", "gla_ba_b", "gla_norm", "na_rpb", "swa_sink", "w_out", "w_gate", "w_up", "w_down", "final_norm"]
SECOND = ["c", "positions", "w_mod", "b_mod", "mix_norm_pre", "mix_norm_post", "w_in", "q_latent_norm", "w_q_up",
          "w_qidx_up", "conv_w", "conv_b", "b_igate", "b_fgate", "attn_out_norm", "mlstm_out_norm", "w_out",
          "ffn_norm_pre", "ffn_norm_post", "w_gate_up", "w_down"]


class Semaphores(dict):

    def __init__(self, nc, stack):
        super().__init__()
        self.nc, self.stack = nc, stack

    def __missing__(self, name):
        self[name] = self.stack.enter_context(self.nc.semaphore(name))
        return self[name]

    def all(self):
        nums = sorted(s.num for s in self.values())
        assert nums == list(range(nums[0], nums[-1] + 1))
        return range(nums[0], nums[-1] + 1)


def program(nc, a, out):
    with ExitStack() as stack:
        def sb(name, n, dt=F32):
            return stack.enter_context(nc.sbuf_tensor(name, [PT, n], dt))[:, :]

        at = {}
        T = dict(X=sb("x_res", NT * D))
        for key, name, n in (("P", "projected", P_N), ("SC", "scratch", SC_N)):
            at[key] = nc.sbuf_base
            T[key] = sb(name, n)
        T.update(W=sb("weights", LAND * UNIT), weights_high=sb("weights_high", 2 * UNIT, F32R),
                 weights_low=sb("weights_low", 2 * UNIT, F32R), C=sb("constants", C_N), G=sb("gates", 4 * D),
                 SM=sb("small", 928), PI=sb("positions_sb", 4, I32))
        for key, high, low_, n in (("SC", "h_high", "h_low", H_N), ("P", "hidden_high_1", "hidden_low_1", 8 * TOK),
                                   ("P", "hidden_high_2", "hidden_low_2", 8 * LAT_T * PT)):
            for i, name in enumerate((high, low_)):
                T[name] = nc.alloc_sbuf_tensor_at(name, [PT, n], F32R, offset=at[key] + 4 * n * i)[:, :]
        T["PS"] = [stack.enter_context(nc.psum_tensor("bank%d" % i, [PT, 512], F32))[:, :] for i in range(8)]
        S = Semaphores(nc, stack)
        X, P = T["X"], T["P"]
        XV = X.rearrange("p (t n) -> p t n", n=D)

        def end_of_layer():
            nc.all_engine_barrier(sems_to_clear=S.all())

        start = [(T["C"], a["constants"]),
                 (XV[:, 0:CTX_T], a["ctx"].rearrange("a (t p) n -> p (a t) n", p=PT)),
                 (XV[:, CTX_T:], a["x"].rearrange("a (t p) n -> p (a t) n", p=PT))]
        for l in range(2):
            def row(name):
                return a[name][l:l + 1]

            w = dict(w_mod=a["w_mod"][l], b_mod=row("b_mod"), c=a["c"], c_ctx=a["c_ctx"].rearrange("(a n) -> a n", a=1),
                     norm1=row("norm_mix"), norm2=row("norm_ffn"), w_in=a["w_in"][l], wa2_f=a["gla_wa2_f"][l],
                     wa2_b=a["gla_wa2_b"][l], ba_f=row("gla_ba_f"), ba_b=row("gla_ba_b"), gla_norm=row("gla_norm"),
                     rpb=a["na_rpb"][l], sink=row("swa_sink"), w_out=a["w_out"][l], w_down=a["w_down"][l],
                     gate=a["w_gate"][l], up=a["w_up"][l], gate_up=(("gate", 0), ("up", 0)), onehot=a["onehot"])
            if l == 0:
                nxt = dict(w_mod=a["w_mod"][1], c=[a["c"], w["c_ctx"]])
            else:
                nxt = dict(w_mod=a["w_mod_2"][0], c=[a["c_2"]])
            layer(nc, T, w, S, False, l == 0, nxt, start if l == 0 else ())
            end_of_layer()

        ssq, rstd = T["SM"][:, 368:372], T["SM"][:, 416:420]
        gain = P[:, 0:D]
        with nc.Block() as block:
            @block.sync
            def _(sp):
                sp.dma_start(gain, a["final_norm"].rearrange("(a n) -> a n", a=1).broadcast_to([PT, D])).then_inc(S["small"], 16)

            @block.vector
            def _(dve):
                for t in range(LAT_T):
                    x = XV[:, CTX_T + t, :]
                    ins = dve.tensor_tensor_reduce(P[:, D * (t + 1):D * (t + 2)], x, x, 1.0, 0.0, ALU.mult, ALU.add, ssq[:, t:t + 1])
                ins.then_inc(S["dve_step"], 1)
                dve.wait_ge(S["dve_step"], 1)
                dve.tensor_scalar(ssq, ssq, 1.0 / D, EPS, ALU.mult, ALU.add).then_inc(S["mean_sq"], 1)
                dve.wait_ge(S["root"], 1)
                dve.reciprocal(rstd, ssq).then_inc(S["dve_step"], 1)
                dve.wait_ge(S["dve_step"], 2)
                dve.wait_ge(S["small"], 16)
                for t in range(LAT_T):
                    x = XV[:, CTX_T + t, :]
                    dve.scalar_tensor_tensor(x, x, rstd[:, t:t + 1], gain, ALU.mult, ALU.mult)

            @block.scalar
            def _(act):
                act.wait_ge(S["mean_sq"], 1)
                act.activation(ssq, ssq, ACT.Sqrt).then_inc(S["root"], 1)
        end_of_layer()

        b = {n: a[n + "_2"] for n in SECOND}
        for l in range(2):
            def row(name):
                return b[name][l:l + 1]

            def mat(name):
                return b[name][l]

            w = dict(w_mod=mat("w_mod"), b_mod=row("b_mod"), c=b["c"], norm1=row("mix_norm_pre"), norm2=row("ffn_norm_pre"),
                     w_in=mat("w_in"), w_q_up=mat("w_q_up"), w_qidx_up=mat("w_qidx_up"), w_out=mat("w_out"),
                     w_down=mat("w_down"), gate=mat("w_gate_up"), gate_up=(("gate", 0), ("gate", FF)),
                     q_latent_norm=row("q_latent_norm"), conv_b=row("conv_b"), conv_w=mat("conv_w"),
                     post1=row("mix_norm_post"), post2=row("ffn_norm_post"), attn_out_norm=row("attn_out_norm"),
                     mlstm_out_norm=row("mlstm_out_norm"), b_igate=row("b_igate"), b_fgate=row("b_fgate"),
                     positions=b["positions"])
            layer(nc, T, w, S, True, False, dict(w_mod=b["w_mod"][1], c=[b["c"]]) if l == 0 else None)
            end_of_layer()

        with nc.Block() as block:
            @block.sync
            def _(sp):
                sp.dma_start(out.rearrange("a (t p) n -> p (a t) n", p=PT), XV[:, CTX_T:]).then_inc(S["stored"], 16)
                sp.wait_ge(S["stored"], 16)


def kernel(**inputs):
    import concourse.bacc as bacc
    from concourse.bass_utils import run_bass_kernel_spmd

    nc = bacc.Bacc("TRN2", target_bir_lowering=False, num_devices=1)
    constants, onehot = shape_constants()
    inputs = {**inputs, "positions_2": np.asarray(inputs["positions_2"]).reshape(LAT_T, PT).T}
    arrays, args = {}, {}
    given = {n: inputs[n] for n in FIRST} | {n + "_2": inputs[n + "_2"] for n in SECOND}
    for name, v in {**given, "constants": constants, "onehot": onehot}.items():
        v = np.ascontiguousarray(v)
        arrays["in_" + name] = v
        args[name] = nc.dram_tensor("in_" + name, v.shape, mybir.dt.from_np(v.dtype), kind="ExternalInput").ap()
    out = nc.dram_tensor("out", (1, LAT_T * PT, D), F32, kind="ExternalOutput").ap()
    program(nc, args, out)
    r = run_bass_kernel_spmd(nc, [arrays], core_ids=[0])
    return r.results[0]["out"]
```
